# Optimizing a Trainium2 kernel written in Bass

```python
import jax, jax.numpy as jnp
from jax import lax
import numpy as np

D_MODEL = 1024
BATCH = 1
SEQ = 128
DEPTH = 1
DEC_BATCH = 1
DEC_SEQ = 256
PAST_LEN = 128

GRID_W = 64
N_HEADS_A = 8
HEAD_DIM_A = 64
D_ATT = N_HEADS_A * HEAD_DIM_A
KH_MAX = 8
KW = 16
Q_BLOCK = 128
D_RNN = 512
N_RG_BLOCKS = 8
RG_BLOCK = D_RNN // N_RG_BLOCKS
CONV_W = 4
CONV_PAD = (2, 1)
RG_C = 8.0
N_EXPERTS = 64
TOP_K = 8
N_GROUPS = 8
TOPK_GROUP = 4
D_EXPERT = 256
D_SHARED = 256
ROUTED_SCALE = 2.5
N_MOD = 6
EPS = 1e-6
NEG = -1e30
D_IN = 3 * D_ATT + 2 * D_RNN + 2 * D_MODEL
SPLITS = (D_ATT, 2 * D_ATT, 3 * D_ATT, 3 * D_ATT + D_RNN, 3 * D_ATT + 2 * D_RNN, 3 * D_ATT + 2 * D_RNN + D_MODEL)

kernel_name = "hybrid_natten_rglru_moe_diffusion_step"

def rmsnorm(x, g):
    xf = x.astype(jnp.float32)
    y = xf * lax.rsqrt(jnp.mean(xf * xf, axis=-1, keepdims=True) + EPS)
    return (y * g.astype(jnp.float32)).astype(x.dtype)

def adaln(cvec, w, b):
    m = jax.nn.silu(cvec) @ w + b
    return m.reshape(cvec.shape[0], N_MOD, D_MODEL)

def modulate(h, m, i):
    return h * (1.0 + m[:, i + 1][:, None, :]) + m[:, i][:, None, :]

def dwconv(x, w, b):
    y = lax.conv_general_dilated(x, w[:, None, :], window_strides=(1,), padding=[CONV_PAD],
                                 dimension_numbers=('NWC', 'WIO', 'NWC'), feature_group_count=D_RNN)
    return y + b

def _lin_combine(e1, e2):
    a1, b1 = e1
    a2, b2 = e2
    return a1 * a2, a2 * b1 + b2

def rglru(xc, wa, ba, wx, bx, lam, h0, reverse):
    B, T, _ = xc.shape
    xb = xc.reshape(B, T, N_RG_BLOCKS, RG_BLOCK)
    r = jax.nn.sigmoid((jnp.einsum('btnd,nde->btne', xb, wa).reshape(B, T, D_RNN) + ba).astype(jnp.float32))
    i = jax.nn.sigmoid((jnp.einsum('btnd,nde->btne', xb, wx).reshape(B, T, D_RNN) + bx).astype(jnp.float32))
    log_a = -RG_C * r * jax.nn.softplus(-lam.astype(jnp.float32))
    a = jnp.exp(log_a)
    u = jnp.sqrt(jnp.maximum(1.0 - jnp.exp(2.0 * log_a), 0.0)) * (i * xc.astype(jnp.float32))
    if reverse:
        a, u = jnp.flip(a, 1), jnp.flip(u, 1)
    a_cum, u_cum = lax.associative_scan(_lin_combine, (a, u), axis=1)
    h = a_cum * h0.astype(jnp.float32)[:, None, :] + u_cum
    h_last = h[:, -1]
    if reverse:
        h = jnp.flip(h, 1)
    return h.astype(xc.dtype), h_last.astype(xc.dtype)

def rg_branch(xr, yg, conv_w, conv_b, rg_wa, rg_ba, rg_wx, rg_bx, rg_lam, h0_f, h0_b):
    xc = dwconv(xr, conv_w, conv_b)
    hf, hf_last = rglru(xc, rg_wa[0], rg_ba[0], rg_wx[0], rg_bx[0], rg_lam[0], h0_f, False)
    hb, hb_last = rglru(xc, rg_wa[1], rg_ba[1], rg_wx[1], rg_bx[1], rg_lam[1], h0_b, True)
    return (hf + hb) * jax.nn.gelu(yg), hf_last, hb_last

def merge(o_a, o_b, ga, gb, w_pa, w_pb, w_out):
    return (jax.nn.sigmoid(ga) * (o_a @ w_pa) + jax.nn.sigmoid(gb) * (o_b @ w_pb)) @ w_out

def ctx_attention(q, k, v):
    B, S, H, dh = q.shape
    nb = S // Q_BLOCK
    qb = q.reshape(B, nb, Q_BLOCK, H, dh).transpose(1, 0, 2, 3, 4)
    scale = HEAD_DIM_A ** -0.5

    def block(qi):
        s = jnp.einsum('bqhd,bshd->bhqs', qi, k).astype(jnp.float32) * scale
        p = jax.nn.softmax(s, axis=-1).astype(v.dtype)
        return jnp.einsum('bhqs,bshd->bqhd', p, v)

    o = lax.map(block, qb)
    return o.transpose(1, 0, 2, 3, 4).reshape(B, S, H * dh)

def na_attention(q, k, v, k_ctx, v_ctx, rpb):
    B, T, H, dh = q.shape
    rows = T // GRID_W
    kh = min(KH_MAX, rows)
    qg = q.reshape(B, rows, GRID_W, H, dh)
    kg = k.reshape(B, rows, GRID_W, H, dh)
    vg = v.reshape(B, rows, GRID_W, H, dh)
    r = jnp.arange(rows)
    row_idx = jnp.clip(r - kh // 2, 0, rows - kh)[:, None] + jnp.arange(kh)[None, :]
    k_rows = kg[:, row_idx]
    v_rows = vg[:, row_idx]
    w = jnp.arange(GRID_W)
    col_start = jnp.clip(w - KW // 2, 0, GRID_W - KW)
    col_in = (w[None, :] >= col_start[:, None]) & (w[None, :] < col_start[:, None] + KW)
    drow = row_idx - r[:, None] + (KH_MAX - 1)
    dcol = jnp.clip(w[None, :] - w[:, None], -(KW - 1), KW - 1) + (KW - 1)
    bias = rpb[:, drow[:, None, :, None], dcol[None, :, None, :]]
    scale = HEAD_DIM_A ** -0.5
    s_loc = jnp.einsum('brwhd,brjkhd->bhrwjk', qg, k_rows).astype(jnp.float32) * scale + bias[None].astype(jnp.float32)
    s_loc = jnp.where(col_in[:, None, :], s_loc, NEG)
    s_ctx = jnp.einsum('brwhd,bshd->bhrws', qg, k_ctx).astype(jnp.float32) * scale
    n_loc = kh * GRID_W
    s = jnp.concatenate([s_loc.reshape(B, H, rows, GRID_W, n_loc), s_ctx], axis=-1)
    p = jax.nn.softmax(s, axis=-1).astype(v.dtype)
    p_loc = p[..., :n_loc].reshape(B, H, rows, GRID_W, kh, GRID_W)
    p_ctx = p[..., n_loc:]
    o = jnp.einsum('bhrwjk,brjkhd->brwhd', p_loc, v_rows) + jnp.einsum('bhrws,bshd->brwhd', p_ctx, v_ctx)
    return o.reshape(B, T, H * dh)

def mixer_context(h, w_in, conv_w, conv_b, rg_wa, rg_ba, rg_wx, rg_bx, rg_lam, w_pa, w_pb, w_out):
    B, S, _ = h.shape
    q, k, v, xr, yg, ga, gb = jnp.split(h @ w_in, SPLITS, axis=-1)
    q = q.reshape(B, S, N_HEADS_A, HEAD_DIM_A)
    k = k.reshape(B, S, N_HEADS_A, HEAD_DIM_A)
    v = v.reshape(B, S, N_HEADS_A, HEAD_DIM_A)
    o_a = ctx_attention(q, k, v)
    h0 = jnp.zeros((B, D_RNN), h.dtype)
    o_b, hf, hb = rg_branch(xr, yg, conv_w, conv_b, rg_wa, rg_ba, rg_wx, rg_bx, rg_lam, h0, h0)
    return merge(o_a, o_b, ga, gb, w_pa, w_pb, w_out), k, v, hf, hb

def mixer_latent(h, k_ctx, v_ctx, h0_f, h0_b, rpb, w_in, conv_w, conv_b, rg_wa, rg_ba, rg_wx, rg_bx, rg_lam, w_pa, w_pb, w_out):
    B, T, _ = h.shape
    q, k, v, xr, yg, ga, gb = jnp.split(h @ w_in, SPLITS, axis=-1)
    q = q.reshape(B, T, N_HEADS_A, HEAD_DIM_A)
    k = k.reshape(B, T, N_HEADS_A, HEAD_DIM_A)
    v = v.reshape(B, T, N_HEADS_A, HEAD_DIM_A)
    o_a = na_attention(q, k, v, k_ctx, v_ctx, rpb)
    o_b, _, _ = rg_branch(xr, yg, conv_w, conv_b, rg_wa, rg_ba, rg_wx, rg_bx, rg_lam, h0_f, h0_b)
    return merge(o_a, o_b, ga, gb, w_pa, w_pb, w_out)

def moe(h, w_router, b_router, w_gate_e, w_up_e, w_down_e, w_gate_s, w_up_s, w_down_s):
    B, T, D = h.shape
    t = h.reshape(B * T, D)
    n = t.shape[0]
    s = jax.nn.sigmoid((t @ w_router).astype(jnp.float32))
    sb = s + b_router.astype(jnp.float32)
    grp = sb.reshape(n, N_GROUPS, N_EXPERTS // N_GROUPS)
    gscore = lax.top_k(grp, 2)[0].sum(-1)
    _, gidx = lax.top_k(gscore, TOPK_GROUP)
    gmask = jax.nn.one_hot(gidx, N_GROUPS, dtype=jnp.float32).sum(1) > 0
    emask = jnp.repeat(gmask, N_EXPERTS // N_GROUPS, axis=1)
    _, idx = lax.top_k(jnp.where(emask, sb, NEG), TOP_K)
    wk = jnp.take_along_axis(s, idx, axis=-1)
    wk = wk / jnp.sum(wk, axis=-1, keepdims=True) * ROUTED_SCALE
    gates = jnp.einsum('nk,nke->ne', wk, jax.nn.one_hot(idx, N_EXPERTS, dtype=jnp.float32)).astype(t.dtype)
    act = jax.nn.silu(jnp.einsum('nd,edf->nef', t, w_gate_e)) * jnp.einsum('nd,edf->nef', t, w_up_e) * gates[:, :, None]
    routed = jnp.einsum('nef,efd->nd', act, w_down_e)
    shared = (jax.nn.silu(t @ w_gate_s) * (t @ w_up_s)) @ w_down_s
    return (routed + shared).reshape(B, T, D)

def setup_inputs(seed: int = 0) -> dict:
    key = jax.random.key(seed)
    ks = jax.random.split(key, 40)

    def nrm(k, shape, scale):
        return jax.random.normal(k, shape, jnp.float32) * scale

    u = jax.random.uniform(ks[20], (DEPTH, 2, D_RNN), jnp.float32, minval=0.9, maxval=0.999)
    a0 = u ** (1.0 / RG_C)
    rg_lam = jnp.log(a0) - jnp.log1p(-a0)
    return {
        "x_prompt": nrm(ks[0], (BATCH, SEQ, D_MODEL), 1.0),
        "x_sample": nrm(ks[1], (DEC_BATCH, DEC_SEQ, D_MODEL), 1.0),
        "cache_k": nrm(ks[2], (DEC_BATCH, DEPTH, PAST_LEN, N_HEADS_A, HEAD_DIM_A), 1.0),
        "cache_v": nrm(ks[3], (DEC_BATCH, DEPTH, PAST_LEN, N_HEADS_A, HEAD_DIM_A), 1.0),
        "state_h_fwd": nrm(ks[4], (DEC_BATCH, DEPTH, D_RNN), 0.5),
        "state_h_bwd": nrm(ks[5], (DEC_BATCH, DEPTH, D_RNN), 0.5),
        "c": nrm(ks[6], (DEC_BATCH, D_MODEL), 1.0),
        "c_ctx": nrm(ks[7], (D_MODEL,), 1.0),
        "norm1_g": 1.0 + nrm(ks[8], (DEPTH, D_MODEL), 0.05),
        "norm2_g": 1.0 + nrm(ks[9], (DEPTH, D_MODEL), 0.05),
        "final_g": 1.0 + nrm(ks[10], (D_MODEL,), 0.05),
        "w_ada": nrm(ks[11], (DEPTH, D_MODEL, N_MOD * D_MODEL), 0.5 * D_MODEL ** -0.5),
        "b_ada": nrm(ks[12], (DEPTH, N_MOD * D_MODEL), 0.02),
        "w_in": nrm(ks[13], (DEPTH, D_MODEL, D_IN), D_MODEL ** -0.5),
        "rpb": nrm(ks[14], (DEPTH, N_HEADS_A, 2 * KH_MAX - 1, 2 * KW - 1), 0.5),
        "conv_w": nrm(ks[15], (DEPTH, CONV_W, D_RNN), CONV_W ** -0.5),
        "conv_b": nrm(ks[16], (DEPTH, D_RNN), 0.02),
        "rg_wa": nrm(ks[17], (DEPTH, 2, N_RG_BLOCKS, RG_BLOCK, RG_BLOCK), RG_BLOCK ** -0.5),
        "rg_ba": nrm(ks[18], (DEPTH, 2, D_RNN), 0.02),
        "rg_wx": nrm(ks[19], (DEPTH, 2, N_RG_BLOCKS, RG_BLOCK, RG_BLOCK), RG_BLOCK ** -0.5),
        "rg_bx": nrm(ks[21], (DEPTH, 2, D_RNN), 0.02),
        "rg_lam": rg_lam,
        "w_pa": nrm(ks[22], (DEPTH, D_ATT, D_MODEL), D_ATT ** -0.5),
        "w_pb": nrm(ks[23], (DEPTH, D_RNN, D_MODEL), D_RNN ** -0.5),
        "w_out": nrm(ks[24], (DEPTH, D_MODEL, D_MODEL), D_MODEL ** -0.5),
        "w_router": nrm(ks[25], (DEPTH, D_MODEL, N_EXPERTS), D_MODEL ** -0.5),
        "b_router": nrm(ks[26], (DEPTH, N_EXPERTS), 0.01),
        "w_gate_e": nrm(ks[27], (DEPTH, N_EXPERTS, D_MODEL, D_EXPERT), D_MODEL ** -0.5),
        "w_up_e": nrm(ks[28], (DEPTH, N_EXPERTS, D_MODEL, D_EXPERT), D_MODEL ** -0.5),
        "w_down_e": nrm(ks[29], (DEPTH, N_EXPERTS, D_EXPERT, D_MODEL), D_EXPERT ** -0.5),
        "w_gate_s": nrm(ks[30], (DEPTH, D_MODEL, D_SHARED), D_MODEL ** -0.5),
        "w_up_s": nrm(ks[31], (DEPTH, D_MODEL, D_SHARED), D_MODEL ** -0.5),
        "w_down_s": nrm(ks[32], (DEPTH, D_SHARED, D_MODEL), D_SHARED ** -0.5),
    }

def reference(x_prompt, x_sample, cache_k, cache_v, state_h_fwd, state_h_bwd, c, c_ctx,
              norm1_g, norm2_g, final_g, w_ada, b_ada, w_in, rpb, conv_w, conv_b,
              rg_wa, rg_ba, rg_wx, rg_bx, rg_lam, w_pa, w_pb, w_out,
              w_router, b_router, w_gate_e, w_up_e, w_down_e, w_gate_s, w_up_s, w_down_s):
    x_ctx = x_prompt
    x_lat = x_sample
    new_k, new_v, new_hf, new_hb = [], [], [], []
    for l in range(DEPTH):
        mix_w = (w_in[l], conv_w[l], conv_b[l], rg_wa[l], rg_ba[l], rg_wx[l], rg_bx[l], rg_lam[l],
                 w_pa[l], w_pb[l], w_out[l])
        moe_w = (w_router[l], b_router[l], w_gate_e[l], w_up_e[l], w_down_e[l],
                 w_gate_s[l], w_up_s[l], w_down_s[l])
        m = adaln(c_ctx[None, :], w_ada[l], b_ada[l])
        h = modulate(rmsnorm(x_ctx, norm1_g[l]), m, 0)
        o, kc, vc, hf, hb = mixer_context(h, *mix_w)
        x_ctx = x_ctx + m[:, 2][:, None, :] * o
        h = modulate(rmsnorm(x_ctx, norm2_g[l]), m, 3)
        x_ctx = x_ctx + m[:, 5][:, None, :] * moe(h, *moe_w)
        new_k.append(kc)
        new_v.append(vc)
        new_hf.append(hf)
        new_hb.append(hb)
        m = adaln(c, w_ada[l], b_ada[l])
        h = modulate(rmsnorm(x_lat, norm1_g[l]), m, 0)
        o = mixer_latent(h, cache_k[:, l], cache_v[:, l], state_h_fwd[:, l], state_h_bwd[:, l], rpb[l], *mix_w)
        x_lat = x_lat + m[:, 2][:, None, :] * o
        h = modulate(rmsnorm(x_lat, norm2_g[l]), m, 3)
        x_lat = x_lat + m[:, 5][:, None, :] * moe(h, *moe_w)
    y_prompt = rmsnorm(x_ctx, final_g)
    y_sample = rmsnorm(x_lat, final_g)
    return (y_prompt, y_sample, jnp.stack(new_k, axis=1), jnp.stack(new_v, axis=1),
            jnp.stack(new_hf, axis=1), jnp.stack(new_hb, axis=1))


_drawn_inputs = setup_inputs


def setup_inputs(seed=0):
    import zlib

    import numpy as np

    out = dict(_drawn_inputs(seed))
    spreads = {}
    factors = {'rpb': 3.898, 'rg_ba': 7.392, 'rg_bx': 6.679, 'cache_k': 4.194, 'cache_v': 3.262}
    for name, (base, spread) in spreads.items():
        noise = np.random.default_rng([zlib.crc32(name.encode()), seed]).standard_normal(out[name].shape)
        drawn = base * np.exp(spread * noise) if base else spread * noise
        out[name] = __import__('jax').numpy.asarray(drawn.astype(out[name].dtype))
    for name, factor in factors.items():
        out[name] = (out[name] * factor).astype(out[name].dtype)
    return out
```

```python
from contextlib import ExitStack

import concourse.bass as bass
from concourse import mybir

F32 = mybir.dt.float32
BF16 = mybir.dt.bfloat16
I32 = mybir.dt.int32
ALU = mybir.AluOpType
ACT = mybir.ActivationFunctionType
AX = mybir.AxisListType.X

P = 128
D = 1024
KD = D // P
NCTX, NLAT = 128, 256
NTOK = NCTX + NLAT
TT = NTOK // P
H, DH = 8, 64
DATT = H * DH
GW = 64
KH, KW = 8, 16
DRNN = 512
CT = DRNN // P
NE, TOPK, NG = 64, 8, 8
GE = NE // NG
FE = 256
EPS = 1e-6
RG_C = 8.0
SCALED = 2.5
BIG = 1e30
CAP = P
MAXPASS = NTOK // CAP
RING = 4
NBLK = NE * MAXPASS
RC = 387
LAT0 = 131
NTAB = NBLK + 3
NVEC = 52
LOWEST = -3.0e38
NSTEP = 24


def hybrid_step(nc, x_prompt, x_sample, cache_k, cache_v, state_f, state_b, c, c_ctx,
                norm1_g, norm2_g, final_g, w_ada, b_ada, w_in, rpb, conv_w, conv_b,
                rg_wa, rg_ba, rg_wx, rg_bx, rg_lam, w_pa, w_pb, w_out,
                w_router, b_router, w_gate_e, w_up_e, w_down_e, w_gate_s, w_up_s, w_down_s,
                y_prompt, y_sample, new_k, new_v, new_hf, new_hb):
    ctx = ExitStack()
    with ctx:
        KB = 1024
        arena = ctx.enter_context(nc.sbuf_tensor("arena", [P, 207 * 256 + 160], F32))
        base = 16512

        def at(name, shape, kb, dt=F32):
            return nc.alloc_sbuf_tensor_at(name, shape, dt, offset=int(base + kb * KB))

        def sem(name):
            return ctx.enter_context(nc.semaphore(name))

        bank = [ctx.enter_context(nc.psum_tensor(f"bank{i}", [P, 512], F32)) for i in range(8)]

        x_sb = at("x_sb", [P, TT, D], 0)
        shared_sb = at("shared_sb", [P, TT, D], 12)
        gate_ffn = at("gate_ffn", [P, 2, D], 24)
        final_g_sb = at("final_g_sb", [P, D], 32)
        small = 36.0
        place, limit = [small], [44]

        def little(name, shape, dt=F32, size=4):
            n = 1
            for s in shape[1:]:
                n *= s
            t = at(name, shape, place[0], dt)
            place[0] += ((n * size + 31) // 32 * 32) / KB
            assert place[0] <= limit[0], name
            return t


        ident = little("ident", [P, P])
        cond_raw = little("cond_raw", [P, 2, KD])
        cond_t = little("cond_t", [P, KD, 2])
        pick = little("pick", [2, 2, P])
        g1_sb = little("g1_sb", [P, KD])
        g2_sb = little("g2_sb", [P, KD])
        mod_t = little("mod_t", [P, 6, KD, 2])
        scale1 = little("scale1", [P, KD, 2])
        scale2 = little("scale2", [P, KD, 2])
        sumsq = little("sumsq", [P, 3, TT])
        minus_half = little("minus_half", [P, TT])
        rstd = little("rstd", [P, 3, TT])
        vec_rows = little("vec_rows", [NVEC, P])
        vec_t = little("vec_t", [P, NVEC])
        half_b = little("half_b", [P, 16])
        neg_lam = little("neg_lam", [P, 8])
        abs_lam = little("abs_lam", [P, 8])
        softplus = little("softplus", [P, 8])
        decay = little("decay", [P, 8])
        decay2 = little("decay2", [P, 8])
        one = little("one", [P, 1])
        quarter = little("quarter", [P, 1])
        h_last = little("h_last", [P, 8])
        h_last_rows = little("h_last_rows", [8, P])
        neg_max = little("neg_max", [P, 2])
        row_sum = little("row_sum", [P, 2])
        row_inv = little("row_inv", [P, 2])
        router_b = little("router_b", [P, NE])
        npass_f = little("npass_f", [P, 4])
        npass_i = little("npass_i", [P, 1], I32)
        slot_val = little("slot_val", [P, RING])
        slot_row = little("slot_row", [P, RING], I32)
        slot_tok = little("slot_tok", [P, RING], I32)
        slot_gate = little("slot_gate", [P, RING])

        EX = 44
        SLOTS = 3
        stream = [at(f"stream{i}", [P, 4096], EX + 16 * i) for i in range(SLOTS)]
        h_t = at("h_t", [P, KD, NTOK], EX + 48)
        merged = at("merged", [P, KD, NTOK], EX + 48)
        h2_t = at("h2_t", [P, KD, NTOK], EX + 48)
        xhat = at("xhat", [P, TT, D], EX + 60)
        bias_sb = at("bias_sb", [P, 6, H, GW], EX + 60)
        q_t = at("q_t", [P, 4, NTOK], EX + 72)
        k_t = at("k_t", [P, 4, NTOK], EX + 78)
        v_sb = at("v_sb", [P, TT, DATT], EX + 84)
        ck_raw = at("ck_raw", [P, DATT], EX + 90)
        ck_t = at("ck_t", [P, 4, P], EX + 92)
        cv_sb = at("cv_sb", [P, DATT], EX + 94)
        s_sb = at("s_sb", [P, 2, 384], EX + 96)
        e_sb = at("e_sb", [P, 2, 384], EX + 99)
        pt_sb = at("pt_sb", [P, 2, 384], EX + 102)
        gate_r = at("gate_r", [P, 2, CT, RC], EX + 60)
        gate_i = at("gate_i", [P, 2, CT, RC], EX + 72.125)
        gate_e = at("gate_e", [P, 2, CT, RC], EX + 84.25)
        gate_mix = at("gate_mix", [P, 2, D], EX + 97)
        xr_pad = at("xr_pad", [P, CT, RC + 3], EX + 105)
        yg = at("yg", [P, CT, NTOK], EX + 111.125)
        ga = at("ga", [P, KD, NTOK], EX + 117.25)
        gated = at("gated", [P, 6, 512], EX + 117.25)
        gb = at("gb", [P, KD, NTOK], EX + 129.25)
        xc = at("xc", [P, CT, RC], EX + 141.25)
        ob_t = at("ob_t", [P, CT, NTOK], EX + 141.25)
        oa_t = at("oa_t", [P, 4, NTOK], EX + 147.5)
        b_row = at("b_row", [2, 2, 512], EX + 153.5)
        m_row = at("m_row", [2, D], EX + 157.5)
        block_w = at("block_w", [P, 2, 2, CT, P], 12)
        k_new = at("k_new", [P, DATT], 20)
        rpb_pad = at("rpb_pad", [7 * H, P], 22)
        col_mask = at("col_mask", [P, GW], 22.5)
        ring_at = [72, 48, 24, 0]
        ring_w = [at(f"ring_w{i}", [P, 2, KD, FE], EX + ring_at[i]) for i in range(RING)]
        ring_d = [at(f"ring_d{i}", [P, 2, D], EX + ring_at[i] + 16) for i in range(RING)]
        xg = [at(f"xg{i}", [P, D], EX + 96 + 4 * i) for i in range(2)]
        hs_t = at("hs_t", [P, 2, NTOK], EX + 104)
        hs_g = at("hs_g", [P, 2, NTOK], EX + 107)
        h2_row = at("h2_row", [P, TT, D], EX + 112)
        xg_t = [at(f"xg_t{i}", [P, KD, CAP], EX + 104 + 4 * i) for i in range(2)]
        y_sb = [at(f"y_sb{i}", [P, D], EX + 112 + 4 * i) for i in range(2)]
        act_sb = at("act_sb", [P, 2, FE], EX + 120)
        silu_sb = at("silu_sb", [P, 2, FE], EX + 122)
        act_t = at("act_t", [P, 2, 2, CAP], EX + 124)
        rank_tab = at("rank_tab", [P, NTAB, TT], EX + 126)
        row_tab = at("row_tab", [P, NTAB, TT, 5], EX + 128.5, BF16)
        onehot = [at(f"onehot{i}", [P, TT, CAP], EX + 134.5 + 0.75 * i, BF16) for i in range(2)]
        slot_no = at("slot_no", [P, TT, CAP], EX + 136)
        place[0] = EX + 137.5
        limit[0] = EX + 163
        w_router_sb = little("w_router_sb", [P, KD, NE])
        score = little("score", [P, TT, NE])
        biased = little("biased", [P, TT, NE])
        group_top = little("group_top", [P, TT, NG, 8])
        group_score = little("group_score", [P, TT, 16])
        best_groups = little("best_groups", [P, TT, 8])
        group_left = little("group_left", [P, TT, 16])
        group_mask = little("group_mask", [P, TT, NG])
        group_pen = little("group_pen", [P, TT, NG])
        masked = little("masked", [P, TT, NE])
        top8 = little("top8", [P, TT, 8])
        left = little("left", [P, TT, NE])
        chosen = little("chosen", [P, TT, NE])
        chosen_b = little("chosen_b", [P, TT, NE], BF16, 2)
        gates = little("gates", [P, TT, NE])
        gate_sum = little("gate_sum", [P, TT])
        ones_row = little("ones_row", [P, NE])
        order = little("order", [P, TT, NE])
        before = little("before", [P, P], BF16, 2)
        before_f = little("before_f", [P, P])
        ones_b = little("ones_b", [P, P], BF16, 2)
        tok_i = little("tok_i", [P, 3, TT], I32)
        tok_hi = little("tok_hi", [P, TT])
        tok_lo = little("tok_lo", [P, TT])
        g_rest = little("g_rest", [P, TT, NE])
        rank_f = little("rank_f", [P, TT, NE])
        picked = at("picked", [P, TT, TOPK, D], EX)

        rpb_dram = nc.dram_tensor("rpb_dram", (7 * H, GW * P), F32, kind="Internal").ap()
        h2_dram = nc.dram_tensor("h2_dram", (NTOK, D), F32, kind="Internal").ap()
        y_dram = nc.dram_tensor("y_dram", (NTOK * TOPK, D), F32, kind="Internal").ap()

        items = ([("ada", i) for i in range(4)] + [("in", i) for i in range(9)]
                 + [("ada", i) for i in range(4, 12)] + [("pa", 0), ("pb", 0)]
                 + [("out", 0), ("out", 1), ("sgu", 0), ("sd", 0)])
        used = {}
        for n, (kind, i) in enumerate(items):
            used[n] = {"ada": ("ada_mm", i + 1), "in": ("w_mm", 4 * (i + 1) - (i >= 2)),
                       "pa": ("merge_mm", KD), "pb": ("merge_mm", KD), "out": ("out_mm", 3 * (i + 1)),
                       "sgu": ("sh_mm", 4), "sd": ("shd_mm", 6)}[kind]
        slot_of, ready_at, sent = {}, {}, [0] * SLOTS
        for n, it in enumerate(items):
            sent[n % SLOTS] += 16 * (2 if it[0] in ("ada", "sgu") else 1)
            slot_of[it], ready_at[it] = n % SLOTS, sent[n % SLOTS]

        S = {n: sem(n) for n in """x_loaded cond_loaded vec_loaded cache_loaded bias_loaded block_loaded
            late_loaded router_loaded rpb_loaded
            pool_step ident_made pick_made consts mask_made rpb_zero blocks_zero tables_made xg_zero
            sumsq1 rstd1 xhat1 xt1 sumsq2 rstd2 xhat2 xt2 sumsq3 rstd3
            cond_silu ada_mm ada_row m_spread mod_copied h_ready vec_mm vec_copied soft_in soft_exp soft_ln
            decay_ready w_mm w_evac ckt_mm ckt_evac kn_mm kn_evac kv_stored rpb_stored
            s_mm s_ready max_ready exp_done p_ready pt_mm pt_evac o_mm o_evac
            pads_zero conv_done gates_mm gates_tanh e2_done e2_capped root_done a_done gelu_done ob_ready
            hl_ready hl_mm hl_copied hl_stored
            merge_mm merge_done bc_mm bc_evac out_mm out_done h2_ready h2r_mm h2r_evac h2_stored
            router_mm score_done chosen_ready rank_mm npass_ready tables_ready
            sh_mm sh_silu sh_act shd_mm shd_evac
            dve_step pool_turn sp_turn num_step onehot_ready idx_mm idx_ready xgt_mm xgt_evac gu_mm silu_done act_ready
            at_mm at_evac y_mm y_ready x2_ready y_done out_stored""".split()}
        stream_ready = [sem(f"stream_ready{i}") for i in range(SLOTS)]
        gathered = [sem(f"gathered{i}") for i in range(2)]
        scattered = [sem(f"scattered{i}") for i in range(2)]
        picked_loaded = [sem(f"picked_loaded{i}") for i in range(TT)]
        ring_ready = [sem(f"ring_ready{i}") for i in range(RING)]

        block = ctx.enter_context(nc.Block())

        def link(eng, s):
            count = [0]

            def go(ins):
                count[0] += 1
                ins.then_inc(s, 1)
                eng.wait_ge(s, count[0])
            return go

        def unit(s):
            return (s, 0) if s < H else ((s - H) // 2, 1 + (s - H) % 2)

        def half_rows(h):
            return slice(DH * (h % 2), DH * (h % 2) + DH)

        def out_rows(t):
            return y_prompt[0] if t == 0 else y_sample[0, (t - 1) * P:t * P, :]

        @block.sync
        def _(sp):
            def stream_item(n):
                kind, i = items[n]
                slot, ready = stream[n % SLOTS], stream_ready[n % SLOTS]
                if n >= SLOTS:
                    sp.wait_ge(S[used[n - SLOTS][0]], used[n - SLOTS][1])
                cols = slice(i * 512, (i + 1) * 512)
                as_k = {"pa": 4, "pb": 4}.get(kind, KD)
                dst = slot[:, :].rearrange("p (k n) -> p k n", k=as_k)
                if kind == "ada":
                    sp.dma_start(dst, w_ada[0].rearrange("(p k) n -> p k n", k=KD)[:, :, cols]).then_inc(ready, 16)
                    if i >= 2:
                        sp.wait_ge(S["ada_row"], i - 1)
                    sp.dma_start(b_row[:, i % 2, :], b_ada[0:1, cols].to_broadcast([2, 512])).then_inc(ready, 16)
                elif kind == "in":
                    sp.dma_start(dst, w_in[0].rearrange("(p k) n -> p k n", k=KD)[:, :, cols]).then_inc(ready, 16)
                elif kind in ("pa", "pb"):
                    w = w_pa if kind == "pa" else w_pb
                    sp.dma_start(dst, w[0].rearrange("(k p) n -> p k n", p=P)).then_inc(ready, 16)
                elif kind == "out":
                    sp.dma_start(dst, w_out[0].rearrange("(k p) n -> p k n", p=P)[:, :, cols]).then_inc(ready, 16)
                elif kind == "sgu":
                    sp.dma_start(slot[:, 0:2048], w_gate_s[0].rearrange("(p k) n -> p (k n)", k=KD)).then_inc(ready, 16)
                    sp.dma_start(slot[:, 2048:4096], w_up_s[0].rearrange("(p k) n -> p (k n)", k=KD)).then_inc(ready, 16)
                else:
                    sp.dma_start(slot[:, 0:2048].rearrange("p (k n) -> p k n", k=2),
                                 w_down_s[0].rearrange("(k p) n -> p k n", p=P)).then_inc(ready, 16)

            for n in range(len(items)):
                stream_item(n)
            sp.wait_ge(S["npass_ready"], 1)
            passes = sp.value_load(npass_i[0:1, 0:1], min_val=1, max_val=MAXPASS)
            sp.wait_ge(S["shd_mm"], 6)
            sp.wait_ge(S["h2r_mm"], 6)
            with sp.Fori(0, passes) as pas:
                with sp.Fori(0, NE // RING) as b:
                    for u in range(RING):
                        sp.wait_ge(S["y_mm"], pas * NE + b * RING + (u + 1))
                        sp.sem_inc(S["sp_turn"], 1)
                        e = bass.ds(b * RING + u, 1)
                        sp.dma_start(ring_w[u][:, 0, :, :].rearrange("p k n -> p (k n)"),
                                     w_gate_e[0, e].rearrange("a (p k) n -> (a p) (k n)", k=KD)).then_inc(ring_ready[u], 16)
                        sp.dma_start(ring_w[u][:, 1, :, :].rearrange("p k n -> p (k n)"),
                                     w_up_e[0, e].rearrange("a (p k) n -> (a p) (k n)", k=KD)).then_inc(ring_ready[u], 16)
                        sp.dma_start(ring_d[u][:, :, :],
                                     w_down_e[0, e].rearrange("a (k p) n -> p (a k) n", p=P)).then_inc(ring_ready[u], 16)
            for s in scattered:
                sp.wait_ge(s, passes * (NE // 2 * 16) + 16)
            by_token = y_dram.rearrange("(t p k) n -> t p (k n)", p=P, k=TOPK)
            for t in range(TT):
                sp.dma_start(picked[:, t, :, :].rearrange("p k n -> p (k n)"), by_token[t]).then_inc(picked_loaded[t], 16)
            for t in range(TT):
                sp.wait_ge(S["y_done"], t + 1)
                sp.dma_start(out_rows(t), x_sb[:, t, :]).then_inc(S["out_stored"], 16)
            sp.wait_ge(S["out_stored"], 16 * TT)

        @block.gpsimd
        def _(pool):
            go = link(pool, S["pool_step"])
            go(pool.memset(ident[:, :], 0.0))
            pool.affine_select(out=ident[:, :], in_=ident[:, :], compare_op=ALU.not_equal, fill=1.0, base=0,
                               pattern=[[-1, P]], channel_multiplier=1).then_inc(S["ident_made"], 1)
            go(pool.memset(pick[:, :, :], 0.0))
            pool.affine_select(out=pick[:, :, :], in_=pick[:, :, :], compare_op=ALU.not_equal, fill=1.0, base=0,
                               pattern=[[-1, 2], [0, P]], channel_multiplier=1).then_inc(S["pick_made"], 1)
            pool.memset(minus_half[:, :], -0.5).then_inc(S["consts"], 1)
            pool.memset(quarter[:, :], 0.25).then_inc(S["consts"], 1)
            pool.memset(one[:, :], 1.0).then_inc(S["consts"], 1)
            pool.memset(rpb_pad[:, :], 0.0).then_inc(S["rpb_zero"], 1)
            pool.memset(block_w[:, :, :, :, :], 0.0).then_inc(S["blocks_zero"], 1)
            go(pool.memset(col_mask[:, :], 0.0))
            for r in range(2):
                rows = slice(GW * r, GW * r + GW)
                low = col_mask[rows, 0:GW - KW]
                go(pool.affine_select(out=low, in_=low, compare_op=ALU.is_ge, fill=-BIG, base=KW // 2,
                                      pattern=[[1, GW - KW]], channel_multiplier=-1))
                high = col_mask[rows, KW:GW]
                ins = pool.affine_select(out=high, in_=high, compare_op=ALU.is_ge, fill=-BIG, base=KW // 2 - 1 - KW,
                                         pattern=[[-1, GW - KW]], channel_multiplier=1)
                ins.then_inc(S["mask_made"], 1)
            pool.wait_ge(S["mask_made"], 2)
            pool.memset(xr_pad[:, :, 0:2], 0.0).then_inc(S["pads_zero"], 1)
            pool.memset(xr_pad[:, :, NCTX + 2:LAT0 + 2], 0.0).then_inc(S["pads_zero"], 1)
            pool.memset(xr_pad[:, :, RC + 2:RC + 3], 0.0).then_inc(S["pads_zero"], 1)

            def rms(n, summed):
                pool.wait_ge(summed, TT)
                go(pool.tensor_scalar(rstd[:, n, :], sumsq[:, n, :], 1.0 / D, EPS, ALU.mult, ALU.add))
                pool.tensor_tensor(rstd[:, n, :], rstd[:, n, :], minus_half[:, :], ALU.pow).then_inc(S[f"rstd{n + 1}"], 1)

            pool.wait_ge(S["consts"], 3)
            rms(0, S["sumsq1"])
            pool.wait_ge(S["merge_done"], KD)
            pool.wait_ge(S["m_spread"], 6)
            pool.wait_ge(S["merge_mm"], KD)
            pool.iota(slot_no[:, :, :], [[0, TT], [1, CAP]], base=0, channel_multiplier=0,
                      allow_small_or_imprecise_dtypes=True).then_inc(S["tables_made"], 1)
            pool.iota(tok_i[:, 0, :], [[P, TT]], base=0, channel_multiplier=1).then_inc(S["tables_made"], 1)
            pool.memset(ones_row[:, :], 1.0).then_inc(S["tables_made"], 1)
            pool.memset(ones_b[:, :], 1.0).then_inc(S["tables_made"], 1)
            go(pool.memset(before_f[:, :], 1.0))
            go(pool.affine_select(out=before_f[:, :], in_=before_f[:, :], compare_op=ALU.is_gt, fill=0.0, base=0,
                                  pattern=[[1, P]], channel_multiplier=-1))
            pool.tensor_copy(before[:, :], before_f[:, :]).then_inc(S["tables_made"], 1)
            pool.memset(group_score[:, :, 8:16], LOWEST).then_inc(S["tables_made"], 1)
            rms(1, S["sumsq2"])
            for i in range(2):
                pool.memset(xg[i][:, :], 0.0).then_inc(S["xg_zero"], 1)

            pool.wait_ge(S["npass_ready"], 1)
            passes = pool.value_load(npass_i[0:1, 0:1], min_val=1, max_val=MAXPASS)
            pool.wait_ge(S["h2_stored"], 16 * TT)
            pool.wait_ge(S["xg_zero"], 2)

            for i in range(2):
                pool.dma_start(y_sb[i][:, 0:KD], h2_dram[0:P, 0:KD]).then_inc(scattered[i], 16)
            def gather(i, u):
                pool.wait_ge(S["idx_ready"], i + 1)
                pool.sem_inc(S["pool_turn"], 1)
                pool.indirect_dma_start(xg[u % 2][:, :], None, h2_dram[:, :],
                                        bass.IndirectOffsetOnAxis(ap=slot_tok[:, u % RING:u % RING + 1], axis=0),
                                        bounds_check=NTOK - 1, oob_is_err=False).then_inc(gathered[u % 2], 16)

            gather(0, 0)
            gather(1, 1)
            with pool.Fori(0, passes * (NE // RING)) as b:
                for u in range(RING):
                    i = b * RING + u
                    pool.wait_ge(S["xgt_mm"], i + 1)
                    gather(i + 2, u + 2)
                    pool.wait_ge(S["y_ready"], 2 * i + 4)
                    pool.sem_inc(S["pool_turn"], 1)
                    pool.indirect_dma_start(y_dram[:, :],
                                            bass.IndirectOffsetOnAxis(ap=slot_row[:, u:u + 1], axis=0),
                                            y_sb[u % 2][:, :], None, bounds_check=NTOK * TOPK - 1,
                                            oob_is_err=False).then_inc(scattered[u % 2], 16)
            for s in gathered:
                pool.wait_ge(s, passes * (NE // 2 * 16) + 16)
                pool.sem_inc(S["pool_turn"], 1)
            rms(2, S["sumsq3"])

        @block.scalar
        def _(act):
            for t in range(TT):
                src = x_prompt[0] if t == 0 else x_sample[0, (t - 1) * P:t * P, :]
                act.dma_start(x_sb[:, t, :], src).then_inc(S["x_loaded"], 16)
            act.dma_start(cond_raw[:, 0, :], c_ctx.rearrange("(p k) -> p k", k=KD)).then_inc(S["cond_loaded"], 16)
            act.dma_start(cond_raw[:, 1, :], c[0].rearrange("(p k) -> p k", k=KD)).then_inc(S["cond_loaded"], 16)
            act.dma_start(g1_sb[:, :], norm1_g[0].rearrange("(p k) -> p k", k=KD)).then_inc(S["cond_loaded"], 16)
            act.dma_start(g2_sb[:, :], norm2_g[0].rearrange("(p k) -> p k", k=KD)).then_inc(S["cond_loaded"], 16)
            at_row = 0
            for ap, n in ((conv_w[0], 16), (conv_b, 4), (rg_ba[0], 8), (rg_bx[0], 8), (rg_lam[0], 8),
                          (state_f[0], 4), (state_b[0], 4)):
                act.dma_start(vec_rows[at_row:at_row + n, :], ap.rearrange("a (t p) -> (a t) p", p=P)).then_inc(S["vec_loaded"], 16)
                at_row += n
            act.wait_ge(S["rpb_zero"], 1)
            for d in range(7):
                act.dma_start(rpb_pad[d * H:(d + 1) * H, P // 2 - KW:P // 2 + KW - 1],
                              rpb[0, :, d + 4, :]).then_inc(S["rpb_loaded"], 16)
            act.wait_ge(S["rpb_loaded"], 7 * 16)
            act.dma_start(rpb_dram.rearrange("r (w c) -> r w c", c=P),
                          rpb_pad[:, :].unsqueeze(1).to_broadcast([7 * H, GW, P])).then_inc(S["rpb_stored"], 16)
            act.dma_start(ck_raw[:, :], cache_k[0, 0].rearrange("s h d -> s (h d)")).then_inc(S["cache_loaded"], 16)
            act.dma_start(cv_sb[:, :], cache_v[0, 0].rearrange("s h d -> s (h d)")).then_inc(S["cache_loaded"], 16)
            act.wait_ge(S["blocks_zero"], 1)
            for d in range(2):
                for kind, w in enumerate((rg_wa, rg_wx)):
                    for par in range(2):
                        rows = slice(DH * par, DH * par + DH)
                        act.dma_start(block_w[rows, d, kind, :, DH * par:DH * par + DH],
                                      w[0, d].rearrange("(t a) d e -> a d t e", a=2)[par]).then_inc(S["block_loaded"], 16)
            act.dma_start(final_g_sb[:, :], final_g.rearrange("(a n) -> a n", a=1).to_broadcast([P, D])).then_inc(S["late_loaded"], 16)
            act.dma_start(router_b[:, :], b_router[0:1, :].to_broadcast([P, NE])).then_inc(S["late_loaded"], 16)
            act.wait_ge(S["x_loaded"], 16 * TT)

            def squares(n, junk, signal):
                for t in range(TT):
                    act.activation(junk[:, t, :], x_sb[:, t, :], ACT.Square,
                                   accum_out=sumsq[:, n, t:t + 1]).then_inc(signal, 1)

            squares(0, xhat, S["sumsq1"])
            act.wait_ge(S["cond_loaded"], 64)
            act.activation(cond_t[:, :, :].rearrange("p k c -> p c k"), cond_raw[:, :, :], ACT.Silu).then_inc(S["cond_silu"], 1)
            act.wait_ge(S["soft_in"], 1)
            act.activation(abs_lam[:, :], abs_lam[:, :], ACT.Exp, scale=-1.0).then_inc(S["soft_exp"], 1)
            act.wait_ge(S["soft_exp"], 1)
            act.wait_ge(S["consts"], 3)
            act.activation(softplus[:, :], abs_lam[:, :], ACT.Ln, bias=one[:, 0:1]).then_inc(S["soft_ln"], 1)

            def mod_copy(i):
                act.wait_ge(S["m_spread"], i + 1)
                act.activation(mod_t[:, i, :, :].rearrange("p k c -> p (k c)"), bank[7][:, 0:2 * KD],
                               ACT.Copy).then_inc(S["mod_copied"], 1)

            mod_copy(0)
            mod_copy(1)
            act.wait_ge(S["rpb_stored"], 16)
            act.wait_ge(S["xt1"], 6)
            for r in range(2):
                src = bass.AP(rpb_dram.tensor, (1 - r) * H * GW * P + P // 2 - 1, [[P - 1, GW], [GW * P, 6 * H], [1, GW]])
                act.dma_start(bias_sb[GW * r:GW * r + GW, :, :, :].rearrange("p s h c -> p (s h) c"), src).then_inc(S["bias_loaded"], 16)

            def evacuate(n):
                act.wait_ge(S["w_mm"], n + 1)
                src = bank[2 + n % 2]
                if n < 4:
                    ins = act.activation(q_t[:, n, :], src[:, 0:NTOK], ACT.Copy, scale=DH ** -0.5)
                elif n < 8:
                    ins = act.activation(k_t[:, n - 4, :], src[:, 0:NTOK], ACT.Copy)
                elif n < 11:
                    ins = act.activation(v_sb[:, n - 8, :], src[:, :], ACT.Copy)
                elif n < 15:
                    if n == 11:
                        act.wait_ge(S["pads_zero"], 3)
                    act.activation(xr_pad[:, n - 11, 2:2 + NCTX], src[:, 0:NCTX], ACT.Copy)
                    ins = act.activation(xr_pad[:, n - 11, LAT0 + 2:LAT0 + 2 + NLAT], src[:, NCTX:NTOK], ACT.Copy)
                elif n < 19:
                    ins = act.activation(yg[:, n - 15, :], src[:, 0:NTOK], ACT.Copy)
                elif n < 27:
                    ins = act.activation(ga[:, n - 19, :], src[:, 0:NTOK], ACT.Tanh, scale=0.5)
                else:
                    ins = act.activation(gb[:, n - 27, :], src[:, 0:NTOK], ACT.Tanh, scale=0.5)
                ins.then_inc(S["w_evac"], 1)

            for n in range(8):
                evacuate(n)
            act.wait_ge(S["ckt_mm"], 1)
            act.activation(ck_t[:, :, :].rearrange("p m s -> p (m s)"), bank[4][:, :], ACT.Copy).then_inc(S["ckt_evac"], 1)
            for n in range(8, 11):
                evacuate(n)
            act.wait_ge(S["kn_mm"], 1)
            act.activation(k_new[:, :], bank[6][:, :], ACT.Copy).then_inc(S["kn_evac"], 1)
            act.wait_ge(S["kn_evac"], 1)
            act.wait_ge(S["w_evac"], 11)
            act.dma_start(new_k[0, 0].rearrange("s h d -> s (h d)"), k_new[:, :]).then_inc(S["kv_stored"], 16)
            act.dma_start(new_v[0, 0].rearrange("s h d -> s (h d)"), v_sb[:, 0, :]).then_inc(S["kv_stored"], 16)
            for s in range(NSTEP + 2):
                if s < NSTEP:
                    h, t = unit(s)
                    act.wait_ge(S["max_ready"], s + 1)
                    if s >= 2:
                        act.wait_ge(S["pt_mm"], s - 1)
                    if t == 0:
                        ins = act.activation(e_sb[:, s % 2, 0:NCTX], bank[s % 2][:, 0:NCTX], ACT.Exp,
                                             bias=neg_max[:, s % 2:s % 2 + 1], accum_out=row_sum[:, s % 2:s % 2 + 1])
                    else:
                        ins = act.activation(e_sb[:, s % 2, :], s_sb[:, s % 2, :], ACT.Exp,
                                             bias=neg_max[:, s % 2:s % 2 + 1], accum_out=row_sum[:, s % 2:s % 2 + 1])
                    ins.then_inc(S["exp_done"], 1)
                    evacuate(11 + s)
                if s >= 2:
                    h, t = unit(s - 2)
                    rows = half_rows(h)
                    act.wait_ge(S["o_mm"], s - 1)
                    act.activation(oa_t[rows, h // 2, t * P:(t + 1) * P], bank[6 + s % 2][rows, 0:P],
                                   ACT.Copy).then_inc(S["o_evac"], 1)
            act.wait_ge(S["kv_stored"], 32)
            act.wait_ge(S["decay_ready"], 1)
            n = 0
            for kind, dst in enumerate((gate_r, gate_i)):
                for d in range(2):
                    for t in range(CT):
                        act.wait_ge(S["gates_mm"], n + 1)
                        j = kind * 8 + d * CT + t
                        act.activation(dst[:, d, t, :], bank[n % 4][:, 0:RC], ACT.Tanh, scale=0.5,
                                       bias=half_b[:, j:j + 1]).then_inc(S["gates_tanh"], 1)
                        n += 1
            act.wait_ge(S["gates_tanh"], 16)
            for d in range(2):
                for t in range(CT):
                    j = d * CT + t
                    act.activation(gate_e[:, d, t, :], gate_r[:, d, t, :], ACT.Exp, scale=decay2[:, j:j + 1],
                                   bias=decay2[:, j:j + 1]).then_inc(S["e2_done"], 1)
            act.wait_ge(S["e2_done"], 8)
            for d in range(2):
                for t in range(CT):
                    j = d * CT + t
                    act.activation(gate_r[:, d, t, :], gate_r[:, d, t, :], ACT.Exp, scale=decay[:, j:j + 1],
                                   bias=decay[:, j:j + 1]).then_inc(S["a_done"], 1)
            act.wait_ge(S["e2_capped"], 1)
            act.activation(gate_e[:, :, :, :], gate_e[:, :, :, :], ACT.Sqrt, scale=-0.25,
                           bias=quarter[:, 0:1]).then_inc(S["root_done"], 1)
            act.activation(yg[:, :, :], yg[:, :, :], ACT.Gelu_apprx_tanh).then_inc(S["gelu_done"], 1)

            def spread_copy(i, dst, scale):
                for n in range(4):
                    at_n = n + (4 if i == 5 else 0)
                    act.wait_ge(S["bc_mm"], at_n + 1)
                    act.activation(dst[:, n // 2, 512 * (n % 2):512 * (n % 2) + 512], bank[4 + n % 2][:, :],
                                   ACT.Copy, scale=scale).then_inc(S["bc_evac"], 1)

            spread_copy(2, gate_mix, 0.5)
            mod_copy(3)
            mod_copy(4)
            spread_copy(5, gate_ffn, 1.0)
            act.wait_ge(S["hl_mm"], 1)
            act.activation(h_last_rows[:, :], bank[6][0:8, 0:P], ACT.Copy).then_inc(S["hl_copied"], 1)
            act.wait_ge(S["hl_copied"], 1)
            act.dma_start(new_hf[0].rearrange("a (t p) -> (a t) p", p=P), h_last_rows[0:4, :]).then_inc(S["hl_stored"], 16)
            act.dma_start(new_hb[0].rearrange("a (t p) -> (a t) p", p=P), h_last_rows[4:8, :]).then_inc(S["hl_stored"], 16)
            act.wait_ge(S["merge_done"], KD)
            act.wait_ge(S["m_spread"], 6)
            act.dma_start(w_router_sb[:, :, :], w_router[0].rearrange("(p k) n -> p k n", k=KD)).then_inc(S["router_loaded"], 16)
            act.wait_ge(S["out_done"], 6)
            squares(1, xhat, S["sumsq2"])
            act.wait_ge(S["router_mm"], 1)
            act.activation(score[:, :, :].rearrange("p t e -> p (t e)"), bank[0][:, 0:TT * NE],
                           ACT.Sigmoid).then_inc(S["score_done"], 1)
            for t in range(TT):
                for half in range(2):
                    n = 2 * t + half
                    act.wait_ge(S["h2r_mm"], n + 1)
                    act.activation(h2_row[:, t, 512 * half:512 * half + 512], bank[6 + n % 2][:, :],
                                   ACT.Copy).then_inc(S["h2r_evac"], 1)
                act.wait_ge(S["h2r_evac"], 2 * t + 2)
                act.dma_start(h2_dram[t * P:(t + 1) * P, :], h2_row[:, t, :]).then_inc(S["h2_stored"], 16)
            for m in range(2):
                act.wait_ge(S["sh_mm"], m + 1)
                act.activation(hs_g[:, m, :], bank[2 + m][:, 0:NTOK], ACT.Silu).then_inc(S["sh_silu"], 1)
            act.wait_ge(S["kv_stored"], 32)
            for n in range(6):
                act.wait_ge(S["shd_mm"], n + 1)
                act.activation(shared_sb[:, n // 2, 512 * (n % 2):512 * (n % 2) + 512], bank[6 + n % 2][:, :],
                               ACT.Copy).then_inc(S["shd_evac"], 1)
            act.wait_ge(S["npass_ready"], 1)
            passes = act.value_load(npass_i[0:1, 0:1], min_val=1, max_val=MAXPASS)
            act.wait_ge(S["h2_stored"], 16 * TT)

            def x_half(i, u):
                act.wait_ge(S["xgt_mm"], i + 1)
                act.activation(xg_t[u % 2][:, 0:4, :].rearrange("p k s -> p (k s)"), bank[0][:, :],
                               ACT.Copy).then_inc(S["xgt_evac"], 1)

            x_half(0, 0)
            with act.Fori(0, passes * (NE // RING)) as b:
                for u in range(RING):
                    i = b * RING + u
                    act.wait_ge(S["gu_mm"], i + 1)
                    act.activation(silu_sb[:, u % 2, :], bank[2 + u % 2][:, 0:FE], ACT.Silu).then_inc(S["silu_done"], 1)
                    x_half(i + 1, u + 1)
                    act.wait_ge(S["y_mm"], i + RING + 1)
                    act.wait_ge(scattered[u % 2], 32 * b + 16 * (u // 2 + 1))
                    act.wait_ge(S["idx_ready"], i + 1)
                    act.activation(y_sb[u % 2][:, 0:512], bank[5][:, :], ACT.Copy,
                                   scale=slot_gate[:, u:u + 1]).then_inc(S["y_ready"], 1)
            act.wait_ge(S["x2_ready"], 3)
            for t in range(TT):
                act.activation(picked[:, t, 1, :], x_sb[:, t, :], ACT.Square,
                               accum_out=sumsq[:, 2, t:t + 1]).then_inc(S["sumsq3"], 1)
            act.wait_ge(S["hl_stored"], 32)

        @block.tensor
        def _(pe):
            def arrived(it):
                pe.wait_ge(stream_ready[slot_of[it]], ready_at[it])
                return stream[slot_of[it]]

            pe.wait_ge(S["ident_made"], 1)
            pe.wait_ge(S["vec_loaded"], 7 * 16)
            pe.transpose(bank[7][:, 0:NVEC], vec_rows[:, :], ident[0:NVEC, 0:NVEC]).then_inc(S["vec_mm"], 1)
            for t in range(TT):
                pe.wait_ge(S["xhat1"], t + 1)
                for half in range(2):
                    for j in range(4):
                        k = 4 * half + j
                        mm = pe.transpose(bank[2 * t + half][:, j * P:(j + 1) * P], xhat[:, t, k:D:KD], ident[:, :])
                    mm.then_inc(S["xt1"], 1)

            def modulation(i):
                for half in range(2):
                    cidx = 2 * i + half
                    w = arrived(("ada", cidx))
                    if cidx == 0:
                        pe.wait_ge(S["cond_silu"], 1)
                    else:
                        pe.wait_ge(S["ada_row"], cidx)
                    for k in range(KD):
                        mm = pe.matmul(bank[6][0:2, :], cond_t[:, k, :], w[:, k * 512:(k + 1) * 512],
                                       start=(k == 0), stop=(k == KD - 1))
                    mm.then_inc(S["ada_mm"], 1)
                pe.wait_ge(S["ada_row"], 2 * i + 2)
                if i in (2, 5):
                    for n in range(4):
                        at_n = n + (4 if i == 5 else 0)
                        if at_n >= 2:
                            pe.wait_ge(S["bc_evac"], at_n - 1)
                        if n == 0:
                            pe.wait_ge(S["pick_made"], 1)
                        mm = pe.matmul(bank[4 + n % 2][:, :], pick[:, n // 2, :], m_row[:, 512 * (n % 2):512 * (n % 2) + 512],
                                       start=True, stop=True)
                        mm.then_inc(S["bc_mm"], 1)
                    pe.wait_ge(S["bc_mm"], at_n + 1)
                    pe.sem_inc(S["m_spread"], 1)
                else:
                    if i == 0:
                        pe.wait_ge(S["vec_copied"], 1)
                    else:
                        pe.wait_ge(S["mod_copied"], {1: 1, 3: 2, 4: 3}[i])
                    for k in range(KD):
                        mm = pe.transpose(bank[7][:, 2 * k:2 * k + 2], m_row[:, k:D:KD], ident[0:2, 0:2])
                    mm.then_inc(S["m_spread"], 1)

            modulation(0)
            modulation(1)
            pe.wait_ge(S["h_ready"], 3)

            def project(n):
                if n >= 2:
                    pe.wait_ge(S["w_evac"], n - 1)
                out = bank[2 + n % 2]
                if 8 <= n < 11:
                    w = arrived(("in", 2))
                    for k in range(KD):
                        mm = pe.matmul(out[:, :], h_t[:, k, (n - 8) * P:(n - 7) * P], w[:, k * 512:(k + 1) * 512],
                                       start=(k == 0), stop=(k == KD - 1))
                else:
                    item, m = divmod(n if n < 8 else n + 1, 4)
                    w = arrived(("in", item))
                    for k in range(KD):
                        mm = pe.matmul(out[:, 0:NTOK], w[:, k * 512 + m * P:k * 512 + (m + 1) * P], h_t[:, k, :],
                                       start=(k == 0), stop=(k == KD - 1))
                mm.then_inc(S["w_mm"], 1)

            for n in range(8):
                project(n)
            pe.wait_ge(S["cache_loaded"], 32)
            for m in range(4):
                mm = pe.transpose(bank[4][:, m * P:(m + 1) * P], ck_raw[:, m * P:(m + 1) * P], ident[:, :])
            mm.then_inc(S["ckt_mm"], 1)
            for n in range(8, 11):
                project(n)
            for m in range(4):
                mm = pe.transpose(bank[6][:, m * P:(m + 1) * P], k_t[:, m, 0:NCTX], ident[:, :])
            mm.then_inc(S["kn_mm"], 1)

            def scores(s):
                h, t = unit(s)
                rows = half_rows(h)
                if s >= 2:
                    pe.wait_ge(S["exp_done"], s - 1)
                q = q_t[rows, h // 2, t * P:(t + 1) * P]
                if t == 0:
                    mm = pe.matmul(bank[s % 2][:, 0:NCTX], q, k_t[rows, h // 2, 0:NCTX], start=True, stop=True)
                else:
                    pe.matmul(bank[s % 2][:, 0:NLAT], q, k_t[rows, h // 2, NCTX:NTOK], start=True, stop=True)
                    mm = pe.matmul(bank[s % 2][:, NLAT:384], q, ck_t[rows, h // 2, :], start=True, stop=True)
                mm.then_inc(S["s_mm"], 1)

            def turn(s):
                pe.wait_ge(S["p_ready"], s + 1)
                if s >= 2:
                    pe.wait_ge(S["pt_evac"], s - 1)
                for j in range(1 if s < H else 3):
                    mm = pe.transpose(bank[4 + s % 2][:, j * P:(j + 1) * P], e_sb[:, s % 2, j * P:(j + 1) * P], ident[:, :])
                mm.then_inc(S["pt_mm"], 1)

            def values(s):
                h, t = unit(s)
                rows = half_rows(h)
                pe.wait_ge(S["pt_evac"], s + 1)
                if s >= 2:
                    pe.wait_ge(S["o_evac"], s - 1)
                heads = slice(h * DH, (h + 1) * DH)
                vs = [v_sb[:, 0, heads]] if t == 0 else [v_sb[:, 1, heads], v_sb[:, 2, heads], cv_sb[:, heads]]
                for j, v in enumerate(vs):
                    mm = pe.matmul(bank[6 + s % 2][rows, 0:P], v, pt_sb[:, s % 2, j * P:(j + 1) * P],
                                   start=(j == 0), stop=(j == len(vs) - 1))
                mm.then_inc(S["o_mm"], 1)

            pe.wait_ge(S["ckt_evac"], 1)
            pe.wait_ge(S["kn_evac"], 1)
            for s in range(NSTEP + 2):
                if s < NSTEP:
                    scores(s)
                    project(11 + s)
                if 1 <= s <= NSTEP:
                    turn(s - 1)
                if s >= 2:
                    values(s - 2)
            pe.wait_ge(S["block_loaded"], 8 * 16)
            pe.wait_ge(S["conv_done"], 1)
            pe.wait_ge(S["w_evac"], 35)
            n = 0
            for kind in range(2):
                for d in range(2):
                    for t in range(CT):
                        if n >= 4:
                            pe.wait_ge(S["gates_tanh"], n - 3)
                        pe.matmul(bank[n % 4][:, 0:RC], block_w[:, d, kind, t, :], xc[:, t, :],
                                  start=True, stop=True).then_inc(S["gates_mm"], 1)
                        n += 1
            pe.wait_ge(S["o_evac"], NSTEP)
            for i in range(2, 6):
                modulation(i)
            wa, wb = arrived(("pa", 0)), arrived(("pb", 0))
            pe.wait_ge(S["gates_tanh"], 16)
            pe.wait_ge(S["ob_ready"], 1)
            for m in range(KD):
                if m >= 2:
                    pe.wait_ge(S["merge_done"], m - 1)
                for out, w, o in ((bank[2 * (m % 2)], wa, oa_t), (bank[2 * (m % 2) + 1], wb, ob_t)):
                    for k in range(4):
                        mm = pe.matmul(out[:, 0:NTOK], w[:, k * D + m * P:k * D + (m + 1) * P], o[:, k, :],
                                       start=(k == 0), stop=(k == 3))
                mm.then_inc(S["merge_mm"], 1)
            pe.wait_ge(S["hl_ready"], 1)
            pe.transpose(bank[6][0:8, 0:P], h_last[:, :], ident[:, :]).then_inc(S["hl_mm"], 1)
            pe.wait_ge(S["merge_done"], KD)
            for half in range(2):
                w = arrived(("out", half))
                for t in range(TT):
                    n = 3 * half + t
                    if n >= 4:
                        pe.wait_ge(S["out_done"], n - 3)
                    for k in range(KD):
                        mm = pe.matmul(bank[n % 4][:, :], merged[:, k, t * P:(t + 1) * P], w[:, k * 512:(k + 1) * 512],
                                       start=(k == 0), stop=(k == KD - 1))
                    mm.then_inc(S["out_mm"], 1)
            for t in range(TT):
                pe.wait_ge(S["xhat2"], t + 1)
                for half in range(2):
                    n = 2 * t + half
                    if n >= 2:
                        pe.wait_ge(S["h2_ready"], n - 1)
                    else:
                        pe.wait_ge(S["bc_evac"], 8)
                    for j in range(4):
                        k = 4 * half + j
                        mm = pe.transpose(bank[4 + n % 2][:, j * P:(j + 1) * P], xhat[:, t, k:D:KD], ident[:, :])
                    mm.then_inc(S["xt2"], 1)
            pe.wait_ge(S["h2_ready"], 6)
            pe.wait_ge(S["router_loaded"], 16)
            for t in range(TT):
                for k in range(KD):
                    mm = pe.matmul(bank[0][:, t * NE:(t + 1) * NE], h2_t[:, k, t * P:(t + 1) * P], w_router_sb[:, k, :],
                                   start=(k == 0), stop=(k == KD - 1))
            mm.then_inc(S["router_mm"], 1)
            pe.wait_ge(S["hl_copied"], 1)
            for n in range(6):
                t, half = divmod(n, 2)
                if n >= 2:
                    pe.wait_ge(S["h2r_evac"], n - 1)
                for j in range(4):
                    mm = pe.transpose(bank[6 + n % 2][:, j * P:(j + 1) * P], h2_t[:, 4 * half + j, t * P:(t + 1) * P], ident[:, :])
                mm.then_inc(S["h2r_mm"], 1)
            w = arrived(("sgu", 0))
            for m in range(4):
                kind, half = divmod(m, 2)
                for k in range(KD):
                    mm = pe.matmul(bank[2 + m][:, 0:NTOK], w[:, kind * 2048 + k * FE + half * P:kind * 2048 + k * FE + (half + 1) * P],
                                   h2_t[:, k, :], start=(k == 0), stop=(k == KD - 1))
                mm.then_inc(S["sh_mm"], 1)
            pe.wait_ge(S["chosen_ready"], 1)
            pe.wait_ge(S["tables_made"], 6)
            for t in range(TT + 1):
                lhs = [ones_b] * min(t, TT) + [before] * (t < TT)
                for j, m in enumerate(lhs):
                    mm = pe.matmul(bank[1][:, t * NE:(t + 1) * NE], m[:, :], chosen_b[:, j, :],
                                   start=(j == 0), stop=(j == len(lhs) - 1))
            mm.then_inc(S["rank_mm"], 1)
            w = arrived(("sd", 0))
            pe.wait_ge(S["sh_act"], 2)
            for n in range(6):
                t, half = divmod(n, 2)
                if n < 2:
                    pe.wait_ge(S["h2r_evac"], 5 + n)
                else:
                    pe.wait_ge(S["shd_evac"], n - 1)
                for k in range(2):
                    mm = pe.matmul(bank[6 + n % 2][:, :], hs_t[:, k, t * P:(t + 1) * P],
                                   w[:, k * D + 512 * half:k * D + 512 * half + 512], start=(k == 0), stop=(k == 1))
                mm.then_inc(S["shd_mm"], 1)
            pe.wait_ge(S["npass_ready"], 1)
            passes = pe.value_load(npass_i[0:1, 0:1], min_val=1, max_val=MAXPASS)
            pe.wait_ge(S["shd_evac"], 6)
            pe.wait_ge(S["tables_ready"], 1)
            pe.sem_inc(S["y_mm"], RING)
            pe.sem_inc(S["y_ready"], 2)

            def block_rows(i, u):
                pe.wait_ge(S["onehot_ready"], i + 1)
                for t in range(TT):
                    mm = pe.matmul(bank[7][:, 0:5], onehot[u % 2][:, t, :], row_tab[:, bass.ds(i, 1), t, :]
                                   .rearrange("p a c -> p (a c)"), start=(t == 0), stop=(t == TT - 1))
                mm.then_inc(S["idx_mm"], 1)

            def turn_tokens(b, u):
                pe.wait_ge(gathered[u % 2], 32 * b + 16 * (u // 2 + 1))
                for k in range(KD):
                    mm = pe.transpose(bank[k // 4][:, (k % 4) * P:(k % 4 + 1) * P], xg[u % 2][:, k * P:(k + 1) * P], ident[:, :])
                mm.then_inc(S["xgt_mm"], 1)

            block_rows(0, 0)
            pe.wait_ge(S["idx_ready"], 1)
            block_rows(1, 1)
            turn_tokens(0, 0)
            with pe.Fori(0, passes * (NE // RING)) as b:
                for u in range(RING):
                    i = b * RING + u
                    pe.wait_ge(ring_ready[u], 48 * b + 48)
                    pe.wait_ge(S["xgt_evac"], 2 * i + 2)
                    for k in range(KD):
                        mm = pe.matmul(bank[2 + u % 2][:, :].rearrange("p (g n) -> p g n", g=2), xg_t[u % 2][:, k, :],
                                       ring_w[u][:, :, k, :], start=(k == 0), stop=(k == KD - 1))
                    mm.then_inc(S["gu_mm"], 1)
                    turn_tokens(b, u + 1)
                    pe.wait_ge(S["act_ready"], i + 1)
                    for k in range(2):
                        mm = pe.transpose(bank[4][:, k * P:(k + 1) * P], act_sb[:, u % 2, k * P:(k + 1) * P], ident[:, :])
                    mm.then_inc(S["at_mm"], 1)
                    pe.wait_ge(S["idx_ready"], i + 2)
                    block_rows(i + 2, u + 2)
                    pe.wait_ge(S["at_evac"], i + 1)
                    pe.wait_ge(S["y_ready"], 2 * i + 2)
                    for half in range(2):
                        for k in range(2):
                            mm = pe.matmul(bank[5 + half][:, :], act_t[:, u % 2, k, :], ring_d[u][:, k, 512 * half:512 * half + 512],
                                           start=(k == 0), stop=(k == 1))
                    mm.then_inc(S["y_mm"], 1)

        @block.vector
        def _(dve):
            go = link(dve, S["dve_step"])
            CW, CB, BA, BX, LAM, H0 = 0, 16, 20, 28, 36, 44
            dve.wait_ge(S["vec_mm"], 1)
            dve.tensor_copy(vec_t[:, :], bank[7][:, 0:NVEC]).then_inc(S["vec_copied"], 1)
            dve.wait_ge(S["vec_copied"], 1)
            go(dve.tensor_scalar(neg_lam[:, :], vec_t[:, LAM:LAM + 8], -1.0, None, ALU.mult))
            dve.tensor_tensor(abs_lam[:, :], vec_t[:, LAM:LAM + 8], neg_lam[:, :], ALU.max).then_inc(S["soft_in"], 1)
            go(dve.tensor_scalar(half_b[:, :], vec_t[:, BA:BA + 16], 0.5, None, ALU.mult))

            def normalise(n, t, signal):
                dve.tensor_scalar(xhat[:, t, :], x_sb[:, t, :], rstd[:, n, t:t + 1], None, ALU.mult).then_inc(signal, 1)

            dve.wait_ge(S["rstd1"], 1)
            dve.wait_ge(S["sumsq1"], 3)
            for t in range(TT):
                normalise(0, t, S["xhat1"])
            dve.wait_ge(S["soft_ln"], 1)
            go(dve.scalar_tensor_tensor(softplus[:, :], neg_lam[:, :], 0.0, softplus[:, :], ALU.max, ALU.add))
            go(dve.tensor_scalar(decay2[:, :], softplus[:, :], -RG_C, None, ALU.mult))
            dve.tensor_scalar(decay[:, :], softplus[:, :], -RG_C / 2, None, ALU.mult).then_inc(S["decay_ready"], 1)

            def row(cidx):
                dve.wait_ge(S["ada_mm"], cidx + 1)
                if cidx % 2 == 0 and cidx:
                    dve.wait_ge(S["m_spread"], cidx // 2)
                dve.tensor_tensor(m_row[:, 512 * (cidx % 2):512 * (cidx % 2) + 512], bank[6][0:2, :],
                                  b_row[:, cidx % 2, :], ALU.add).then_inc(S["ada_row"], 1)

            for cidx in range(4):
                row(cidx)

            def scales(dst, i, g):
                dve.wait_ge(S["cond_loaded"], 64)
                go(dve.scalar_tensor_tensor(dst[:, :, :], mod_t[:, i, :, :], 1.0,
                                            g[:, :].unsqueeze(2).to_broadcast([P, KD, 2]), ALU.add, ALU.mult))

            dve.wait_ge(S["mod_copied"], 2)
            scales(scale1, 1, g1_sb)
            for t in range(TT):
                cond = int(t > 0)
                for k in range(KD):
                    dve.wait_ge(S["xt1"], 2 * t + k // 4 + 1)
                    ins = dve.tensor_scalar(h_t[:, k, t * P:(t + 1) * P], bank[2 * t + k // 4][:, (k % 4) * P:(k % 4 + 1) * P],
                                            scale1[:, k, cond:cond + 1], mod_t[:, 0, k, cond:cond + 1], ALU.mult, ALU.add)
                ins.then_inc(S["h_ready"], 1)
            dve.wait_ge(S["bias_loaded"], 32)
            dve.wait_ge(S["mask_made"], 2)
            go(dve.tensor_tensor(bias_sb[:, :, :, :].rearrange("p s h c -> p (s h) c"),
                                 bias_sb[:, :, :, :].rearrange("p s h c -> p (s h) c"),
                                 col_mask[:, :].unsqueeze(1).to_broadcast([P, 6 * H, GW]), ALU.add))
            for s in range(NSTEP + 1):
                if s < NSTEP:
                    h, t = unit(s)
                    b = s % 2
                    dve.wait_ge(S["s_mm"], s + 1)
                    if t == 0:
                        dve.tensor_reduce(neg_max[:, b:b + 1], bank[b][:, 0:NCTX], AX, ALU.max, negate=True).then_inc(S["max_ready"], 1)
                    else:
                        first = 2 if t == 1 else 0
                        dve.tensor_tensor(s_sb[:, b, 0:NLAT].rearrange("p (j c) -> p j c", c=GW),
                                          bank[b][:, 0:NLAT].rearrange("p (j c) -> p j c", c=GW),
                                          bias_sb[:, first:first + 4, h, :], ALU.add)
                        go(dve.tensor_copy(s_sb[:, b, NLAT:384], bank[b][:, NLAT:384]))
                        dve.tensor_reduce(neg_max[:, b:b + 1], s_sb[:, b, :], AX, ALU.max, negate=True).then_inc(S["max_ready"], 1)
                    n = NCTX if t == 0 else 384
                    dve.wait_ge(S["exp_done"], s + 1)
                    go(dve.reciprocal(row_inv[:, b:b + 1], row_sum[:, b:b + 1]))
                    dve.tensor_scalar(e_sb[:, b, 0:n], e_sb[:, b, 0:n], row_inv[:, b:b + 1], None, ALU.mult).then_inc(S["p_ready"], 1)
                if s >= 1:
                    n = NCTX if s - 1 < H else 384
                    dve.wait_ge(S["pt_mm"], s)
                    if s >= 3:
                        dve.wait_ge(S["o_mm"], s - 2)
                    dve.tensor_copy(pt_sb[:, (s - 1) % 2, 0:n], bank[4 + (s - 1) % 2][:, 0:n]).then_inc(S["pt_evac"], 1)
                if 9 <= s < 9 + CT:
                    t = s - 9
                    dve.wait_ge(S["w_evac"], 15)
                    go(dve.tensor_scalar(xc[:, t, :], xr_pad[:, t, 0:RC], vec_t[:, CW + t:CW + t + 1],
                                         vec_t[:, CB + t:CB + t + 1], ALU.mult, ALU.add))
                    for tap in range(1, 4):
                        j = CW + tap * CT + t
                        go(dve.scalar_tensor_tensor(xc[:, t, :], xr_pad[:, t, tap:tap + RC], vec_t[:, j:j + 1],
                                                    xc[:, t, :], ALU.mult, ALU.add))
            dve.engine_nop().then_inc(S["conv_done"], 1)
            row(4)
            dve.wait_ge(S["e2_done"], 8)
            dve.tensor_scalar(gate_e[:, :, :, :], gate_e[:, :, :, :], 1.0, None, ALU.min).then_inc(S["e2_capped"], 1)
            row(5)
            dve.wait_ge(S["gates_tanh"], 16)
            for d in range(2):
                go(dve.scalar_tensor_tensor(gate_i[:, d, :, :], gate_i[:, d, :, :], 1.0, xc[:, :, :], ALU.add, ALU.mult))
            row(6)
            dve.wait_ge(S["root_done"], 1)
            for d in range(2):
                go(dve.tensor_tensor(gate_e[:, d, :, :], gate_e[:, d, :, :], gate_i[:, d, :, :], ALU.mult))
            row(7)
            dve.wait_ge(S["a_done"], 8)
            for d in range(2):
                for t in range(CT):
                    for lo, hi, init in ((0, NCTX, 0.0), (LAT0, RC, vec_t[:, H0 + CT * d + t:H0 + CT * d + t + 1])):
                        cut = slice(lo, hi) if d == 0 else slice(hi - 1, lo - 1 if lo else None, -1)
                        ins = dve.tensor_tensor_scan(gate_i[:, d, t, cut], gate_r[:, d, t, cut], gate_e[:, d, t, cut],
                                                     init, ALU.mult, ALU.add)
                        go(ins)
                row(8 + d)
            go(dve.tensor_copy(h_last[:, 0:CT], gate_i[:, 0, :, NCTX - 1]))
            dve.tensor_copy(h_last[:, CT:2 * CT], gate_i[:, 1, :, 0]).then_inc(S["hl_ready"], 1)
            dve.wait_ge(S["gelu_done"], 1)
            for lo, hi, at_tok in ((0, NCTX, 0), (LAT0, RC, NCTX)):
                dst = ob_t[:, :, at_tok:at_tok + hi - lo]
                go(dve.tensor_tensor(dst, gate_i[:, 0, :, lo:hi], gate_i[:, 1, :, lo:hi], ALU.add))
                go(dve.tensor_tensor(dst, dst, yg[:, :, at_tok:at_tok + hi - lo], ALU.mult))
            row(10)
            dve.engine_nop().then_inc(S["ob_ready"], 1)
            row(11)
            for m in range(KD):
                dve.wait_ge(S["merge_mm"], m + 1)
                for gate, ps in ((ga, bank[2 * (m % 2)]), (gb, bank[2 * (m % 2) + 1])):
                    go(dve.scalar_tensor_tensor(gate[:, m, :], gate[:, m, :], 1.0, ps[:, 0:NTOK], ALU.add, ALU.mult))
                dve.tensor_tensor(merged[:, m, :], ga[:, m, :], gb[:, m, :], ALU.add).then_inc(S["merge_done"], 1)
            dve.wait_ge(S["bc_evac"], 4)
            for n in range(6):
                half, t = divmod(n, 3)
                cols = slice(512 * half, 512 * half + 512)
                dve.wait_ge(S["out_mm"], n + 1)
                go(dve.tensor_tensor(gated[:, n, :], bank[n % 4][:, :], gate_mix[:, int(t > 0), cols], ALU.mult))
                dve.tensor_tensor(x_sb[:, t, cols], x_sb[:, t, cols], gated[:, n, :], ALU.add).then_inc(S["out_done"], 1)
            dve.wait_ge(S["mod_copied"], 4)
            scales(scale2, 4, g2_sb)
            dve.wait_ge(S["rstd2"], 1)
            dve.wait_ge(S["sumsq2"], 3)
            for t in range(TT):
                normalise(1, t, S["xhat2"])
            for t in range(TT):
                cond = int(t > 0)
                for k in range(KD):
                    n = 2 * t + k // 4
                    dve.wait_ge(S["xt2"], n + 1)
                    ins = dve.tensor_scalar(h2_t[:, k, t * P:(t + 1) * P], bank[4 + n % 2][:, (k % 4) * P:(k % 4 + 1) * P],
                                            scale2[:, k, cond:cond + 1], mod_t[:, 3, k, cond:cond + 1], ALU.mult, ALU.add)
                    if k % 4 == 3:
                        ins.then_inc(S["h2_ready"], 1)
            dve.wait_ge(S["tables_made"], 6)
            dve.wait_ge(S["late_loaded"], 32)
            dve.wait_ge(S["score_done"], 1)
            go(dve.tensor_tensor(biased[:, :, :], score[:, :, :], router_b[:, :].unsqueeze(1).to_broadcast([P, TT, NE]), ALU.add))
            for t in range(TT):
                for g in range(NG):
                    ins = dve.max(group_top[:, t, g, :], biased[:, t, g * GE:(g + 1) * GE])
            go(ins)
            go(dve.tensor_tensor(group_score[:, :, 0:NG], group_top[:, :, :, 0], group_top[:, :, :, 1], ALU.add))
            for t in range(TT):
                ins = dve.max(best_groups[:, t, :], group_score[:, t, 0:8])
            go(ins)
            go(dve.memset(best_groups[:, :, 4:8], LOWEST))
            for t in range(TT):
                ins = dve.match_replace(group_left[:, t, 0:12], best_groups[:, t, :], group_score[:, t, 0:12], BIG)
            go(ins)
            go(dve.tensor_scalar(group_mask[:, :, :], group_left[:, :, 0:NG], BIG, None, ALU.is_equal))
            go(dve.tensor_scalar(group_pen[:, :, :], group_mask[:, :, :], BIG, -BIG, ALU.mult, ALU.add))
            by_group = lambda ap: ap.rearrange("p t (g e) -> p (t g) e", e=GE)
            spread = lambda ap: ap.rearrange("p t g -> p (t g)").unsqueeze(2).to_broadcast([P, TT * NG, GE])
            go(dve.tensor_tensor(by_group(masked[:, :, :]), by_group(biased[:, :, :]), spread(group_mask[:, :, :]), ALU.mult))
            go(dve.tensor_tensor(by_group(masked[:, :, :]), by_group(masked[:, :, :]), spread(group_pen[:, :, :]), ALU.add))
            for t in range(TT):
                ins = dve.max(top8[:, t, :], masked[:, t, :])
            go(ins)
            for t in range(TT):
                ins = dve.match_replace(left[:, t, :], top8[:, t, :], masked[:, t, :], LOWEST)
            go(ins)
            go(dve.tensor_scalar(chosen[:, :, :], left[:, :, :], LOWEST, None, ALU.is_equal))
            dve.tensor_copy(chosen_b[:, :, :], chosen[:, :, :]).then_inc(S["chosen_ready"], 1)
            for m in range(2):
                dve.wait_ge(S["sh_silu"], m + 1)
                dve.wait_ge(S["sh_mm"], m + 3)
                dve.tensor_tensor(hs_t[:, m, :], hs_g[:, m, :], bank[4 + m][:, 0:NTOK], ALU.mult).then_inc(S["sh_act"], 1)
            go(dve.tensor_tensor(gates[:, :, :], score[:, :, :], chosen[:, :, :], ALU.mult))
            go(dve.tensor_reduce(gate_sum[:, :], gates[:, :, :], AX, ALU.add))
            go(dve.reciprocal(gate_sum[:, :], gate_sum[:, :]))
            for t in range(TT):
                ins = dve.tensor_scalar(gates[:, t, :], gates[:, t, :], gate_sum[:, t:t + 1], SCALED, ALU.mult, ALU.mult)
            go(ins)
            for t in range(TT):
                ins = dve.tensor_tensor_scan(order[:, t, :], ones_row[:, :], chosen[:, t, :], 0.0, ALU.mult, ALU.add)
            go(ins)
            go(dve.tensor_tensor(order[:, :, :], order[:, :, :], chosen[:, :, :], ALU.subtract))
            go(dve.tensor_single_scalar(tok_i[:, 1, :], tok_i[:, 0, :], 4, op=ALU.logical_shift_right))
            go(dve.tensor_single_scalar(tok_i[:, 2, :], tok_i[:, 0, :], 15, op=ALU.bitwise_and))
            go(dve.tensor_scalar(tok_hi[:, :], tok_i[:, 1, :], -128.0, 128.0, ALU.add, ALU.mult))
            go(dve.tensor_scalar(tok_lo[:, :], tok_i[:, 2, :], 8.0, None, ALU.mult))
            go(dve.memset(row_tab[:, NBLK:NTAB, :, :], 0.0))
            for t in range(TT):
                col = lambda j: row_tab[:, 0:NE, t, j]
                go(dve.tensor_scalar(col(0), ones_row[:, :], tok_hi[:, t:t + 1], None, ALU.mult))
                go(dve.tensor_scalar(col(1), order[:, t, :], tok_lo[:, t:t + 1], None, ALU.add))
                go(dve.tensor_copy(col(2), gates[:, t, :]))
                go(dve.tensor_tensor(g_rest[:, t, :], gates[:, t, :], col(2), ALU.subtract))
                go(dve.tensor_copy(col(3), g_rest[:, t, :]))
                go(dve.tensor_tensor(g_rest[:, t, :], g_rest[:, t, :], col(3), ALU.subtract))
                go(dve.tensor_copy(col(4), g_rest[:, t, :]))
            for pas in range(1, MAXPASS):
                go(dve.tensor_copy(row_tab[:, pas * NE:(pas + 1) * NE, :, :], row_tab[:, 0:NE, :, :]))
            dve.wait_ge(S["rank_mm"], 1)
            go(dve.scalar_tensor_tensor(rank_f[:, :, :], bank[1][:, 0:TT * NE].rearrange("p (t e) -> p t e", t=TT), 1.0,
                                        chosen[:, :, :], ALU.add, ALU.mult))
            for pas in range(MAXPASS):
                go(dve.tensor_scalar(rank_tab[:, pas * NE:(pas + 1) * NE, :].rearrange("p e t -> p t e"), rank_f[:, :, :],
                                     -1.0 - CAP * pas, None, ALU.add))
            go(dve.memset(rank_tab[:, NBLK:NTAB, :], -1.0))
            go(dve.tensor_reduce(npass_f[:, 0:1], bank[1][:, TT * NE:(TT + 1) * NE], AX, ALU.max))
            go(dve.tensor_scalar(npass_f[:, 1:2], npass_f[:, 0:1], CAP + 0.5, None, ALU.is_gt))
            go(dve.tensor_scalar(npass_f[:, 2:3], npass_f[:, 0:1], 2 * CAP + 0.5, 1.0, ALU.is_gt, ALU.add))
            go(dve.tensor_tensor(npass_i[:, 0:1], npass_f[:, 1:2], npass_f[:, 2:3], ALU.add))
            dve.engine_nop().then_inc(S["tables_ready"], 1)
            dve.engine_nop().then_inc(S["npass_ready"], 1)
            passes = dve.value_load(npass_i[0:1, 0:1], min_val=1, max_val=MAXPASS)

            def select(i, u):
                dve.tensor_tensor(onehot[u % 2][:, :, :], slot_no[:, :, :],
                                  rank_tab[:, bass.ds(i, 1), :].rearrange("p a t -> p (a t)").unsqueeze(2)
                                  .to_broadcast([P, TT, CAP]), ALU.is_equal).then_inc(S["onehot_ready"], 1)

            def numbers(i, u):
                u = u % RING
                dve.wait_ge(S["idx_mm"], i + 1)
                dve.tensor_reduce(slot_val[:, u:u + 1], bank[7][:, 0:2], AX, ALU.add).then_inc(S["num_step"], 1)
                dve.tensor_reduce(slot_gate[:, u:u + 1], bank[7][:, 2:5], AX, ALU.add).then_inc(S["num_step"], 1)
                dve.wait_ge(S["num_step"], 3 * i + 2)
                dve.tensor_scalar(slot_row[:, u:u + 1], slot_val[:, u:u + 1], float(128 * 128), None, ALU.add).then_inc(S["num_step"], 1)
                dve.wait_ge(S["num_step"], 3 * i + 3)
                dve.tensor_single_scalar(slot_tok[:, u:u + 1], slot_row[:, u:u + 1], 3,
                                         op=ALU.logical_shift_right).then_inc(S["idx_ready"], 1)

            def x_half(i, u):
                dve.wait_ge(S["xgt_mm"], i + 1)
                dve.tensor_copy(xg_t[u % 2][:, 4:8, :].rearrange("p k s -> p (k s)"), bank[1][:, :]).then_inc(S["xgt_evac"], 1)

            select(0, 0)
            select(1, 1)
            numbers(0, 0)
            select(2, 2)
            numbers(1, 1)
            x_half(0, 0)
            with dve.Fori(0, passes * (NE // RING)) as b:
                for u in range(RING):
                    i = b * RING + u
                    dve.wait_ge(S["silu_done"], i + 1)
                    dve.tensor_tensor(act_sb[:, u % 2, :], silu_sb[:, u % 2, :], bank[2 + u % 2][:, FE:2 * FE],
                                      ALU.mult).then_inc(S["act_ready"], 1)
                    x_half(i + 1, u + 1)
                    dve.wait_ge(S["at_mm"], i + 1)
                    dve.tensor_copy(act_t[:, u % 2, :, :].rearrange("p k s -> p (k s)"), bank[4][:, 0:FE]).then_inc(S["at_evac"], 1)
                    dve.wait_ge(scattered[u % 2], 32 * b + 16 * (u // 2 + 1))
                    numbers(i + 2, u + 2)
                    select(i + 3, u + 3)
                    dve.wait_ge(S["y_mm"], i + RING + 1)
                    dve.wait_ge(scattered[u % 2], 32 * b + 16 * (u // 2 + 1))
                    dve.tensor_scalar(y_sb[u % 2][:, 512:D], bank[6][:, :], slot_gate[:, u:u + 1], None,
                                      ALU.mult).then_inc(S["y_ready"], 1)
            for t in range(TT):
                dve.wait_ge(picked_loaded[t], 16)
                if t == 0:
                    dve.wait_ge(S["shd_evac"], 6)
                    dve.wait_ge(S["bc_evac"], 8)
                for k in range(TOPK):
                    go(dve.tensor_tensor(shared_sb[:, t, :], shared_sb[:, t, :], picked[:, t, k, :], ALU.add))
                go(dve.tensor_tensor(shared_sb[:, t, :], shared_sb[:, t, :], gate_ffn[:, int(t > 0), :], ALU.mult))
                dve.tensor_tensor(x_sb[:, t, :], x_sb[:, t, :], shared_sb[:, t, :], ALU.add).then_inc(S["x2_ready"], 1)
            dve.wait_ge(S["rstd3"], 1)
            dve.wait_ge(S["sumsq3"], 3)
            for t in range(TT):
                dve.scalar_tensor_tensor(x_sb[:, t, :], x_sb[:, t, :], rstd[:, 2, t:t + 1], final_g_sb[:, :],
                                         ALU.mult, ALU.mult).then_inc(S["y_done"], 1)


_INS = ['x_prompt', 'x_sample', 'cache_k', 'cache_v', 'state_h_fwd', 'state_h_bwd', 'c', 'c_ctx', 'norm1_g', 'norm2_g',
        'final_g', 'w_ada', 'b_ada', 'w_in', 'rpb', 'conv_w', 'conv_b', 'rg_wa', 'rg_ba', 'rg_wx', 'rg_bx', 'rg_lam',
        'w_pa', 'w_pb', 'w_out', 'w_router', 'b_router', 'w_gate_e', 'w_up_e', 'w_down_e', 'w_gate_s', 'w_up_s', 'w_down_s']
_OUTS = [(1, 128, 1024), (1, 256, 1024), (1, 1, 128, 8, 64), (1, 1, 128, 8, 64), (1, 1, 512), (1, 1, 512)]


def kernel(**inputs):
    import numpy as _np
    import concourse.bacc as _bacc
    from concourse import mybir as _mybir
    from concourse.bass_utils import run_bass_kernel_spmd as _run

    nc = _bacc.Bacc("TRN2", target_bir_lowering=False, num_devices=1)
    arrays, args = {}, []
    for name in _INS:
        a = _np.ascontiguousarray(inputs[name])
        arrays[f"in_{name}_dram"] = a
        args.append(nc.dram_tensor(f"in_{name}_dram", a.shape, _mybir.dt.from_np(a.dtype), kind="ExternalInput").ap())
    for i, shape in enumerate(_OUTS):
        args.append(nc.dram_tensor(f"out_{i}_dram", shape, _mybir.dt.float32, kind="ExternalOutput").ap())
    hybrid_step(nc, *args)
    r = _run(nc, [arrays], core_ids=[0])
    return tuple(r.results[0][f"out_{i}_dram"] for i in range(len(_OUTS)))
```

```python
from contextlib import ExitStack

import concourse.bass as bass
from concourse import mybir

F32 = mybir.dt.float32
BF16 = mybir.dt.bfloat16
I32 = mybir.dt.int32
F32R = mybir.dt.float32r
ALU = mybir.AluOpType
ACT = mybir.ActivationFunctionType
AX = mybir.AxisListType.X

P = 128
D = 1024
KD = D // P
NCTX, NLAT = 128, 256
NTOK = NCTX + NLAT
TT = NTOK // P
H, DH = 8, 64
DATT = H * DH
GW = 64
KH, KW = 8, 16
DRNN = 512
CT = DRNN // P
NE, TOPK, NG = 64, 8, 8
GE = NE // NG
FE = 256
EPS = 1e-6
RG_C = 8.0
SCALED = 2.5
BIG = 1e30
CAP = P
MAXPASS = NTOK // CAP
RAW = 2
UN = 8
NK = 3
NBLK = NE * MAXPASS
RC = 387
LAT0 = 131
NTAB = NBLK + 4
NVEC = 52
LOWEST = -3.0e38
NSTEP = 24


def hybrid_step(nc, x_prompt, x_sample, cache_k, cache_v, state_f, state_b, c, c_ctx,
                norm1_g, norm2_g, final_g, w_ada, b_ada, w_in, rpb, conv_w, conv_b,
                rg_wa, rg_ba, rg_wx, rg_bx, rg_lam, w_pa, w_pb, w_out,
                w_router, b_router, w_gate_e, w_up_e, w_down_e, w_gate_s, w_up_s, w_down_s,
                y_prompt, y_sample, new_k, new_v, new_hf, new_hb):
    ctx = ExitStack()
    with ctx:
        KB = 1024
        arena = ctx.enter_context(nc.sbuf_tensor("arena", [P, 207 * 256 + 160], F32))
        base = 16512

        def at(name, shape, kb, dt=F32):
            return nc.alloc_sbuf_tensor_at(name, shape, dt, offset=int(base + kb * KB))

        def sem(name):
            return ctx.enter_context(nc.semaphore(name))

        bank = [ctx.enter_context(nc.psum_tensor(f"bank{i}", [P, 512], F32)) for i in range(8)]

        x_sb = at("x_sb", [P, TT, D], 0)
        shared_sb = at("shared_sb", [P, TT, D], 12)
        gate_ffn = at("gate_ffn", [P, 2, D], 24)
        final_g_sb = at("final_g_sb", [P, D], 32)
        small = 36.0
        place, limit = [small], [44]

        def little(name, shape, dt=F32, size=4):
            n = 1
            for s in shape[1:]:
                n *= s
            t = at(name, shape, place[0], dt)
            place[0] += ((n * size + 31) // 32 * 32) / KB
            assert place[0] <= limit[0], name
            return t


        ident = little("ident", [P, P])
        cond_raw = little("cond_raw", [P, 2, KD])
        cond_t = little("cond_t", [P, KD, 2])
        pick = little("pick", [2, 2, P])
        g1_sb = little("g1_sb", [P, KD])
        g2_sb = little("g2_sb", [P, KD])
        mod_t = little("mod_t", [P, 6, KD, 2])
        scale1 = little("scale1", [P, KD, 2])
        scale2 = little("scale2", [P, KD, 2])
        sumsq = little("sumsq", [P, 3, TT])
        minus_half = little("minus_half", [P, TT])
        rstd = little("rstd", [P, 3, TT])
        vec_rows = little("vec_rows", [NVEC, P])
        vec_t = little("vec_t", [P, NVEC])
        half_b = little("half_b", [P, 16])
        neg_lam = little("neg_lam", [P, 8])
        abs_lam = little("abs_lam", [P, 8])
        softplus = little("softplus", [P, 8])
        decay = little("decay", [P, 8])
        decay2 = little("decay2", [P, 8])
        one = little("one", [P, 1])
        quarter = little("quarter", [P, 1])
        h_last = little("h_last", [P, 8])
        h_last_rows = little("h_last_rows", [8, P])
        neg_max = little("neg_max", [P, 2])
        row_sum = little("row_sum", [P, 2])
        row_inv = little("row_inv", [P, 2])
        router_b = little("router_b", [P, NE])
        load_f = little("load_f", [P, 4])
        more_i = little("more_i", [P, 1], I32)
        slot_val = little("slot_val", [P, UN])
        slot_row = little("slot_row", [P, UN], I32)
        slot_tok = little("slot_tok", [P, UN], I32)
        slot_gate = little("slot_gate", [P, UN])

        EX = 44
        SLOTS = 3
        stream = [at(f"stream{i}", [P, 4096], EX + 16 * i) for i in range(SLOTS)]
        h_t = at("h_t", [P, KD, NTOK], EX + 48)
        merged = at("merged", [P, KD, NTOK], EX + 48)
        h2_t = at("h2_t", [P, KD, NTOK], EX + 48)
        xhat = at("xhat", [P, TT, D], EX + 60)
        bias_sb = at("bias_sb", [P, 6, H, GW], EX + 60)
        q_t = at("q_t", [P, 4, NTOK], EX + 72)
        k_t = at("k_t", [P, 4, NTOK], EX + 78)
        v_sb = at("v_sb", [P, TT, DATT], EX + 84)
        ck_raw = at("ck_raw", [P, DATT], EX + 90)
        ck_t = at("ck_t", [P, 4, P], EX + 92)
        cv_sb = at("cv_sb", [P, DATT], EX + 94)
        s_sb = at("s_sb", [P, 2, 384], EX + 96)
        e_sb = at("e_sb", [P, 2, 384], EX + 99)
        pt_sb = at("pt_sb", [P, 2, 384], EX + 102)
        gate_r = at("gate_r", [P, 2, CT, RC], EX + 60)
        gate_i = at("gate_i", [P, 2, CT, RC], EX + 72.125)
        gate_e = at("gate_e", [P, 2, CT, RC], EX + 84.25)
        gate_mix = at("gate_mix", [P, 2, D], EX + 97)
        xr_pad = at("xr_pad", [P, CT, RC + 3], EX + 105)
        yg = at("yg", [P, CT, NTOK], EX + 111.125)
        ga = at("ga", [P, KD, NTOK], EX + 117.25)
        gated = at("gated", [P, 6, 512], EX + 117.25)
        gb = at("gb", [P, KD, NTOK], EX + 129.25)
        xc = at("xc", [P, CT, RC], EX + 141.25)
        ob_t = at("ob_t", [P, CT, NTOK], EX + 141.25)
        oa_t = at("oa_t", [P, 4, NTOK], EX + 147.5)
        b_row = at("b_row", [2, 2, 512], EX + 153.5)
        m_row = at("m_row", [2, D], EX + 157.5)
        block_w = at("block_w", [P, 2, 2, CT, P], 12)
        k_new = at("k_new", [P, DATT], 20)
        rpb_pad = at("rpb_pad", [7 * H, P], 22)
        col_mask = at("col_mask", [P, GW], 22.5)
        w_hi = [at(f"w_hi{j}", [P, 2048], EX + 16 * j, F32R) for j in range(NK)]
        w_lo = [at(f"w_lo{j}", [P, 2048], EX + 16 * j + 8, F32R) for j in range(NK)]
        xg = [at(f"xg{i}", [P, D], EX + 48 + 4 * i) for i in range(2)]
        act_sb = at("act_sb", [P, FE], EX + 56)
        silu_sb = at("silu_sb", [P, FE], EX + 57)
        raw = [[at(f"raw{i}_{j}", [P, 2048], EX + 60 + 24 * i + 8 * j) for j in range(NK)] for i in range(RAW)]
        xhat2 = at("xhat2", [P, TT, D], EX + 105)
        hs_t = at("hs_t", [P, 2, NTOK], EX + 108)
        hs_g = at("hs_g", [P, 2, NTOK], EX + 111)
        h2_row = at("h2_row", [P, TT, D], EX + 150.5)
        x_hi = at("x_hi", [P, KD * CAP], EX + 108, F32R)
        x_lo = at("x_lo", [P, KD * CAP], EX + 112, F32R)
        y_sb = [at(f"y_sb{i}", [P, D], EX + 116 + 4 * i) for i in range(2)]
        a_hi = at("a_hi", [P, 2 * CAP], EX + 124, F32R)
        a_lo = at("a_lo", [P, 2 * CAP], EX + 125, F32R)
        rank_tab = at("rank_tab", [P, NTAB, TT], EX + 126)
        row_tab = at("row_tab", [P, NTAB, TT, 5], EX + 128.5, BF16)
        onehot = [at(f"onehot{i}", [P, TT, CAP], EX + 134.5 + 0.75 * i, BF16) for i in range(2)]
        slot_no = at("slot_no", [P, TT, CAP], EX + 136)
        place[0] = EX + 137.5
        limit[0] = EX + 150.5
        w_router_sb = little("w_router_sb", [P, KD, NE])
        score = little("score", [P, TT, NE])
        biased = little("biased", [P, TT, NE])
        group_top = little("group_top", [P, TT, NG, 8])
        group_score = little("group_score", [P, TT, 16])
        best_groups = little("best_groups", [P, TT, 8])
        group_left = little("group_left", [P, TT, 16])
        group_mask = little("group_mask", [P, TT, NG])
        group_pen = little("group_pen", [P, TT, NG])
        masked = little("masked", [P, TT, NE])
        top8 = little("top8", [P, TT, 8])
        left = little("left", [P, TT, NE])
        chosen = little("chosen", [P, TT, NE])
        chosen_b = little("chosen_b", [P, TT, NE], BF16, 2)
        gates = little("gates", [P, TT, NE])
        gate_sum = little("gate_sum", [P, TT])
        ones_row = little("ones_row", [P, NE])
        order = little("order", [P, TT, NE])
        before = little("before", [P, P], BF16, 2)
        before_f = little("before_f", [P, P])
        ones_b = little("ones_b", [P, P], BF16, 2)
        tok_i = little("tok_i", [P, 3, TT], I32)
        tok_hi = little("tok_hi", [P, TT])
        tok_lo = little("tok_lo", [P, TT])
        g_rest = little("g_rest", [P, TT, NE])
        rank_f = little("rank_f", [P, TT, NE])
        picked_at = [60, 68, 84, 92, 76, 100, 0, 8, 16, 24, 32, 40]
        picked = [[at(f"picked{q}_{t}", [P, 2, D], EX + picked_at[TT * q + t]) for t in range(TT)] for q in range(TOPK // 2)]

        rpb_dram = nc.dram_tensor("rpb_dram", (7 * H, GW * P), F32, kind="Internal").ap()
        h2_dram = nc.dram_tensor("h2_dram", (NTOK, D), F32, kind="Internal").ap()
        y_dram = nc.dram_tensor("y_dram", (NTOK * TOPK, D), F32, kind="Internal").ap()

        items = ([("ada", i) for i in range(4)] + [("in", i) for i in range(9)]
                 + [("ada", i) for i in range(4, 12)] + [("pa", 0), ("pb", 0)]
                 + [("out", 0), ("out", 1), ("sgu", 0), ("sd", 0)])
        used = {}
        for n, (kind, i) in enumerate(items):
            used[n] = {"ada": ("ada_mm", i + 1), "in": ("w_mm", 4 * (i + 1) - (i >= 2)),
                       "pa": ("merge_mm", KD), "pb": ("merge_mm", KD), "out": ("out_mm", 3 * (i + 1)),
                       "sgu": ("sh_mm", 4), "sd": ("shd_mm", 6)}[kind]
        slot_of, ready_at, sent = {}, {}, [0] * SLOTS
        for n, it in enumerate(items):
            sent[n % SLOTS] += 16 * (2 if it[0] in ("ada", "sgu") else 1)
            slot_of[it], ready_at[it] = n % SLOTS, sent[n % SLOTS]

        S = {n: sem(n) for n in """x_loaded cond_loaded vec_loaded cache_loaded bias_loaded block_loaded
            late_loaded router_loaded rpb_loaded
            pool_step ident_made pick_made consts mask_made rpb_zero blocks_zero tables_made xg_zero
            sumsq1 rstd1 xhat1 xt1 sumsq2 rstd2 xhat2 xt2 sumsq3 rstd3
            cond_silu ada_mm ada_row m_spread mod_copied h_ready vec_mm vec_copied soft_in soft_exp soft_ln
            decay_ready w_mm w_evac ckt_mm ckt_evac kn_mm kn_evac kv_stored rpb_stored
            s_mm s_ready max_ready exp_done p_ready pt_mm pt_evac o_mm o_evac
            pads_zero conv_done gates_mm gates_tanh e2_done e2_capped root_done a_done gelu_done ob_ready
            hl_ready hl_mm hl_copied hl_stored
            merge_mm merge_done bc_mm bc_evac out_mm out_done h2_ready h2r_mm h2r_evac h2_stored
            router_mm score_done chosen_ready rank_mm passes_ready tables_ready
            sh_mm sh_silu sh_act shd_mm shd_evac
            dve_step pool_turn sp_turn num_step onehot_ready idx_mm idx_ready xgt_mm x_hi_ready x_lo_ready silu_done act_ready
            at_mm a_hi_ready a_lo_ready y_ready x2_ready y_done out_stored""".split()}
        stream_ready = [sem(f"stream_ready{i}") for i in range(SLOTS)]
        gathered = [sem(f"gathered{i}") for i in range(2)]
        scattered = [sem(f"scattered{i}") for i in range(2)]
        picked_loaded = [[sem(f"picked_loaded{q}_{t}") for t in range(TT)] for q in range(TOPK // 2)]
        raw_ready = [[sem(f"raw_ready{i}_{j}") for j in range(NK)] for i in range(RAW)]
        hi_ready = [sem(f"hi_ready{j}") for j in range(NK)]
        lo_ready = [sem(f"lo_ready{j}") for j in range(NK)]
        chunk_used = [sem(f"chunk_used{j}") for j in range(NK)]

        block = ctx.enter_context(nc.Block())

        def link(eng, s):
            count = [0]

            def go(ins):
                count[0] += 1
                ins.then_inc(s, 1)
                eng.wait_ge(s, count[0])
            return go

        def unit(s):
            return (s, 0) if s < H else ((s - H) // 2, 1 + (s - H) % 2)

        def half_rows(h):
            return slice(DH * (h % 2), DH * (h % 2) + DH)

        def out_rows(t):
            return y_prompt[0] if t == 0 else y_sample[0, (t - 1) * P:t * P, :]

        @block.sync
        def _(sp):
            def stream_item(n):
                kind, i = items[n]
                slot, ready = stream[n % SLOTS], stream_ready[n % SLOTS]
                if n >= SLOTS:
                    sp.wait_ge(S[used[n - SLOTS][0]], used[n - SLOTS][1])
                cols = slice(i * 512, (i + 1) * 512)
                as_k = {"pa": 4, "pb": 4}.get(kind, KD)
                dst = slot[:, :].rearrange("p (k n) -> p k n", k=as_k)
                if kind == "ada":
                    sp.dma_start(dst, w_ada[0].rearrange("(p k) n -> p k n", k=KD)[:, :, cols]).then_inc(ready, 16)
                    if i >= 2:
                        sp.wait_ge(S["ada_row"], i - 1)
                    sp.dma_start(b_row[:, i % 2, :], b_ada[0:1, cols].to_broadcast([2, 512])).then_inc(ready, 16)
                elif kind == "in":
                    sp.dma_start(dst, w_in[0].rearrange("(p k) n -> p k n", k=KD)[:, :, cols]).then_inc(ready, 16)
                elif kind in ("pa", "pb"):
                    w = w_pa if kind == "pa" else w_pb
                    sp.dma_start(dst, w[0].rearrange("(k p) n -> p k n", p=P)).then_inc(ready, 16)
                elif kind == "out":
                    sp.dma_start(dst, w_out[0].rearrange("(k p) n -> p k n", p=P)[:, :, cols]).then_inc(ready, 16)
                elif kind == "sgu":
                    sp.dma_start(slot[:, 0:2048], w_gate_s[0].rearrange("(p k) n -> p (k n)", k=KD)).then_inc(ready, 16)
                    sp.dma_start(slot[:, 2048:4096], w_up_s[0].rearrange("(p k) n -> p (k n)", k=KD)).then_inc(ready, 16)
                else:
                    sp.dma_start(slot[:, 0:2048].rearrange("p (k n) -> p k n", k=2),
                                 w_down_s[0].rearrange("(k p) n -> p k n", p=P)).then_inc(ready, 16)

            for n in range(len(items)):
                stream_item(n)
            def load_chunk(i, u, j, e):
                if e is None:
                    e = slice(u, u + 1)
                    if u >= RAW:
                        sp.wait_ge(lo_ready[j], i - RAW + 1)
                else:
                    sp.wait_ge(lo_ready[j], i - (RAW - 1))
                    sp.sem_inc(S["sp_turn"], 1)
                dst, ready = raw[u % RAW][j], raw_ready[u % RAW][j]
                if j < 2:
                    for g, w in enumerate((w_gate_e, w_up_e)):
                        rows = w[0, e].rearrange("a (p h k) n -> (a p) h (k n)", h=2, k=KD // 2)[:, j, :]
                        sp.dma_start(dst[:, g * 1024:(g + 1) * 1024], rows).then_inc(ready, 16)
                else:
                    sp.dma_start(dst[:, :].rearrange("p (k n) -> p k n", k=2),
                                 w_down_e[0, e].rearrange("a (k p) n -> p (a k) n", p=P)).then_inc(ready, 16)

            def load_turn(b, first):
                for u in range(UN):
                    if first and u == 0:
                        sp.wait_ge(S["ob_ready"], 1)
                    if first and u == 1:
                        sp.wait_ge(S["xt2"], 6)
                    for j in range(NK):
                        load_chunk(u if first else b[0] * NE + b[1] * UN + u, u, j,
                                   None if first else bass.ds(b[1] * UN + u, 1))

            load_turn(None, True)
            sp.wait_ge(S["passes_ready"], 1)
            passes = sp.value_load(more_i[0:1, 0:1], min_val=0, max_val=MAXPASS - 1) + 1
            with sp.Fori(1, NE // UN) as b:
                load_turn((0, b), False)
            with sp.If(passes >= 2):
                with sp.Fori(1, passes) as pas:
                    with sp.Fori(0, NE // UN) as b:
                        load_turn((pas, b), False)
            sp.end_ifs()
            for j in range(2):
                sp.wait_ge(lo_ready[j], passes * NE - 1)
                sp.sem_inc(S["sp_turn"], 1)
                for g, w in enumerate((w_gate_e, w_up_e)):
                    sp.dma_start(raw[0][j][:, g * 1024:g * 1024 + 4], w[0, 0, 0:P, 0:4]).then_inc(raw_ready[0][j], 16)
            by_token = y_dram.rearrange("(t p k) n -> t p k n", p=P, k=TOPK)
            for q in range(TOPK // 2):
                for par in range(2):
                    sp.wait_ge(scattered[par], passes * (NE // 2 * 16) + 16 * (1 - (TOPK // 2 - 1 - q)))
                    sp.sem_inc(S["sp_turn"], 1)
                for t in range(TT):
                    n = TT * q + t
                    if n < 6:
                        j = (0, 1, 0, 1, 2, 2)[n]
                        sp.wait_ge(lo_ready[j], passes * NE + (1, 1, 0, 0, -1, 0)[n])
                        sp.sem_inc(S["sp_turn"], 1)
                    elif n < 10:
                        sp.wait_ge(lo_ready[n // 2 - 3], passes * NE + 1)
                        sp.sem_inc(S["sp_turn"], 1)
                    else:
                        sp.wait_ge(chunk_used[2], passes * NE)
                        sp.sem_inc(S["sp_turn"], 1)
                    sp.dma_start(picked[q][t][:, :, :], by_token[t][:, 2 * q:2 * q + 2, :]).then_inc(picked_loaded[q][t], 16)
            for t in range(TT):
                sp.wait_ge(S["y_done"], t + 1)
                sp.dma_start(out_rows(t), x_sb[:, t, :]).then_inc(S["out_stored"], 16)
            sp.wait_ge(S["out_stored"], 16 * TT)

        @block.gpsimd
        def _(pool):
            go = link(pool, S["pool_step"])
            go(pool.memset(ident[:, :], 0.0))
            pool.affine_select(out=ident[:, :], in_=ident[:, :], compare_op=ALU.not_equal, fill=1.0, base=0,
                               pattern=[[-1, P]], channel_multiplier=1).then_inc(S["ident_made"], 1)
            go(pool.memset(pick[:, :, :], 0.0))
            pool.affine_select(out=pick[:, :, :], in_=pick[:, :, :], compare_op=ALU.not_equal, fill=1.0, base=0,
                               pattern=[[-1, 2], [0, P]], channel_multiplier=1).then_inc(S["pick_made"], 1)
            pool.memset(minus_half[:, :], -0.5).then_inc(S["consts"], 1)
            pool.memset(quarter[:, :], 0.25).then_inc(S["consts"], 1)
            pool.memset(one[:, :], 1.0).then_inc(S["consts"], 1)
            pool.memset(rpb_pad[:, :], 0.0).then_inc(S["rpb_zero"], 1)
            pool.memset(block_w[:, :, :, :, :], 0.0).then_inc(S["blocks_zero"], 1)
            go(pool.memset(col_mask[:, :], 0.0))
            for r in range(2):
                rows = slice(GW * r, GW * r + GW)
                low = col_mask[rows, 0:GW - KW]
                go(pool.affine_select(out=low, in_=low, compare_op=ALU.is_ge, fill=-BIG, base=KW // 2,
                                      pattern=[[1, GW - KW]], channel_multiplier=-1))
                high = col_mask[rows, KW:GW]
                ins = pool.affine_select(out=high, in_=high, compare_op=ALU.is_ge, fill=-BIG, base=KW // 2 - 1 - KW,
                                         pattern=[[-1, GW - KW]], channel_multiplier=1)
                ins.then_inc(S["mask_made"], 1)
            pool.wait_ge(S["mask_made"], 2)
            pool.memset(xr_pad[:, :, 0:2], 0.0).then_inc(S["pads_zero"], 1)
            pool.memset(xr_pad[:, :, NCTX + 2:LAT0 + 2], 0.0).then_inc(S["pads_zero"], 1)
            pool.memset(xr_pad[:, :, RC + 2:RC + 3], 0.0).then_inc(S["pads_zero"], 1)

            def rms(n, summed):
                pool.wait_ge(summed, TT)
                go(pool.tensor_scalar(rstd[:, n, :], sumsq[:, n, :], 1.0 / D, EPS, ALU.mult, ALU.add))
                pool.tensor_tensor(rstd[:, n, :], rstd[:, n, :], minus_half[:, :], ALU.pow).then_inc(S[f"rstd{n + 1}"], 1)

            pool.wait_ge(S["consts"], 3)
            rms(0, S["sumsq1"])
            pool.wait_ge(S["merge_done"], KD)
            pool.wait_ge(S["m_spread"], 6)
            pool.wait_ge(S["merge_mm"], KD)
            pool.iota(slot_no[:, :, :], [[0, TT], [1, CAP]], base=0, channel_multiplier=0,
                      allow_small_or_imprecise_dtypes=True).then_inc(S["tables_made"], 1)
            pool.iota(tok_i[:, 0, :], [[P, TT]], base=0, channel_multiplier=1).then_inc(S["tables_made"], 1)
            pool.memset(ones_row[:, :], 1.0).then_inc(S["tables_made"], 1)
            pool.memset(ones_b[:, :], 1.0).then_inc(S["tables_made"], 1)
            go(pool.memset(before_f[:, :], 1.0))
            go(pool.affine_select(out=before_f[:, :], in_=before_f[:, :], compare_op=ALU.is_gt, fill=0.0, base=0,
                                  pattern=[[1, P]], channel_multiplier=-1))
            pool.tensor_copy(before[:, :], before_f[:, :]).then_inc(S["tables_made"], 1)
            pool.memset(group_score[:, :, 8:16], LOWEST).then_inc(S["tables_made"], 1)
            rms(1, S["sumsq2"])
            pool.wait_ge(S["router_mm"], 1)
            pool.wait_ge(S["h2r_mm"], 6)
            pool.wait_ge(S["sh_mm"], 4)
            for i in range(2):
                pool.memset(xg[i][:, :], 0.0).then_inc(S["xg_zero"], 1)

            pool.wait_ge(S["passes_ready"], 1)
            passes = pool.value_load(more_i[0:1, 0:1], min_val=0, max_val=MAXPASS - 1) + 1
            pool.wait_ge(S["h2_stored"], 16 * TT)
            pool.wait_ge(S["xg_zero"], 2)

            for i in range(2):
                pool.dma_start(y_sb[i][:, 0:KD], h2_dram[0:P, 0:KD]).then_inc(scattered[i], 16)

            def gather(i, u):
                pool.wait_ge(S["idx_ready"], i + 1)
                pool.sem_inc(S["pool_turn"], 1)
                pool.indirect_dma_start(xg[u % 2][:, :], None, h2_dram[:, :],
                                        bass.IndirectOffsetOnAxis(ap=slot_tok[:, u % UN:u % UN + 1], axis=0),
                                        bounds_check=NTOK - 1, oob_is_err=False).then_inc(gathered[u % 2], 16)

            def scatter(i, u):
                pool.wait_ge(S["y_ready"], i + 1)
                pool.sem_inc(S["pool_turn"], 1)
                pool.indirect_dma_start(y_dram[:, :],
                                        bass.IndirectOffsetOnAxis(ap=slot_row[:, u % UN:u % UN + 1], axis=0),
                                        y_sb[u % 2][:, :], None, bounds_check=NTOK * TOPK - 1,
                                        oob_is_err=False).then_inc(scattered[u % 2], 16)

            def block_turn(b, first):
                for u in range(UN):
                    i = u if first else b * UN + u
                    pool.wait_ge(S["xgt_mm"], i + 1)
                    gather(i + 2, u + 2)
                    if not (first and u == 0):
                        scatter(i - 1, u - 1)

            gather(0, 0)
            gather(1, 1)
            block_turn(0, True)
            with pool.Fori(1, passes * (NE // UN)) as b:
                block_turn(b, False)
            scatter(passes * NE - 1, UN - 1)
            for s in gathered:
                pool.wait_ge(s, passes * (NE // 2 * 16) + 16)
                pool.sem_inc(S["pool_turn"], 1)
            rms(2, S["sumsq3"])

        @block.scalar
        def _(act):
            for t in range(TT):
                src = x_prompt[0] if t == 0 else x_sample[0, (t - 1) * P:t * P, :]
                act.dma_start(x_sb[:, t, :], src).then_inc(S["x_loaded"], 16)
            act.dma_start(cond_raw[:, 0, :], c_ctx.rearrange("(p k) -> p k", k=KD)).then_inc(S["cond_loaded"], 16)
            act.dma_start(cond_raw[:, 1, :], c[0].rearrange("(p k) -> p k", k=KD)).then_inc(S["cond_loaded"], 16)
            act.dma_start(g1_sb[:, :], norm1_g[0].rearrange("(p k) -> p k", k=KD)).then_inc(S["cond_loaded"], 16)
            act.dma_start(g2_sb[:, :], norm2_g[0].rearrange("(p k) -> p k", k=KD)).then_inc(S["cond_loaded"], 16)
            at_row = 0
            for ap, n in ((conv_w[0], 16), (conv_b, 4), (rg_ba[0], 8), (rg_bx[0], 8), (rg_lam[0], 8),
                          (state_f[0], 4), (state_b[0], 4)):
                act.dma_start(vec_rows[at_row:at_row + n, :], ap.rearrange("a (t p) -> (a t) p", p=P)).then_inc(S["vec_loaded"], 16)
                at_row += n
            act.wait_ge(S["rpb_zero"], 1)
            for d in range(7):
                act.dma_start(rpb_pad[d * H:(d + 1) * H, P // 2 - KW:P // 2 + KW - 1],
                              rpb[0, :, d + 4, :]).then_inc(S["rpb_loaded"], 16)
            act.wait_ge(S["rpb_loaded"], 7 * 16)
            act.dma_start(rpb_dram.rearrange("r (w c) -> r w c", c=P),
                          rpb_pad[:, :].unsqueeze(1).to_broadcast([7 * H, GW, P])).then_inc(S["rpb_stored"], 16)
            act.dma_start(ck_raw[:, :], cache_k[0, 0].rearrange("s h d -> s (h d)")).then_inc(S["cache_loaded"], 16)
            act.dma_start(cv_sb[:, :], cache_v[0, 0].rearrange("s h d -> s (h d)")).then_inc(S["cache_loaded"], 16)
            act.wait_ge(S["blocks_zero"], 1)
            for d in range(2):
                for kind, w in enumerate((rg_wa, rg_wx)):
                    for par in range(2):
                        rows = slice(DH * par, DH * par + DH)
                        act.dma_start(block_w[rows, d, kind, :, DH * par:DH * par + DH],
                                      w[0, d].rearrange("(t a) d e -> a d t e", a=2)[par]).then_inc(S["block_loaded"], 16)
            act.dma_start(final_g_sb[:, :], final_g.rearrange("(a n) -> a n", a=1).to_broadcast([P, D])).then_inc(S["late_loaded"], 16)
            act.dma_start(router_b[:, :], b_router[0:1, :].to_broadcast([P, NE])).then_inc(S["late_loaded"], 16)
            act.wait_ge(S["x_loaded"], 16 * TT)

            def squares(n, junk, signal):
                for t in range(TT):
                    act.activation(junk[:, t, :], x_sb[:, t, :], ACT.Square,
                                   accum_out=sumsq[:, n, t:t + 1]).then_inc(signal, 1)

            squares(0, xhat, S["sumsq1"])
            act.wait_ge(S["cond_loaded"], 64)
            act.activation(cond_t[:, :, :].rearrange("p k c -> p c k"), cond_raw[:, :, :], ACT.Silu).then_inc(S["cond_silu"], 1)
            act.wait_ge(S["soft_in"], 1)
            act.activation(abs_lam[:, :], abs_lam[:, :], ACT.Exp, scale=-1.0).then_inc(S["soft_exp"], 1)
            act.wait_ge(S["soft_exp"], 1)
            act.wait_ge(S["consts"], 3)
            act.activation(softplus[:, :], abs_lam[:, :], ACT.Ln, bias=one[:, 0:1]).then_inc(S["soft_ln"], 1)

            def mod_copy(i):
                act.wait_ge(S["m_spread"], i + 1)
                act.activation(mod_t[:, i, :, :].rearrange("p k c -> p (k c)"), bank[7][:, 0:2 * KD],
                               ACT.Copy).then_inc(S["mod_copied"], 1)

            mod_copy(0)
            mod_copy(1)
            act.wait_ge(S["rpb_stored"], 16)
            act.wait_ge(S["xt1"], 6)
            for r in range(2):
                src = bass.AP(rpb_dram.tensor, (1 - r) * H * GW * P + P // 2 - 1, [[P - 1, GW], [GW * P, 6 * H], [1, GW]])
                act.dma_start(bias_sb[GW * r:GW * r + GW, :, :, :].rearrange("p s h c -> p (s h) c"), src).then_inc(S["bias_loaded"], 16)

            def evacuate(n):
                act.wait_ge(S["w_mm"], n + 1)
                src = bank[2 + n % 2]
                if n < 4:
                    ins = act.activation(q_t[:, n, :], src[:, 0:NTOK], ACT.Copy, scale=DH ** -0.5)
                elif n < 8:
                    ins = act.activation(k_t[:, n - 4, :], src[:, 0:NTOK], ACT.Copy)
                elif n < 11:
                    ins = act.activation(v_sb[:, n - 8, :], src[:, :], ACT.Copy)
                elif n < 15:
                    if n == 11:
                        act.wait_ge(S["pads_zero"], 3)
                    act.activation(xr_pad[:, n - 11, 2:2 + NCTX], src[:, 0:NCTX], ACT.Copy)
                    ins = act.activation(xr_pad[:, n - 11, LAT0 + 2:LAT0 + 2 + NLAT], src[:, NCTX:NTOK], ACT.Copy)
                elif n < 19:
                    ins = act.activation(yg[:, n - 15, :], src[:, 0:NTOK], ACT.Copy)
                elif n < 27:
                    ins = act.activation(ga[:, n - 19, :], src[:, 0:NTOK], ACT.Tanh, scale=0.5)
                else:
                    ins = act.activation(gb[:, n - 27, :], src[:, 0:NTOK], ACT.Tanh, scale=0.5)
                ins.then_inc(S["w_evac"], 1)

            for n in range(8):
                evacuate(n)
            act.wait_ge(S["ckt_mm"], 1)
            act.activation(ck_t[:, :, :].rearrange("p m s -> p (m s)"), bank[4][:, :], ACT.Copy).then_inc(S["ckt_evac"], 1)
            for n in range(8, 11):
                evacuate(n)
            act.wait_ge(S["kn_mm"], 1)
            act.activation(k_new[:, :], bank[6][:, :], ACT.Copy).then_inc(S["kn_evac"], 1)
            act.wait_ge(S["kn_evac"], 1)
            act.wait_ge(S["w_evac"], 11)
            act.dma_start(new_k[0, 0].rearrange("s h d -> s (h d)"), k_new[:, :]).then_inc(S["kv_stored"], 16)
            act.dma_start(new_v[0, 0].rearrange("s h d -> s (h d)"), v_sb[:, 0, :]).then_inc(S["kv_stored"], 16)
            for s in range(NSTEP + 2):
                if s < NSTEP:
                    h, t = unit(s)
                    act.wait_ge(S["max_ready"], s + 1)
                    if s >= 2:
                        act.wait_ge(S["pt_mm"], s - 1)
                    if t == 0:
                        ins = act.activation(e_sb[:, s % 2, 0:NCTX], bank[s % 2][:, 0:NCTX], ACT.Exp,
                                             bias=neg_max[:, s % 2:s % 2 + 1], accum_out=row_sum[:, s % 2:s % 2 + 1])
                    else:
                        ins = act.activation(e_sb[:, s % 2, :], s_sb[:, s % 2, :], ACT.Exp,
                                             bias=neg_max[:, s % 2:s % 2 + 1], accum_out=row_sum[:, s % 2:s % 2 + 1])
                    ins.then_inc(S["exp_done"], 1)
                    evacuate(11 + s)
                if s >= 2:
                    h, t = unit(s - 2)
                    rows = half_rows(h)
                    act.wait_ge(S["o_mm"], s - 1)
                    act.activation(oa_t[rows, h // 2, t * P:(t + 1) * P], bank[6 + s % 2][rows, 0:P],
                                   ACT.Copy).then_inc(S["o_evac"], 1)
            act.wait_ge(S["kv_stored"], 32)
            act.wait_ge(S["decay_ready"], 1)
            n = 0
            for kind, dst in enumerate((gate_r, gate_i)):
                for d in range(2):
                    for t in range(CT):
                        act.wait_ge(S["gates_mm"], n + 1)
                        j = kind * 8 + d * CT + t
                        act.activation(dst[:, d, t, :], bank[n % 4][:, 0:RC], ACT.Tanh, scale=0.5,
                                       bias=half_b[:, j:j + 1]).then_inc(S["gates_tanh"], 1)
                        n += 1
            act.wait_ge(S["gates_tanh"], 16)
            for d in range(2):
                for t in range(CT):
                    j = d * CT + t
                    act.activation(gate_e[:, d, t, :], gate_r[:, d, t, :], ACT.Exp, scale=decay2[:, j:j + 1],
                                   bias=decay2[:, j:j + 1]).then_inc(S["e2_done"], 1)
            act.wait_ge(S["e2_done"], 8)
            for d in range(2):
                for t in range(CT):
                    j = d * CT + t
                    act.activation(gate_r[:, d, t, :], gate_r[:, d, t, :], ACT.Exp, scale=decay[:, j:j + 1],
                                   bias=decay[:, j:j + 1]).then_inc(S["a_done"], 1)
            act.wait_ge(S["e2_capped"], 1)
            act.activation(gate_e[:, :, :, :], gate_e[:, :, :, :], ACT.Sqrt, scale=-0.25,
                           bias=quarter[:, 0:1]).then_inc(S["root_done"], 1)
            act.activation(yg[:, :, :], yg[:, :, :], ACT.Gelu_apprx_tanh).then_inc(S["gelu_done"], 1)

            def spread_copy(i, dst, scale):
                for n in range(4):
                    at_n = n + (4 if i == 5 else 0)
                    act.wait_ge(S["bc_mm"], at_n + 1)
                    act.activation(dst[:, n // 2, 512 * (n % 2):512 * (n % 2) + 512], bank[4 + n % 2][:, :],
                                   ACT.Copy, scale=scale).then_inc(S["bc_evac"], 1)

            spread_copy(2, gate_mix, 0.5)
            mod_copy(3)
            mod_copy(4)
            spread_copy(5, gate_ffn, 1.0)
            act.wait_ge(S["hl_mm"], 1)
            act.activation(h_last_rows[:, :], bank[6][0:8, 0:P], ACT.Copy).then_inc(S["hl_copied"], 1)
            act.wait_ge(S["hl_copied"], 1)
            act.dma_start(new_hf[0].rearrange("a (t p) -> (a t) p", p=P), h_last_rows[0:4, :]).then_inc(S["hl_stored"], 16)
            act.dma_start(new_hb[0].rearrange("a (t p) -> (a t) p", p=P), h_last_rows[4:8, :]).then_inc(S["hl_stored"], 16)
            act.wait_ge(S["merge_done"], KD)
            act.wait_ge(S["m_spread"], 6)
            act.dma_start(w_router_sb[:, :, :], w_router[0].rearrange("(p k) n -> p k n", k=KD)).then_inc(S["router_loaded"], 16)
            act.wait_ge(S["out_done"], 6)
            squares(1, xhat2, S["sumsq2"])
            act.wait_ge(S["router_mm"], 1)
            act.activation(score[:, :, :].rearrange("p t e -> p (t e)"), bank[0][:, 0:TT * NE],
                           ACT.Sigmoid).then_inc(S["score_done"], 1)
            for t in range(TT):
                for half in range(2):
                    n = 2 * t + half
                    act.wait_ge(S["h2r_mm"], n + 1)
                    act.activation(h2_row[:, t, 512 * half:512 * half + 512], bank[6 + n % 2][:, :],
                                   ACT.Copy).then_inc(S["h2r_evac"], 1)
                act.wait_ge(S["h2r_evac"], 2 * t + 2)
                act.dma_start(h2_dram[t * P:(t + 1) * P, :], h2_row[:, t, :]).then_inc(S["h2_stored"], 16)
            for m in range(2):
                act.wait_ge(S["sh_mm"], m + 1)
                act.activation(hs_g[:, m, :], bank[2 + m][:, 0:NTOK], ACT.Silu).then_inc(S["sh_silu"], 1)
            act.wait_ge(S["kv_stored"], 32)
            for n in range(6):
                act.wait_ge(S["shd_mm"], n + 1)
                act.activation(shared_sb[:, n // 2, 512 * (n % 2):512 * (n % 2) + 512], bank[6 + n % 2][:, :],
                               ACT.Copy).then_inc(S["shd_evac"], 1)
            act.wait_ge(S["passes_ready"], 1)
            passes = act.value_load(more_i[0:1, 0:1], min_val=0, max_val=MAXPASS - 1) + 1
            act.wait_ge(S["h2_stored"], 16 * TT)

            def hi(i, u, j, first):
                if first:
                    act.wait_ge(raw_ready[u % RAW][j], (16 if j == 2 else 32) * (u // RAW + 1))
                    if u:
                        act.wait_ge(chunk_used[j], u)
                else:
                    act.wait_ge(raw_ready[u % RAW][j], (i - u % RAW) * ((16 if j == 2 else 32) // RAW) + (16 if j == 2 else 32))
                    act.wait_ge(chunk_used[j], i)
                act.activation(w_hi[j][:, :], raw[u % RAW][j][:, :], ACT.Copy).then_inc(hi_ready[j], 1)

            def x_high(i):
                act.wait_ge(S["xgt_mm"], i + 1)
                for half in range(2):
                    act.activation(x_hi[:, half * 512:half * 512 + 512], bank[half][:, :], ACT.Copy).then_inc(S["x_hi_ready"], 1)

            def rows_out(i, u, first):
                act.wait_ge(chunk_used[2], i + 1)
                act.wait_ge(S["idx_ready"], i + 1)
                act.wait_ge(scattered[u % 2], 16 * (u // 2 + 1) if first else (i - u % 2) * 8 + 16)
                for half in range(2):
                    ins = act.activation(y_sb[u % 2][:, half * 512:half * 512 + 512], bank[5 + half][:, :], ACT.Copy,
                                         scale=slot_gate[:, u:u + 1])
                ins.then_inc(S["y_ready"], 1)

            def block_turn(b, first):
                for u in range(UN):
                    i = u if first else b * UN + u
                    head = first and u == 0
                    if not head:
                        hi(i - 1, (u - 1) % UN, 2, first and u > 0)
                    hi(i + 1, u + 1, 0, first)
                    act.wait_ge(chunk_used[1], i + 1)
                    act.activation(silu_sb[:, :], bank[2 + u % 2][:, 0:FE], ACT.Silu).then_inc(S["silu_done"], 1)
                    x_high(i + 1)
                    hi(i + 1, u + 1, 1, first)
                    if not head:
                        rows_out(i - 1, (u - 1) % UN, first)
                    act.wait_ge(S["at_mm"], i + 1)
                    act.activation(a_hi[:, :], bank[4][:, 0:FE], ACT.Copy).then_inc(S["a_hi_ready"], 1)

            hi(0, 0, 0, True)
            hi(0, 0, 1, True)
            x_high(0)
            block_turn(0, True)
            with act.Fori(1, passes * (NE // UN)) as b:
                block_turn(b, False)
            hi(passes * NE - 1, UN - 1, 2, False)
            rows_out(passes * NE - 1, UN - 1, False)
            act.wait_ge(S["x2_ready"], 3)
            for t in range(TT):
                act.activation(picked[0][t][:, 0, :], x_sb[:, t, :], ACT.Square,
                               accum_out=sumsq[:, 2, t:t + 1]).then_inc(S["sumsq3"], 1)
            act.wait_ge(S["hl_stored"], 32)

        @block.tensor
        def _(pe):
            def arrived(it):
                pe.wait_ge(stream_ready[slot_of[it]], ready_at[it])
                return stream[slot_of[it]]

            pe.wait_ge(S["ident_made"], 1)
            pe.wait_ge(S["vec_loaded"], 7 * 16)
            pe.transpose(bank[7][:, 0:NVEC], vec_rows[:, :], ident[0:NVEC, 0:NVEC]).then_inc(S["vec_mm"], 1)
            for t in range(TT):
                pe.wait_ge(S["xhat1"], t + 1)
                for half in range(2):
                    for j in range(4):
                        k = 4 * half + j
                        mm = pe.transpose(bank[2 * t + half][:, j * P:(j + 1) * P], xhat[:, t, k:D:KD], ident[:, :])
                    mm.then_inc(S["xt1"], 1)

            def modulation(i):
                for half in range(2):
                    cidx = 2 * i + half
                    w = arrived(("ada", cidx))
                    if cidx == 0:
                        pe.wait_ge(S["cond_silu"], 1)
                    else:
                        pe.wait_ge(S["ada_row"], cidx)
                    for k in range(KD):
                        mm = pe.matmul(bank[6][0:2, :], cond_t[:, k, :], w[:, k * 512:(k + 1) * 512],
                                       start=(k == 0), stop=(k == KD - 1))
                    mm.then_inc(S["ada_mm"], 1)
                pe.wait_ge(S["ada_row"], 2 * i + 2)
                if i in (2, 5):
                    for n in range(4):
                        at_n = n + (4 if i == 5 else 0)
                        if at_n >= 2:
                            pe.wait_ge(S["bc_evac"], at_n - 1)
                        if n == 0:
                            pe.wait_ge(S["pick_made"], 1)
                        mm = pe.matmul(bank[4 + n % 2][:, :], pick[:, n // 2, :], m_row[:, 512 * (n % 2):512 * (n % 2) + 512],
                                       start=True, stop=True)
                        mm.then_inc(S["bc_mm"], 1)
                    pe.wait_ge(S["bc_mm"], at_n + 1)
                    pe.sem_inc(S["m_spread"], 1)
                else:
                    if i == 0:
                        pe.wait_ge(S["vec_copied"], 1)
                    else:
                        pe.wait_ge(S["mod_copied"], {1: 1, 3: 2, 4: 3}[i])
                    for k in range(KD):
                        mm = pe.transpose(bank[7][:, 2 * k:2 * k + 2], m_row[:, k:D:KD], ident[0:2, 0:2])
                    mm.then_inc(S["m_spread"], 1)

            modulation(0)
            modulation(1)
            pe.wait_ge(S["h_ready"], 3)

            def project(n):
                if n >= 2:
                    pe.wait_ge(S["w_evac"], n - 1)
                out = bank[2 + n % 2]
                if 8 <= n < 11:
                    w = arrived(("in", 2))
                    for k in range(KD):
                        mm = pe.matmul(out[:, :], h_t[:, k, (n - 8) * P:(n - 7) * P], w[:, k * 512:(k + 1) * 512],
                                       start=(k == 0), stop=(k == KD - 1))
                else:
                    item, m = divmod(n if n < 8 else n + 1, 4)
                    w = arrived(("in", item))
                    for k in range(KD):
                        mm = pe.matmul(out[:, 0:NTOK], w[:, k * 512 + m * P:k * 512 + (m + 1) * P], h_t[:, k, :],
                                       start=(k == 0), stop=(k == KD - 1))
                mm.then_inc(S["w_mm"], 1)

            for n in range(8):
                project(n)
            pe.wait_ge(S["cache_loaded"], 32)
            for m in range(4):
                mm = pe.transpose(bank[4][:, m * P:(m + 1) * P], ck_raw[:, m * P:(m + 1) * P], ident[:, :])
            mm.then_inc(S["ckt_mm"], 1)
            for n in range(8, 11):
                project(n)
            for m in range(4):
                mm = pe.transpose(bank[6][:, m * P:(m + 1) * P], k_t[:, m, 0:NCTX], ident[:, :])
            mm.then_inc(S["kn_mm"], 1)

            def scores(s):
                h, t = unit(s)
                rows = half_rows(h)
                if s >= 2:
                    pe.wait_ge(S["exp_done"], s - 1)
                q = q_t[rows, h // 2, t * P:(t + 1) * P]
                if t == 0:
                    mm = pe.matmul(bank[s % 2][:, 0:NCTX], q, k_t[rows, h // 2, 0:NCTX], start=True, stop=True)
                else:
                    pe.matmul(bank[s % 2][:, 0:NLAT], q, k_t[rows, h // 2, NCTX:NTOK], start=True, stop=True)
                    mm = pe.matmul(bank[s % 2][:, NLAT:384], q, ck_t[rows, h // 2, :], start=True, stop=True)
                mm.then_inc(S["s_mm"], 1)

            def turn(s):
                pe.wait_ge(S["p_ready"], s + 1)
                if s >= 2:
                    pe.wait_ge(S["pt_evac"], s - 1)
                for j in range(1 if s < H else 3):
                    mm = pe.transpose(bank[4 + s % 2][:, j * P:(j + 1) * P], e_sb[:, s % 2, j * P:(j + 1) * P], ident[:, :])
                mm.then_inc(S["pt_mm"], 1)

            def values(s):
                h, t = unit(s)
                rows = half_rows(h)
                pe.wait_ge(S["pt_evac"], s + 1)
                if s >= 2:
                    pe.wait_ge(S["o_evac"], s - 1)
                heads = slice(h * DH, (h + 1) * DH)
                vs = [v_sb[:, 0, heads]] if t == 0 else [v_sb[:, 1, heads], v_sb[:, 2, heads], cv_sb[:, heads]]
                for j, v in enumerate(vs):
                    mm = pe.matmul(bank[6 + s % 2][rows, 0:P], v, pt_sb[:, s % 2, j * P:(j + 1) * P],
                                   start=(j == 0), stop=(j == len(vs) - 1))
                mm.then_inc(S["o_mm"], 1)

            pe.wait_ge(S["ckt_evac"], 1)
            pe.wait_ge(S["kn_evac"], 1)
            for s in range(NSTEP + 2):
                if s < NSTEP:
                    scores(s)
                    project(11 + s)
                if 1 <= s <= NSTEP:
                    turn(s - 1)
                if s >= 2:
                    values(s - 2)
            pe.wait_ge(S["block_loaded"], 8 * 16)
            pe.wait_ge(S["conv_done"], 1)
            pe.wait_ge(S["w_evac"], 35)
            n = 0
            for kind in range(2):
                for d in range(2):
                    for t in range(CT):
                        if n >= 4:
                            pe.wait_ge(S["gates_tanh"], n - 3)
                        pe.matmul(bank[n % 4][:, 0:RC], block_w[:, d, kind, t, :], xc[:, t, :],
                                  start=True, stop=True).then_inc(S["gates_mm"], 1)
                        n += 1
            pe.wait_ge(S["o_evac"], NSTEP)
            for i in range(2, 6):
                modulation(i)
            wa, wb = arrived(("pa", 0)), arrived(("pb", 0))
            pe.wait_ge(S["gates_tanh"], 16)
            pe.wait_ge(S["ob_ready"], 1)
            for m in range(KD):
                if m >= 2:
                    pe.wait_ge(S["merge_done"], m - 1)
                for out, w, o in ((bank[2 * (m % 2)], wa, oa_t), (bank[2 * (m % 2) + 1], wb, ob_t)):
                    for k in range(4):
                        mm = pe.matmul(out[:, 0:NTOK], w[:, k * D + m * P:k * D + (m + 1) * P], o[:, k, :],
                                       start=(k == 0), stop=(k == 3))
                mm.then_inc(S["merge_mm"], 1)
            pe.wait_ge(S["hl_ready"], 1)
            pe.transpose(bank[6][0:8, 0:P], h_last[:, :], ident[:, :]).then_inc(S["hl_mm"], 1)
            pe.wait_ge(S["merge_done"], KD)
            for half in range(2):
                w = arrived(("out", half))
                for t in range(TT):
                    n = 3 * half + t
                    if n >= 4:
                        pe.wait_ge(S["out_done"], n - 3)
                    for k in range(KD):
                        mm = pe.matmul(bank[n % 4][:, :], merged[:, k, t * P:(t + 1) * P], w[:, k * 512:(k + 1) * 512],
                                       start=(k == 0), stop=(k == KD - 1))
                    mm.then_inc(S["out_mm"], 1)
            for t in range(TT):
                pe.wait_ge(S["xhat2"], t + 1)
                for half in range(2):
                    n = 2 * t + half
                    if n >= 2:
                        pe.wait_ge(S["h2_ready"], n - 1)
                    else:
                        pe.wait_ge(S["bc_evac"], 8)
                    for j in range(4):
                        k = 4 * half + j
                        mm = pe.transpose(bank[4 + n % 2][:, j * P:(j + 1) * P], xhat2[:, t, k:D:KD], ident[:, :])
                    mm.then_inc(S["xt2"], 1)
            pe.wait_ge(S["h2_ready"], 6)
            pe.wait_ge(S["router_loaded"], 16)
            for t in range(TT):
                for k in range(KD):
                    mm = pe.matmul(bank[0][:, t * NE:(t + 1) * NE], h2_t[:, k, t * P:(t + 1) * P], w_router_sb[:, k, :],
                                   start=(k == 0), stop=(k == KD - 1))
            mm.then_inc(S["router_mm"], 1)
            pe.wait_ge(S["hl_copied"], 1)
            for n in range(6):
                t, half = divmod(n, 2)
                if n >= 2:
                    pe.wait_ge(S["h2r_evac"], n - 1)
                for j in range(4):
                    mm = pe.transpose(bank[6 + n % 2][:, j * P:(j + 1) * P], h2_t[:, 4 * half + j, t * P:(t + 1) * P], ident[:, :])
                mm.then_inc(S["h2r_mm"], 1)
            w = arrived(("sgu", 0))
            for m in range(4):
                kind, half = divmod(m, 2)
                for k in range(KD):
                    mm = pe.matmul(bank[2 + m][:, 0:NTOK], w[:, kind * 2048 + k * FE + half * P:kind * 2048 + k * FE + (half + 1) * P],
                                   h2_t[:, k, :], start=(k == 0), stop=(k == KD - 1))
                mm.then_inc(S["sh_mm"], 1)
            pe.wait_ge(S["chosen_ready"], 1)
            pe.wait_ge(S["tables_made"], 6)
            for t in range(TT + 1):
                lhs = [ones_b] * min(t, TT) + [before] * (t < TT)
                for j, m in enumerate(lhs):
                    mm = pe.matmul(bank[1][:, t * NE:(t + 1) * NE], m[:, :], chosen_b[:, j, :],
                                   start=(j == 0), stop=(j == len(lhs) - 1))
            mm.then_inc(S["rank_mm"], 1)
            w = arrived(("sd", 0))
            pe.wait_ge(S["sh_act"], 2)
            for n in range(6):
                t, half = divmod(n, 2)
                if n < 2:
                    pe.wait_ge(S["h2r_evac"], 5 + n)
                else:
                    pe.wait_ge(S["shd_evac"], n - 1)
                for k in range(2):
                    mm = pe.matmul(bank[6 + n % 2][:, :], hs_t[:, k, t * P:(t + 1) * P],
                                   w[:, k * D + 512 * half:k * D + 512 * half + 512], start=(k == 0), stop=(k == 1))
                mm.then_inc(S["shd_mm"], 1)
            pe.wait_ge(S["passes_ready"], 1)
            passes = pe.value_load(more_i[0:1, 0:1], min_val=0, max_val=MAXPASS - 1) + 1
            pe.wait_ge(S["shd_evac"], 6)
            pe.wait_ge(S["tables_ready"], 1)
            def block_rows(i, u):
                pe.wait_ge(S["onehot_ready"], i + 1)
                for t in range(TT):
                    mm = pe.matmul(bank[7][:, 0:5], onehot[u % 2][:, t, :], row_tab[:, bass.ds(i, 1), t, :]
                                   .rearrange("p a c -> p (a c)"), start=(t == 0), stop=(t == TT - 1))
                mm.then_inc(S["idx_mm"], 1)

            def turn_tokens(i, u, first):
                pe.wait_ge(gathered[u % 2], 16 * (u // 2 + 1) if first else (i - u % 2) * 8 + 16)
                for k in range(KD):
                    mm = pe.transpose(bank[k // 4][:, (k % 4) * P:(k % 4 + 1) * P], xg[u % 2][:, k * P:(k + 1) * P], ident[:, :])
                mm.then_inc(S["xgt_mm"], 1)

            def three_products(out, high, low, w_high, w_low, start, stop):
                pe.matmul(out, low, w_high, start=start, stop=False)
                pe.matmul(out, high, w_low, start=False, stop=False)
                return pe.matmul(out, high, w_high, start=False, stop=stop)

            def gate_up(i, u, j):
                pe.wait_ge(lo_ready[j], i + 1)
                if j == 0:
                    pe.wait_ge(S["x_hi_ready"], 2 * i + 2)
                    pe.wait_ge(S["x_lo_ready"], 2 * i + 2)
                wide = [w[j][:, :].rearrange("p (g k n) -> p g k n", g=2, n=FE) for w in (w_hi, w_lo)]
                for k in range(KD // 2):
                    cols = slice((4 * j + k) * CAP, (4 * j + k + 1) * CAP)
                    mm = three_products(bank[2 + u % 2][:, :].rearrange("p (g n) -> p g n", g=2), x_hi[:, cols], x_lo[:, cols],
                                        wide[0][:, :, k, :], wide[1][:, :, k, :], j == 0 and k == 0, j == 1 and k == 3)
                mm.then_inc(chunk_used[j], 1)

            def down(i, first):
                pe.wait_ge(lo_ready[2], i + 1)
                pe.wait_ge(S["a_lo_ready"], i + 1)
                if not first:
                    pe.wait_ge(S["y_ready"], i)
                for half in range(2):
                    for k in range(2):
                        cols, wc = slice(k * CAP, (k + 1) * CAP), slice(k * D + 512 * half, k * D + 512 * half + 512)
                        mm = three_products(bank[5 + half][:, :], a_hi[:, cols], a_lo[:, cols],
                                            w_hi[2][:, wc], w_lo[2][:, wc], k == 0, k == 1)
                mm.then_inc(chunk_used[2], 1)

            def block_turn(b, first):
                for u in range(UN):
                    i = u if first else b * UN + u
                    gate_up(i, u, 0)
                    gate_up(i, u, 1)
                    turn_tokens(i + 1, u + 1, first)
                    if not (first and u == 0):
                        down(i - 1, first and u == 1)
                    pe.wait_ge(S["act_ready"], i + 1)
                    for k in range(2):
                        mm = pe.transpose(bank[4][:, k * P:(k + 1) * P], act_sb[:, k * P:(k + 1) * P], ident[:, :])
                    mm.then_inc(S["at_mm"], 1)
                    pe.wait_ge(S["idx_ready"], i + 3)
                    block_rows(i + 3, u + 3)

            block_rows(0, 0)
            for i in (1, 2):
                pe.wait_ge(S["idx_ready"], i)
                block_rows(i, i)
            turn_tokens(0, 0, True)
            block_turn(0, True)
            with pe.Fori(1, passes * (NE // UN)) as b:
                block_turn(b, False)
            down(passes * NE - 1, False)

        @block.vector
        def _(dve):
            go = link(dve, S["dve_step"])
            CW, CB, BA, BX, LAM, H0 = 0, 16, 20, 28, 36, 44
            dve.wait_ge(S["vec_mm"], 1)
            dve.tensor_copy(vec_t[:, :], bank[7][:, 0:NVEC]).then_inc(S["vec_copied"], 1)
            dve.wait_ge(S["vec_copied"], 1)
            go(dve.tensor_scalar(neg_lam[:, :], vec_t[:, LAM:LAM + 8], -1.0, None, ALU.mult))
            dve.tensor_tensor(abs_lam[:, :], vec_t[:, LAM:LAM + 8], neg_lam[:, :], ALU.max).then_inc(S["soft_in"], 1)
            go(dve.tensor_scalar(half_b[:, :], vec_t[:, BA:BA + 16], 0.5, None, ALU.mult))

            def normalise(n, t, dst, signal):
                dve.tensor_scalar(dst[:, t, :], x_sb[:, t, :], rstd[:, n, t:t + 1], None, ALU.mult).then_inc(signal, 1)

            dve.wait_ge(S["rstd1"], 1)
            dve.wait_ge(S["sumsq1"], 3)
            for t in range(TT):
                normalise(0, t, xhat, S["xhat1"])
            dve.wait_ge(S["soft_ln"], 1)
            go(dve.scalar_tensor_tensor(softplus[:, :], neg_lam[:, :], 0.0, softplus[:, :], ALU.max, ALU.add))
            go(dve.tensor_scalar(decay2[:, :], softplus[:, :], -RG_C, None, ALU.mult))
            dve.tensor_scalar(decay[:, :], softplus[:, :], -RG_C / 2, None, ALU.mult).then_inc(S["decay_ready"], 1)

            def row(cidx):
                dve.wait_ge(S["ada_mm"], cidx + 1)
                if cidx % 2 == 0 and cidx:
                    dve.wait_ge(S["m_spread"], cidx // 2)
                dve.tensor_tensor(m_row[:, 512 * (cidx % 2):512 * (cidx % 2) + 512], bank[6][0:2, :],
                                  b_row[:, cidx % 2, :], ALU.add).then_inc(S["ada_row"], 1)

            for cidx in range(4):
                row(cidx)

            def scales(dst, i, g):
                dve.wait_ge(S["cond_loaded"], 64)
                go(dve.scalar_tensor_tensor(dst[:, :, :], mod_t[:, i, :, :], 1.0,
                                            g[:, :].unsqueeze(2).to_broadcast([P, KD, 2]), ALU.add, ALU.mult))

            dve.wait_ge(S["mod_copied"], 2)
            scales(scale1, 1, g1_sb)
            for t in range(TT):
                cond = int(t > 0)
                for k in range(KD):
                    dve.wait_ge(S["xt1"], 2 * t + k // 4 + 1)
                    ins = dve.tensor_scalar(h_t[:, k, t * P:(t + 1) * P], bank[2 * t + k // 4][:, (k % 4) * P:(k % 4 + 1) * P],
                                            scale1[:, k, cond:cond + 1], mod_t[:, 0, k, cond:cond + 1], ALU.mult, ALU.add)
                ins.then_inc(S["h_ready"], 1)
            dve.wait_ge(S["bias_loaded"], 32)
            dve.wait_ge(S["mask_made"], 2)
            go(dve.tensor_tensor(bias_sb[:, :, :, :].rearrange("p s h c -> p (s h) c"),
                                 bias_sb[:, :, :, :].rearrange("p s h c -> p (s h) c"),
                                 col_mask[:, :].unsqueeze(1).to_broadcast([P, 6 * H, GW]), ALU.add))
            for s in range(NSTEP + 1):
                if s < NSTEP:
                    h, t = unit(s)
                    b = s % 2
                    dve.wait_ge(S["s_mm"], s + 1)
                    if t == 0:
                        dve.tensor_reduce(neg_max[:, b:b + 1], bank[b][:, 0:NCTX], AX, ALU.max, negate=True).then_inc(S["max_ready"], 1)
                    else:
                        first = 2 if t == 1 else 0
                        dve.tensor_tensor(s_sb[:, b, 0:NLAT].rearrange("p (j c) -> p j c", c=GW),
                                          bank[b][:, 0:NLAT].rearrange("p (j c) -> p j c", c=GW),
                                          bias_sb[:, first:first + 4, h, :], ALU.add)
                        go(dve.tensor_copy(s_sb[:, b, NLAT:384], bank[b][:, NLAT:384]))
                        dve.tensor_reduce(neg_max[:, b:b + 1], s_sb[:, b, :], AX, ALU.max, negate=True).then_inc(S["max_ready"], 1)
                    n = NCTX if t == 0 else 384
                    dve.wait_ge(S["exp_done"], s + 1)
                    go(dve.reciprocal(row_inv[:, b:b + 1], row_sum[:, b:b + 1]))
                    dve.tensor_scalar(e_sb[:, b, 0:n], e_sb[:, b, 0:n], row_inv[:, b:b + 1], None, ALU.mult).then_inc(S["p_ready"], 1)
                if s >= 1:
                    n = NCTX if s - 1 < H else 384
                    dve.wait_ge(S["pt_mm"], s)
                    if s >= 3:
                        dve.wait_ge(S["o_mm"], s - 2)
                    dve.tensor_copy(pt_sb[:, (s - 1) % 2, 0:n], bank[4 + (s - 1) % 2][:, 0:n]).then_inc(S["pt_evac"], 1)
                if 9 <= s < 9 + CT:
                    t = s - 9
                    dve.wait_ge(S["w_evac"], 15)
                    go(dve.tensor_scalar(xc[:, t, :], xr_pad[:, t, 0:RC], vec_t[:, CW + t:CW + t + 1],
                                         vec_t[:, CB + t:CB + t + 1], ALU.mult, ALU.add))
                    for tap in range(1, 4):
                        j = CW + tap * CT + t
                        go(dve.scalar_tensor_tensor(xc[:, t, :], xr_pad[:, t, tap:tap + RC], vec_t[:, j:j + 1],
                                                    xc[:, t, :], ALU.mult, ALU.add))
            dve.engine_nop().then_inc(S["conv_done"], 1)
            row(4)
            dve.wait_ge(S["e2_done"], 8)
            dve.tensor_scalar(gate_e[:, :, :, :], gate_e[:, :, :, :], 1.0, None, ALU.min).then_inc(S["e2_capped"], 1)
            row(5)
            dve.wait_ge(S["gates_tanh"], 16)
            for d in range(2):
                go(dve.scalar_tensor_tensor(gate_i[:, d, :, :], gate_i[:, d, :, :], 1.0, xc[:, :, :], ALU.add, ALU.mult))
            row(6)
            dve.wait_ge(S["root_done"], 1)
            for d in range(2):
                go(dve.tensor_tensor(gate_e[:, d, :, :], gate_e[:, d, :, :], gate_i[:, d, :, :], ALU.mult))
            row(7)
            dve.wait_ge(S["a_done"], 8)
            for d in range(2):
                for t in range(CT):
                    for lo, hi, init in ((0, NCTX, 0.0), (LAT0, RC, vec_t[:, H0 + CT * d + t:H0 + CT * d + t + 1])):
                        cut = slice(lo, hi) if d == 0 else slice(hi - 1, lo - 1 if lo else None, -1)
                        ins = dve.tensor_tensor_scan(gate_i[:, d, t, cut], gate_r[:, d, t, cut], gate_e[:, d, t, cut],
                                                     init, ALU.mult, ALU.add)
                        go(ins)
                row(8 + d)
            go(dve.tensor_copy(h_last[:, 0:CT], gate_i[:, 0, :, NCTX - 1]))
            dve.tensor_copy(h_last[:, CT:2 * CT], gate_i[:, 1, :, 0]).then_inc(S["hl_ready"], 1)
            dve.wait_ge(S["gelu_done"], 1)
            for lo, hi, at_tok in ((0, NCTX, 0), (LAT0, RC, NCTX)):
                dst = ob_t[:, :, at_tok:at_tok + hi - lo]
                go(dve.tensor_tensor(dst, gate_i[:, 0, :, lo:hi], gate_i[:, 1, :, lo:hi], ALU.add))
                go(dve.tensor_tensor(dst, dst, yg[:, :, at_tok:at_tok + hi - lo], ALU.mult))
            row(10)
            dve.engine_nop().then_inc(S["ob_ready"], 1)
            row(11)
            for m in range(KD):
                dve.wait_ge(S["merge_mm"], m + 1)
                for gate, ps in ((ga, bank[2 * (m % 2)]), (gb, bank[2 * (m % 2) + 1])):
                    go(dve.scalar_tensor_tensor(gate[:, m, :], gate[:, m, :], 1.0, ps[:, 0:NTOK], ALU.add, ALU.mult))
                dve.tensor_tensor(merged[:, m, :], ga[:, m, :], gb[:, m, :], ALU.add).then_inc(S["merge_done"], 1)
            dve.wait_ge(S["bc_evac"], 4)
            for n in range(6):
                half, t = divmod(n, 3)
                cols = slice(512 * half, 512 * half + 512)
                dve.wait_ge(S["out_mm"], n + 1)
                go(dve.tensor_tensor(gated[:, n, :], bank[n % 4][:, :], gate_mix[:, int(t > 0), cols], ALU.mult))
                dve.tensor_tensor(x_sb[:, t, cols], x_sb[:, t, cols], gated[:, n, :], ALU.add).then_inc(S["out_done"], 1)
            dve.wait_ge(S["mod_copied"], 4)
            scales(scale2, 4, g2_sb)
            dve.wait_ge(S["rstd2"], 1)
            dve.wait_ge(S["sumsq2"], 3)
            for t in range(TT):
                normalise(1, t, xhat2, S["xhat2"])
            for t in range(TT):
                cond = int(t > 0)
                for k in range(KD):
                    n = 2 * t + k // 4
                    dve.wait_ge(S["xt2"], n + 1)
                    ins = dve.tensor_scalar(h2_t[:, k, t * P:(t + 1) * P], bank[4 + n % 2][:, (k % 4) * P:(k % 4 + 1) * P],
                                            scale2[:, k, cond:cond + 1], mod_t[:, 3, k, cond:cond + 1], ALU.mult, ALU.add)
                    if k % 4 == 3:
                        ins.then_inc(S["h2_ready"], 1)
            dve.wait_ge(S["tables_made"], 6)
            dve.wait_ge(S["late_loaded"], 32)
            dve.wait_ge(S["score_done"], 1)
            go(dve.tensor_tensor(biased[:, :, :], score[:, :, :], router_b[:, :].unsqueeze(1).to_broadcast([P, TT, NE]), ALU.add))
            for t in range(TT):
                for g in range(NG):
                    ins = dve.max(group_top[:, t, g, :], biased[:, t, g * GE:(g + 1) * GE])
            go(ins)
            go(dve.tensor_tensor(group_score[:, :, 0:NG], group_top[:, :, :, 0], group_top[:, :, :, 1], ALU.add))
            for t in range(TT):
                ins = dve.max(best_groups[:, t, :], group_score[:, t, 0:8])
            go(ins)
            go(dve.memset(best_groups[:, :, 4:8], LOWEST))
            for t in range(TT):
                ins = dve.match_replace(group_left[:, t, 0:12], best_groups[:, t, :], group_score[:, t, 0:12], BIG)
            go(ins)
            go(dve.tensor_scalar(group_mask[:, :, :], group_left[:, :, 0:NG], BIG, None, ALU.is_equal))
            go(dve.tensor_scalar(group_pen[:, :, :], group_mask[:, :, :], BIG, -BIG, ALU.mult, ALU.add))
            by_group = lambda ap: ap.rearrange("p t (g e) -> p (t g) e", e=GE)
            spread = lambda ap: ap.rearrange("p t g -> p (t g)").unsqueeze(2).to_broadcast([P, TT * NG, GE])
            go(dve.tensor_tensor(by_group(masked[:, :, :]), by_group(biased[:, :, :]), spread(group_mask[:, :, :]), ALU.mult))
            go(dve.tensor_tensor(by_group(masked[:, :, :]), by_group(masked[:, :, :]), spread(group_pen[:, :, :]), ALU.add))
            for t in range(TT):
                ins = dve.max(top8[:, t, :], masked[:, t, :])
            go(ins)
            for t in range(TT):
                ins = dve.match_replace(left[:, t, :], top8[:, t, :], masked[:, t, :], LOWEST)
            go(ins)
            go(dve.tensor_scalar(chosen[:, :, :], left[:, :, :], LOWEST, None, ALU.is_equal))
            dve.tensor_copy(chosen_b[:, :, :], chosen[:, :, :]).then_inc(S["chosen_ready"], 1)
            for m in range(2):
                dve.wait_ge(S["sh_silu"], m + 1)
                dve.wait_ge(S["sh_mm"], m + 3)
                dve.tensor_tensor(hs_t[:, m, :], hs_g[:, m, :], bank[4 + m][:, 0:NTOK], ALU.mult).then_inc(S["sh_act"], 1)
            go(dve.tensor_tensor(gates[:, :, :], score[:, :, :], chosen[:, :, :], ALU.mult))
            go(dve.tensor_reduce(gate_sum[:, :], gates[:, :, :], AX, ALU.add))
            go(dve.reciprocal(gate_sum[:, :], gate_sum[:, :]))
            for t in range(TT):
                ins = dve.tensor_scalar(gates[:, t, :], gates[:, t, :], gate_sum[:, t:t + 1], SCALED, ALU.mult, ALU.mult)
            go(ins)
            for t in range(TT):
                ins = dve.tensor_tensor_scan(order[:, t, :], ones_row[:, :], chosen[:, t, :], 0.0, ALU.mult, ALU.add)
            go(ins)
            go(dve.tensor_tensor(order[:, :, :], order[:, :, :], chosen[:, :, :], ALU.subtract))
            go(dve.tensor_single_scalar(tok_i[:, 1, :], tok_i[:, 0, :], 4, op=ALU.logical_shift_right))
            go(dve.tensor_single_scalar(tok_i[:, 2, :], tok_i[:, 0, :], 15, op=ALU.bitwise_and))
            go(dve.tensor_scalar(tok_hi[:, :], tok_i[:, 1, :], -128.0, 128.0, ALU.add, ALU.mult))
            go(dve.tensor_scalar(tok_lo[:, :], tok_i[:, 2, :], 8.0, None, ALU.mult))
            go(dve.memset(row_tab[:, NBLK:NTAB, :, :], 0.0))
            for t in range(TT):
                col = lambda j: row_tab[:, 0:NE, t, j]
                go(dve.tensor_scalar(col(0), ones_row[:, :], tok_hi[:, t:t + 1], None, ALU.mult))
                go(dve.tensor_scalar(col(1), order[:, t, :], tok_lo[:, t:t + 1], None, ALU.add))
                go(dve.tensor_copy(col(2), gates[:, t, :]))
                go(dve.tensor_tensor(g_rest[:, t, :], gates[:, t, :], col(2), ALU.subtract))
                go(dve.tensor_copy(col(3), g_rest[:, t, :]))
                go(dve.tensor_tensor(g_rest[:, t, :], g_rest[:, t, :], col(3), ALU.subtract))
                go(dve.tensor_copy(col(4), g_rest[:, t, :]))
            for pas in range(1, MAXPASS):
                go(dve.tensor_copy(row_tab[:, pas * NE:(pas + 1) * NE, :, :], row_tab[:, 0:NE, :, :]))
            dve.wait_ge(S["rank_mm"], 1)
            go(dve.scalar_tensor_tensor(rank_f[:, :, :], bank[1][:, 0:TT * NE].rearrange("p (t e) -> p t e", t=TT), 1.0,
                                        chosen[:, :, :], ALU.add, ALU.mult))
            for pas in range(MAXPASS):
                go(dve.tensor_scalar(rank_tab[:, pas * NE:(pas + 1) * NE, :].rearrange("p e t -> p t e"), rank_f[:, :, :],
                                     -1.0 - CAP * pas, None, ALU.add))
            go(dve.memset(rank_tab[:, NBLK:NTAB, :], -1.0))
            go(dve.tensor_reduce(load_f[:, 0:1], bank[1][:, TT * NE:(TT + 1) * NE], AX, ALU.max))
            go(dve.tensor_scalar(load_f[:, 1:2], load_f[:, 0:1], CAP + 0.5, None, ALU.is_gt))
            go(dve.tensor_scalar(load_f[:, 2:3], load_f[:, 0:1], 2 * CAP + 0.5, None, ALU.is_gt))
            go(dve.tensor_tensor(more_i[:, 0:1], load_f[:, 1:2], load_f[:, 2:3], ALU.add))
            dve.engine_nop().then_inc(S["tables_ready"], 1)
            dve.engine_nop().then_inc(S["passes_ready"], 1)
            passes = dve.value_load(more_i[0:1, 0:1], min_val=0, max_val=MAXPASS - 1) + 1

            def select(i, u):
                dve.tensor_tensor(onehot[u % 2][:, :, :], slot_no[:, :, :],
                                  rank_tab[:, bass.ds(i, 1), :].rearrange("p a t -> p (a t)").unsqueeze(2)
                                  .to_broadcast([P, TT, CAP]), ALU.is_equal).then_inc(S["onehot_ready"], 1)

            def numbers(i, u):
                u = u % UN
                dve.wait_ge(S["idx_mm"], i + 1)
                dve.tensor_reduce(slot_val[:, u:u + 1], bank[7][:, 0:2], AX, ALU.add).then_inc(S["num_step"], 1)
                dve.tensor_reduce(slot_gate[:, u:u + 1], bank[7][:, 2:5], AX, ALU.add).then_inc(S["num_step"], 1)
                dve.wait_ge(S["num_step"], 3 * i + 2)
                dve.tensor_scalar(slot_row[:, u:u + 1], slot_val[:, u:u + 1], float(128 * 128), None, ALU.add).then_inc(S["num_step"], 1)
                dve.wait_ge(S["num_step"], 3 * i + 3)
                dve.tensor_single_scalar(slot_tok[:, u:u + 1], slot_row[:, u:u + 1], 3,
                                         op=ALU.logical_shift_right).then_inc(S["idx_ready"], 1)

            def lo(i, u, j):
                dve.wait_ge(hi_ready[j], i + 1)
                dve.tensor_tensor(w_lo[j][:, :], raw[u % RAW][j][:, :], w_hi[j][:, :].bitcast(F32),
                                  ALU.subtract).then_inc(lo_ready[j], 1)

            def x_low(i):
                for half in range(2):
                    cols = slice(half * 512, half * 512 + 512)
                    dve.wait_ge(S["x_hi_ready"], 2 * i + 1 + half)
                    dve.tensor_tensor(x_lo[:, cols], bank[half][:, :], x_hi[:, cols].bitcast(F32),
                                      ALU.subtract).then_inc(S["x_lo_ready"], 1)

            def block_turn(b, first):
                for u in range(UN):
                    i = u if first else b * UN + u
                    if not (first and u == 0):
                        lo(i - 1, u - 1, 2)
                    lo(i + 1, u + 1, 0)
                    dve.wait_ge(S["silu_done"], i + 1)
                    dve.tensor_tensor(act_sb[:, :], silu_sb[:, :], bank[2 + u % 2][:, FE:2 * FE],
                                      ALU.mult).then_inc(S["act_ready"], 1)
                    x_low(i + 1)
                    lo(i + 1, u + 1, 1)
                    dve.wait_ge(S["a_hi_ready"], i + 1)
                    dve.tensor_tensor(a_lo[:, :], bank[4][:, 0:FE], a_hi[:, :].bitcast(F32), ALU.subtract).then_inc(S["a_lo_ready"], 1)
                    numbers(i + 3, u + 3)
                    select(i + 4, u + 4)

            select(0, 0)
            select(1, 1)
            numbers(0, 0)
            select(2, 2)
            numbers(1, 1)
            select(3, 3)
            numbers(2, 2)
            lo(0, 0, 0)
            lo(0, 0, 1)
            x_low(0)
            block_turn(0, True)
            with dve.Fori(1, passes * (NE // UN)) as b:
                block_turn(b, False)
            lo(passes * NE - 1, UN - 1, 2)
            dve.wait_ge(S["shd_evac"], 6)
            dve.wait_ge(S["bc_evac"], 8)
            for q in range(TOPK // 2):
                for t in range(TT):
                    dve.wait_ge(picked_loaded[q][t], 16)
                    for k in range(2):
                        go(dve.tensor_tensor(shared_sb[:, t, :], shared_sb[:, t, :], picked[q][t][:, k, :], ALU.add))
                    if q == TOPK // 2 - 1:
                        go(dve.tensor_tensor(shared_sb[:, t, :], shared_sb[:, t, :], gate_ffn[:, int(t > 0), :], ALU.mult))
                        dve.tensor_tensor(x_sb[:, t, :], x_sb[:, t, :], shared_sb[:, t, :], ALU.add).then_inc(S["x2_ready"], 1)
            dve.wait_ge(S["rstd3"], 1)
            dve.wait_ge(S["sumsq3"], 3)
            for t in range(TT):
                dve.scalar_tensor_tensor(x_sb[:, t, :], x_sb[:, t, :], rstd[:, 2, t:t + 1], final_g_sb[:, :],
                                         ALU.mult, ALU.mult).then_inc(S["y_done"], 1)


_INS = ['x_prompt', 'x_sample', 'cache_k', 'cache_v', 'state_h_fwd', 'state_h_bwd', 'c', 'c_ctx', 'norm1_g', 'norm2_g',
        'final_g', 'w_ada', 'b_ada', 'w_in', 'rpb', 'conv_w', 'conv_b', 'rg_wa', 'rg_ba', 'rg_wx', 'rg_bx', 'rg_lam',
        'w_pa', 'w_pb', 'w_out', 'w_router', 'b_router', 'w_gate_e', 'w_up_e', 'w_down_e', 'w_gate_s', 'w_up_s', 'w_down_s']
_OUTS = [(1, 128, 1024), (1, 256, 1024), (1, 1, 128, 8, 64), (1, 1, 128, 8, 64), (1, 1, 512), (1, 1, 512)]


def kernel(**inputs):
    import numpy as _np
    import concourse.bacc as _bacc
    from concourse import mybir as _mybir
    from concourse.bass_utils import run_bass_kernel_spmd as _run

    nc = _bacc.Bacc("TRN2", target_bir_lowering=False, num_devices=1)
    arrays, args = {}, []
    for name in _INS:
        a = _np.ascontiguousarray(inputs[name])
        arrays[f"in_{name}_dram"] = a
        args.append(nc.dram_tensor(f"in_{name}_dram", a.shape, _mybir.dt.from_np(a.dtype), kind="ExternalInput").ap())
    for i, shape in enumerate(_OUTS):
        args.append(nc.dram_tensor(f"out_{i}_dram", shape, _mybir.dt.float32, kind="ExternalOutput").ap())
    hybrid_step(nc, *args)
    r = _run(nc, [arrays], core_ids=[0])
    return tuple(r.results[0][f"out_{i}_dram"] for i in range(len(_OUTS)))
```

```python
from contextlib import ExitStack

import concourse.bass as bass
from concourse import mybir

F32 = mybir.dt.float32
BF16 = mybir.dt.bfloat16
I32 = mybir.dt.int32
F32R = mybir.dt.float32r
ALU = mybir.AluOpType
ACT = mybir.ActivationFunctionType
AX = mybir.AxisListType.X

P = 128
D = 1024
KD = D // P
NCTX, NLAT = 128, 256
NTOK = NCTX + NLAT
TT = NTOK // P
H, DH = 8, 64
DATT = H * DH
GW = 64
KH, KW = 8, 16
DRNN = 512
CT = DRNN // P
NE, TOPK, NG = 64, 8, 8
GE = NE // NG
FE = 256
EPS = 1e-6
RG_C = 8.0
SCALED = 2.5
BIG = 1e30
CAP = P
MAXPASS = NTOK // CAP
RAW = 2
UN = 8
NK = 3
NBLK = NE * MAXPASS
RC = 387
LAT0 = 131
NTAB = NBLK + 4
NVEC = 52
LOWEST = -3.0e38
CH = 256
NADA = 6 * D // CH
NSTEP = 24


def hybrid_step(nc, x_prompt, x_sample, cache_k, cache_v, state_f, state_b, c, c_ctx,
                norm1_g, norm2_g, final_g, w_ada, b_ada, w_in, rpb, conv_w, conv_b,
                rg_wa, rg_ba, rg_wx, rg_bx, rg_lam, w_pa, w_pb, w_out,
                w_router, b_router, w_gate_e, w_up_e, w_down_e, w_gate_s, w_up_s, w_down_s,
                y_prompt, y_sample, new_k, new_v, new_hf, new_hb):
    ctx = ExitStack()
    with ctx:
        KB = 1024
        arena = ctx.enter_context(nc.sbuf_tensor("arena", [P, 207 * 256 + 160], F32))
        base = 16512

        def at(name, shape, kb, dt=F32):
            return nc.alloc_sbuf_tensor_at(name, shape, dt, offset=int(base + kb * KB))

        def sem(name):
            return ctx.enter_context(nc.semaphore(name))

        bank = [ctx.enter_context(nc.psum_tensor(f"bank{i}", [P, 512], F32)) for i in range(8)]

        x_sb = at("x_sb", [P, TT, D], 0)
        shared_sb = at("shared_sb", [P, TT, D], 12)
        gate_ffn = at("gate_ffn", [P, 2, D], 24)
        final_g_sb = at("final_g_sb", [P, D], 32)
        small = 36.0
        place, limit = [small], [44]

        def little(name, shape, dt=F32, size=4):
            n = 1
            for s in shape[1:]:
                n *= s
            t = at(name, shape, place[0], dt)
            place[0] += ((n * size + 31) // 32 * 32) / KB
            assert place[0] <= limit[0], name
            return t


        ident = little("ident", [P, P])
        cond_raw = little("cond_raw", [P, 2, KD])
        cond_t = little("cond_t", [P, KD, 2])
        pick = little("pick", [2, 2, P])
        g1_sb = little("g1_sb", [P, KD])
        g2_sb = little("g2_sb", [P, KD])
        mod_t = little("mod_t", [P, 6, KD, 2])
        scale1 = little("scale1", [P, KD, 2])
        scale2 = little("scale2", [P, KD, 2])
        sumsq = little("sumsq", [P, 3, TT])
        minus_half = little("minus_half", [P, TT])
        rstd = little("rstd", [P, 3, TT])
        vec_rows = little("vec_rows", [NVEC, P])
        vec_t = little("vec_t", [P, NVEC])
        half_b = little("half_b", [P, 16])
        neg_lam = little("neg_lam", [P, 8])
        abs_lam = little("abs_lam", [P, 8])
        softplus = little("softplus", [P, 8])
        decay = little("decay", [P, 8])
        decay2 = little("decay2", [P, 8])
        one = little("one", [P, 1])
        quarter = little("quarter", [P, 1])
        h_last = little("h_last", [P, 8])
        h_last_rows = little("h_last_rows", [8, P])
        neg_max = little("neg_max", [P, 2])
        row_sum = little("row_sum", [P, 2])
        row_inv = little("row_inv", [P, 2])
        router_b = little("router_b", [P, NE])
        load_f = little("load_f", [P, 4])
        more_i = little("more_i", [P, 1], I32)
        slot_val = little("slot_val", [P, UN])
        slot_tok = little("slot_tok", [P, UN], I32)
        slot_gate = little("slot_gate", [P, UN])

        EX = 44
        SLOTS, HIGHS = 4, 2
        chunk_raw = [at(f"chunk_raw{i}", [P, 2048], EX + 8 * i) for i in range(SLOTS)]
        chunk_lo = [at(f"chunk_lo{i}", [P, 2048], EX + 8 * i, F32R) for i in range(SLOTS)]
        chunk_hi = [at(f"chunk_hi{i}", [P, 2048], EX + 32 + 8 * i, F32R) for i in range(HIGHS)]
        h_t = at("h_t", [P, KD, NTOK], EX + 48)
        h_lo = at("h_lo", [P, KD, NTOK], EX + 48, F32R)
        h_hi = at("h_hi", [P, KD, NTOK], 24, F32R)
        merged_lo = at("merged_lo", [P, KD, NTOK], EX + 48, F32R)
        merged_hi = at("merged_hi", [P, KD, NTOK], EX + 84.25, F32R)
        h2_hi = at("h2_hi", [P, KD, NTOK], EX + 84, F32R)
        h2_lo = at("h2_lo", [P, KD, NTOK], EX + 96, F32R)
        merged = at("merged", [P, KD, NTOK], EX + 48)
        h2_t = at("h2_t", [P, KD, NTOK], EX + 48)
        xhat = at("xhat", [P, TT, D], EX + 60)
        bias_sb = at("bias_sb", [P, 6, H, GW], EX + 60)
        q_t = at("q_t", [P, 4, NTOK], EX + 72)
        k_t = at("k_t", [P, 4, NTOK], EX + 78)
        v_sb = at("v_sb", [P, TT, DATT], EX + 84)
        ck_raw = at("ck_raw", [P, DATT], EX + 90)
        ck_t = at("ck_t", [P, 4, P], EX + 92)
        cv_sb = at("cv_sb", [P, DATT], EX + 94)
        s_sb = at("s_sb", [P, 2, 384], EX + 96)
        e_sb = at("e_sb", [P, 2, 384], EX + 99)
        pt_sb = at("pt_sb", [P, 2, 384], EX + 102)
        gate_r = at("gate_r", [P, 2, CT, RC], EX + 60)
        gate_i = at("gate_i", [P, 2, CT, RC], EX + 72.125)
        gate_e = at("gate_e", [P, 2, CT, RC], EX + 84.25)
        gate_mix = at("gate_mix", [P, 2, D], EX + 97)
        xr_pad = at("xr_pad", [P, CT, RC + 3], EX + 105)
        yg = at("yg", [P, CT, NTOK], EX + 111.125)
        ga = at("ga", [P, KD, NTOK], EX + 117.25)
        gated = at("gated", [P, 12, CH], EX + 117.25)
        gb = at("gb", [P, KD, NTOK], EX + 129.25)
        xc = at("xc", [P, CT, RC], EX + 141.25)
        ob_t = at("ob_t", [P, CT, NTOK], EX + 141.25)
        oa_t = at("oa_t", [P, 4, NTOK], EX + 147.5)
        oa_lo = at("oa_lo", [P, 4, NTOK], EX + 147.5, F32R)
        ob_lo = at("ob_lo", [P, CT, NTOK], EX + 141.25, F32R)
        oa_hi = at("oa_hi", [P, 4, NTOK], EX + 105, F32R)
        ob_hi = at("ob_hi", [P, CT, NTOK], EX + 111.125, F32R)
        BROWS = 6
        b_row = at("b_row", [2, BROWS, CH], EX + 153.5)
        m_row = at("m_row", [2, D], EX + 159.5)
        block_w = at("block_w", [P, 2, 2, CT, P], 12)
        k_new = at("k_new", [P, DATT], 20)
        rpb_pad = at("rpb_pad", [7 * H, P], 22)
        col_mask = at("col_mask", [P, GW], 22.5)
        w_hi = [at(f"w_hi{j}", [P, 2048], EX + 16 * j, F32R) for j in range(NK)]
        w_lo = [at(f"w_lo{j}", [P, 2048], EX + 16 * j + 8, F32R) for j in range(NK)]
        xg = [at(f"xg{i}", [P, D], EX + 48 + 4 * i) for i in range(2)]
        act_sb = at("act_sb", [P, FE], EX + 56)
        silu_sb = at("silu_sb", [P, FE], EX + 57)
        raw = [[at(f"raw{i}_{j}", [P, 2048], EX + 60 + 24 * i + 8 * j) for j in range(NK)] for i in range(RAW)]
        xhat2 = at("xhat2", [P, TT, D], EX + 105)
        hs_t = at("hs_t", [P, 2, NTOK], EX + 108)
        hs_g = at("hs_g", [P, 2, NTOK], EX + 111)
        hs_lo = at("hs_lo", [P, 2, NTOK], EX + 108, F32R)
        hs_hi = at("hs_hi", [P, 2, NTOK], EX + 114, F32R)
        h2_row = at("h2_row", [P, TT, D], EX + 150.5)
        x_hi = at("x_hi", [P, KD * CAP], EX + 108, F32R)
        x_lo = at("x_lo", [P, KD * CAP], EX + 112, F32R)
        y_sb = [at(f"y_sb{i}", [P, D], EX + 116 + 4 * i) for i in range(2)]
        a_hi = at("a_hi", [P, 2 * CAP], EX + 124, F32R)
        a_lo = at("a_lo", [P, 2 * CAP], EX + 125, F32R)
        rank_tab = at("rank_tab", [P, NTAB, TT], EX + 126)
        row_tab = at("row_tab", [P, NTAB, TT, 5], EX + 128.5, BF16)
        onehot = [at(f"onehot{i}", [P, TT, CAP], EX + 134.5 + 0.75 * i, BF16) for i in range(2)]
        slot_no = at("slot_no", [P, TT, CAP], EX + 136)
        place[0] = EX + 137.5
        limit[0] = EX + 150.5
        w_router_sb = little("w_router_sb", [P, KD, NE])
        score = little("score", [P, TT, NE])
        biased = little("biased", [P, TT, NE])
        group_top = little("group_top", [P, TT, NG, 8])
        group_score = little("group_score", [P, TT, 16])
        best_groups = little("best_groups", [P, TT, 8])
        group_left = little("group_left", [P, TT, 16])
        group_mask = little("group_mask", [P, TT, NG])
        group_pen = little("group_pen", [P, TT, NG])
        masked = little("masked", [P, TT, NE])
        top8 = little("top8", [P, TT, 8])
        left = little("left", [P, TT, NE])
        chosen = little("chosen", [P, TT, NE])
        chosen_b = little("chosen_b", [P, TT, NE], BF16, 2)
        gates = little("gates", [P, TT, NE])
        gate_sum = little("gate_sum", [P, TT])
        ones_row = little("ones_row", [P, NE])
        before = little("before", [P, P], BF16, 2)
        before_f = little("before_f", [P, P])
        ones_b = little("ones_b", [P, P], BF16, 2)
        lane = little("lane", [P, 1])
        g_rest = little("g_rest", [P, TT, NE])
        rank_f = little("rank_f", [P, TT, NE])
        ffn = [at(f"ffn{t}", [P, D], EX + 60 + 8 * t) for t in range(TT)]
        squared = [at(f"squared{t}", [P, D], EX + 64 + 8 * t) for t in range(TT)]

        rpb_dram = nc.dram_tensor("rpb_dram", (7 * H, GW * P), F32, kind="Internal").ap()
        h2_dram = nc.dram_tensor("h2_dram", (NTOK, D), F32, kind="Internal").ap()
        y_dram = nc.dram_tensor("y_dram", (NTOK, D), F32, kind="Internal").ap()

        chunks = ([("ada", i) for i in range(NADA // 3)] + [("in", i) for i in range(18)]
                  + [("ada", i) for i in range(NADA // 3, NADA)] + [("pa", 0), ("pb", 0), ("pa", 1), ("pb", 1)]
                  + [("out", i) for i in range(4)] + [("sgu", 0), ("sgu", 1), ("sd", 0)])
        number = {c: n for n, c in enumerate(chunks)}
        tiles_through = [2 * (j + 1) if j < 4 else 8 + 3 * (j - 3) if j < 6 else 14 + 2 * (j - 5) for j in range(18)]
        used = [{"ada": ("ada_mm", i + 1), "in": ("w_mm", tiles_through[i] if kind == "in" else 0),
                 "pa": ("merge_mm", 8 * i + 4), "pb": ("merge_mm", 8 * i + 8), "out": ("out_mm", 3 * (i + 1)),
                 "sgu": ("sh_mm", 2 * (i + 1)), "sd": ("shd_mm", 6)}[kind] for kind, i in chunks]
        splits = [n for n, (kind, i) in enumerate(chunks) if kind != "ada"]
        split_no = {n: j for j, n in enumerate(splits)}
        arrival, so_far = [], [0] * SLOTS
        for n, (kind, i) in enumerate(chunks):
            so_far[n % SLOTS] += 32 if kind == "ada" else 16
            arrival.append(so_far[n % SLOTS])

        S = {n: sem(n) for n in """added cond_loaded vec_loaded cache_loaded bias_loaded block_loaded
            late_loaded router_loaded rpb_loaded
            pool_step ident_made pick_made consts mask_made rpb_zero blocks_zero tables_made xg_zero
            sumsq1 rstd1 xhat1 xt1 sumsq2 rstd2 xhat2 xt2 sumsq3 rstd3
            cond_silu chunk_high chunk_ready ada_mm ada_row m_spread mod_copied h_last h_made h_high h_ready scale1_ready vec_mm vec_copied soft_in soft_exp soft_ln
            decay_ready w_mm w_evac ckt_mm ckt_evac kn_mm kn_evac kv_stored rpb_stored
            s_mm s_ready max_ready exp_done p_ready pt_mm pt_evac o_mm o_evac
            pads_zero conv_done gates_mm gates_tanh e2_done e2_capped root_done a_done gelu_done ob_ready
            hl_ready hl_mm hl_copied hl_stored
            oa_high ob_high oa_ready ob_split merged_high merged_ready h2_high h2_split hs_high hs_ready merge_mm merge_gated merge_done bc_mm bc_evac out_mm out_done h2_ready h2r_mm h2r_evac h2_stored
            router_mm score_done chosen_ready rank_mm passes_ready tables_ready
            sh_mm sh_silu sh_act shd_mm shd_evac
            dve_step pool_turn sp_turn num_step onehot_ready idx_mm idx_ready xgt_mm x_hi_ready x_lo_ready silu_done act_ready
            at_mm a_hi_ready a_lo_ready y_ready x2_ready y_done out_stored""".split()}
        chunk_loaded = [sem(f"chunk_loaded{i}") for i in range(SLOTS)]
        gathered = [sem(f"gathered{i}") for i in range(2)]
        ffn_loaded = [sem(f"ffn_loaded{t}") for t in range(TT)]
        x_loaded = [sem(f"x_loaded{t}") for t in range(TT)]
        raw_ready = [[sem(f"raw_ready{i}_{j}") for j in range(NK)] for i in range(RAW)]
        hi_ready = [sem(f"hi_ready{j}") for j in range(NK)]
        lo_ready = [sem(f"lo_ready{j}") for j in range(NK)]
        chunk_used = [sem(f"chunk_used{j}") for j in range(NK)]

        block = ctx.enter_context(nc.Block())

        def link(eng, s):
            count = [0]

            def go(ins):
                count[0] += 1
                ins.then_inc(s, 1)
                eng.wait_ge(s, count[0])
            return go

        def unit(s):
            return (s, 0) if s < H else ((s - H) // 2, 1 + (s - H) % 2)

        def split_high(act, n):
            j = split_no[n]
            act.wait_ge(chunk_loaded[n % SLOTS], arrival[n])
            if j >= HIGHS:
                act.wait_ge(S[used[splits[j - HIGHS]][0]], used[splits[j - HIGHS]][1])
            act.activation(chunk_hi[j % HIGHS][:, :], chunk_raw[n % SLOTS][:, :], ACT.Copy).then_inc(S["chunk_high"], 1)

        def split_low(dve, n):
            j = split_no[n]
            dve.wait_ge(S["chunk_high"], j + 1)
            dve.tensor_tensor(chunk_lo[n % SLOTS][:, :], chunk_raw[n % SLOTS][:, :], chunk_hi[j % HIGHS][:, :].bitcast(F32),
                              ALU.subtract).then_inc(S["chunk_ready"], 1)

        def half_rows(h):
            return slice(DH * (h % 2), DH * (h % 2) + DH)

        def out_rows(t):
            return y_prompt[0] if t == 0 else y_sample[0, (t - 1) * P:t * P, :]

        @block.sync
        def _(sp):
            def load_weights(n):
                kind, i = chunks[n]
                dst, loaded = chunk_raw[n % SLOTS], chunk_loaded[n % SLOTS]
                if n >= SLOTS:
                    sp.wait_ge(S[used[n - SLOTS][0]], used[n - SLOTS][1])
                cols = slice(i * CH, (i + 1) * CH)
                by_k = dst[:, :].rearrange("p (k n) -> p k n", k=KD)
                if kind == "ada":
                    sp.dma_start(by_k, w_ada[0].rearrange("(p k) n -> p k n", k=KD)[:, :, cols]).then_inc(loaded, 16)
                    if i >= BROWS:
                        sp.wait_ge(S["ada_row"], i - BROWS + 1)
                    sp.dma_start(b_row[:, i % BROWS, :], b_ada[0:1, cols].to_broadcast([2, CH])).then_inc(loaded, 16)
                elif kind == "in":
                    sp.dma_start(by_k, w_in[0].rearrange("(p k) n -> p k n", k=KD)[:, :, cols]).then_inc(loaded, 16)
                elif kind in ("pa", "pb"):
                    w = w_pa if kind == "pa" else w_pb
                    sp.dma_start(dst[:, :].rearrange("p (k n) -> p k n", k=4),
                                 w[0].rearrange("(k p) n -> p k n", p=P)[:, :, 512 * i:512 * i + 512]).then_inc(loaded, 16)
                elif kind == "out":
                    sp.dma_start(by_k, w_out[0].rearrange("(k p) n -> p k n", p=P)[:, :, cols]).then_inc(loaded, 16)
                elif kind == "sgu":
                    w = w_up_s if i else w_gate_s
                    sp.dma_start(dst[:, :], w[0].rearrange("(p k) n -> p (k n)", k=KD)).then_inc(loaded, 16)
                else:
                    sp.dma_start(dst[:, :].rearrange("p (k n) -> p k n", k=2),
                                 w_down_s[0].rearrange("(k p) n -> p k n", p=P)).then_inc(loaded, 16)

            for t in range(TT):
                src = x_prompt[0] if t == 0 else x_sample[0, (t - 1) * P:t * P, :]
                sp.dma_start(x_sb[:, t, :], src).then_inc(x_loaded[t], 16)
            for n in range(len(chunks)):
                load_weights(n)
            def load_chunk(i, u, j, e):
                if e is None:
                    e = slice(u, u + 1)
                    if u >= RAW:
                        sp.wait_ge(lo_ready[j], i - RAW + 1)
                else:
                    sp.wait_ge(lo_ready[j], i - (RAW - 1))
                    sp.sem_inc(S["sp_turn"], 1)
                dst, ready = raw[u % RAW][j], raw_ready[u % RAW][j]
                if j < 2:
                    for g, w in enumerate((w_gate_e, w_up_e)):
                        rows = w[0, e].rearrange("a (p h k) n -> (a p) h (k n)", h=2, k=KD // 2)[:, j, :]
                        sp.dma_start(dst[:, g * 1024:(g + 1) * 1024], rows).then_inc(ready, 16)
                else:
                    sp.dma_start(dst[:, :].rearrange("p (k n) -> p k n", k=2),
                                 w_down_e[0, e].rearrange("a (k p) n -> p (a k) n", p=P)).then_inc(ready, 16)

            def load_turn(b, first):
                for u in range(UN):
                    if first and u == 0:
                        sp.wait_ge(S["ob_ready"], 1)
                    if first and u == 1:
                        sp.wait_ge(S["sh_mm"], 4)
                    for j in range(NK):
                        load_chunk(u if first else b[0] * NE + b[1] * UN + u, u, j,
                                   None if first else bass.ds(b[1] * UN + u, 1))

            load_turn(None, True)
            sp.wait_ge(S["passes_ready"], 1)
            passes = sp.value_load(more_i[0:1, 0:1], min_val=0, max_val=MAXPASS - 1) + 1
            with sp.Fori(1, NE // UN) as b:
                load_turn((0, b), False)
            with sp.If(passes >= 2):
                with sp.Fori(1, passes) as pas:
                    with sp.Fori(0, NE // UN) as b:
                        load_turn((pas, b), False)
            sp.end_ifs()
            for j in range(2):
                sp.wait_ge(lo_ready[j], passes * NE - 1)
                sp.sem_inc(S["sp_turn"], 1)
                for g, w in enumerate((w_gate_e, w_up_e)):
                    sp.dma_start(raw[0][j][:, g * 1024:g * 1024 + 4], w[0, 0, 0:P, 0:4]).then_inc(raw_ready[0][j], 16)
            sp.wait_ge(S["added"], passes * (NE * 16) + 16 * TT)
            sp.sem_inc(S["sp_turn"], 1)
            for t in range(TT):
                sp.dma_start(ffn[t][:, :], y_dram[t * P:(t + 1) * P, :]).then_inc(ffn_loaded[t], 16)
            for t in range(TT):
                sp.wait_ge(S["y_done"], t + 1)
                sp.dma_start(out_rows(t), x_sb[:, t, :]).then_inc(S["out_stored"], 16)
            sp.wait_ge(S["out_stored"], 16 * TT)

        @block.gpsimd
        def _(pool):
            go = link(pool, S["pool_step"])
            go(pool.memset(ident[:, :], 0.0))
            pool.affine_select(out=ident[:, :], in_=ident[:, :], compare_op=ALU.not_equal, fill=1.0, base=0,
                               pattern=[[-1, P]], channel_multiplier=1).then_inc(S["ident_made"], 1)
            go(pool.memset(pick[:, :, :], 0.0))
            pool.affine_select(out=pick[:, :, :], in_=pick[:, :, :], compare_op=ALU.not_equal, fill=1.0, base=0,
                               pattern=[[-1, 2], [0, P]], channel_multiplier=1).then_inc(S["pick_made"], 1)
            pool.memset(minus_half[:, :], -0.5).then_inc(S["consts"], 1)
            pool.memset(quarter[:, :], 0.25).then_inc(S["consts"], 1)
            pool.memset(one[:, :], 1.0).then_inc(S["consts"], 1)
            pool.memset(rpb_pad[:, :], 0.0).then_inc(S["rpb_zero"], 1)
            pool.memset(block_w[:, :, :, :, :], 0.0).then_inc(S["blocks_zero"], 1)
            go(pool.memset(col_mask[:, :], 0.0))
            for r in range(2):
                rows = slice(GW * r, GW * r + GW)
                low = col_mask[rows, 0:GW - KW]
                go(pool.affine_select(out=low, in_=low, compare_op=ALU.is_ge, fill=-BIG, base=KW // 2,
                                      pattern=[[1, GW - KW]], channel_multiplier=-1))
                high = col_mask[rows, KW:GW]
                ins = pool.affine_select(out=high, in_=high, compare_op=ALU.is_ge, fill=-BIG, base=KW // 2 - 1 - KW,
                                         pattern=[[-1, GW - KW]], channel_multiplier=1)
                ins.then_inc(S["mask_made"], 1)
            pool.wait_ge(S["mask_made"], 2)
            pool.memset(xr_pad[:, :, 0:2], 0.0).then_inc(S["pads_zero"], 1)
            pool.memset(xr_pad[:, :, NCTX + 2:LAT0 + 2], 0.0).then_inc(S["pads_zero"], 1)
            pool.memset(xr_pad[:, :, RC + 2:RC + 3], 0.0).then_inc(S["pads_zero"], 1)

            def rms(n, summed):
                for t in range(TT):
                    pool.wait_ge(summed, t + 1)
                    at_t = rstd[:, n, t:t + 1]
                    go(pool.tensor_scalar(at_t, sumsq[:, n, t:t + 1], 1.0 / D, EPS, ALU.mult, ALU.add))
                    pool.tensor_tensor(at_t, at_t, minus_half[:, 0:1], ALU.pow).then_inc(S[f"rstd{n + 1}"], 1)

            pool.wait_ge(S["consts"], 3)
            rms(0, S["sumsq1"])
            at_row = 0
            for ap, n in ((conv_w[0], 16), (conv_b, 4), (rg_ba[0], 8), (rg_bx[0], 8), (rg_lam[0], 8),
                          (state_f[0], 4), (state_b[0], 4)):
                pool.dma_start(vec_rows[at_row:at_row + n, :], ap.rearrange("a (t p) -> (a t) p", p=P)).then_inc(S["vec_loaded"], 16)
                at_row += n
            pool.wait_ge(S["rpb_zero"], 1)
            for d in range(7):
                pool.dma_start(rpb_pad[d * H:(d + 1) * H, P // 2 - KW:P // 2 + KW - 1],
                              rpb[0, :, d + 4, :]).then_inc(S["rpb_loaded"], 16)
            pool.wait_ge(S["merge_done"], KD)
            pool.wait_ge(S["m_spread"], 6)
            pool.wait_ge(S["merge_mm"], 2 * KD)
            pool.iota(slot_no[:, :, :], [[0, TT], [1, CAP]], base=0, channel_multiplier=0,
                      allow_small_or_imprecise_dtypes=True).then_inc(S["tables_made"], 1)
            pool.iota(lane[:, :], [[0, 1]], base=0, channel_multiplier=1,
                      allow_small_or_imprecise_dtypes=True).then_inc(S["tables_made"], 1)
            pool.memset(ones_row[:, :], 1.0).then_inc(S["tables_made"], 1)
            pool.memset(ones_b[:, :], 1.0).then_inc(S["tables_made"], 1)
            go(pool.memset(before_f[:, :], 1.0))
            go(pool.affine_select(out=before_f[:, :], in_=before_f[:, :], compare_op=ALU.is_gt, fill=0.0, base=0,
                                  pattern=[[1, P]], channel_multiplier=-1))
            pool.tensor_copy(before[:, :], before_f[:, :]).then_inc(S["tables_made"], 1)
            pool.memset(group_score[:, :, 8:16], LOWEST).then_inc(S["tables_made"], 1)
            rms(1, S["sumsq2"])
            pool.wait_ge(S["router_mm"], 1)
            pool.wait_ge(S["h2r_mm"], 6)
            pool.wait_ge(S["sh_mm"], 4)
            for i in range(2):
                pool.memset(xg[i][:, :], 0.0).then_inc(S["xg_zero"], 1)

            pool.wait_ge(S["passes_ready"], 1)
            passes = pool.value_load(more_i[0:1, 0:1], min_val=0, max_val=MAXPASS - 1) + 1
            pool.wait_ge(S["h2_stored"], 16 * TT)
            pool.wait_ge(S["xg_zero"], 2)

            def gather(i, u):
                pool.wait_ge(S["idx_ready"], i + 1)
                pool.sem_inc(S["pool_turn"], 1)
                pool.indirect_dma_start(xg[u % 2][:, :], None, h2_dram[:, :],
                                        bass.IndirectOffsetOnAxis(ap=slot_tok[:, u % UN:u % UN + 1], axis=0),
                                        bounds_check=NTOK - 1, oob_is_err=False).then_inc(gathered[u % 2], 16)

            def scatter(i, u, first=False):
                pool.wait_ge(S["y_ready"], i + 1)
                if not first:
                    pool.sem_inc(S["pool_turn"], 1)
                pool.wait_ge(S["added"], 16 * i + 16 * TT)
                pool.sem_inc(S["pool_turn"], 1)
                pool.indirect_dma_start(y_dram[:, :],
                                        bass.IndirectOffsetOnAxis(ap=slot_tok[:, u % UN:u % UN + 1], axis=0),
                                        y_sb[u % 2][:, :], None, bounds_check=NTOK - 1,
                                        oob_is_err=False, compute_op=ALU.add).then_inc(S["added"], 16)

            def block_turn(b, first):
                for u in range(UN):
                    i = u if first else b * UN + u
                    pool.wait_ge(S["xgt_mm"], i + 1)
                    gather(i + 2, u + 2)
                    if not (first and u == 0):
                        scatter(i - 1, u - 1)

            gather(0, 0)
            gather(1, 1)
            pool.wait_ge(S["shd_evac"], 6)
            for t in range(TT):
                pool.dma_start(y_dram[t * P:(t + 1) * P, :], shared_sb[:, t, :]).then_inc(S["added"], 16)
            block_turn(0, True)
            with pool.Fori(1, passes * (NE // UN)) as b:
                block_turn(b, False)
            scatter(passes * NE - 1, UN - 1)
            for s in gathered:
                pool.wait_ge(s, passes * (NE // 2 * 16) + 16)
                pool.sem_inc(S["pool_turn"], 1)
            rms(2, S["sumsq3"])

        @block.scalar
        def _(act):
            act.dma_start(cond_raw[:, 0, :], c_ctx.rearrange("(p k) -> p k", k=KD)).then_inc(S["cond_loaded"], 16)
            act.dma_start(cond_raw[:, 1, :], c[0].rearrange("(p k) -> p k", k=KD)).then_inc(S["cond_loaded"], 16)
            act.dma_start(g1_sb[:, :], norm1_g[0].rearrange("(p k) -> p k", k=KD)).then_inc(S["cond_loaded"], 16)
            act.dma_start(g2_sb[:, :], norm2_g[0].rearrange("(p k) -> p k", k=KD)).then_inc(S["cond_loaded"], 16)

            def squares(n, junk, signal):
                for t in range(TT):
                    if n == 0:
                        act.wait_ge(x_loaded[t], 16)
                    else:
                        act.wait_ge(S["out_done"], 10 + t)
                    act.activation(junk[:, t, :], x_sb[:, t, :], ACT.Square,
                                   accum_out=sumsq[:, n, t:t + 1]).then_inc(signal, 1)

            squares(0, xhat, S["sumsq1"])
            act.wait_ge(S["cond_loaded"], 64)
            act.activation(cond_t[:, :, :].rearrange("p k c -> p c k"), cond_raw[:, :, :], ACT.Silu).then_inc(S["cond_silu"], 1)
            def mod_copy(i):
                act.wait_ge(S["m_spread"], i + 1)
                act.activation(mod_t[:, i, :, :].rearrange("p k c -> p (k c)"), bank[7][:, 0:2 * KD],
                               ACT.Copy).then_inc(S["mod_copied"], 1)

            mod_copy(0)
            split_high(act, 8)
            split_high(act, 9)
            mod_copy(1)
            act.wait_ge(S["mod_copied"], 2)
            act.wait_ge(S["scale1_ready"], 1)
            act.wait_ge(S["xt1"], 6)
            for k in range(KD):
                ins = act.activation(h_t[:, k, 2 * P:3 * P], bank[4 + k // 4][:, (k % 4) * P:(k % 4 + 1) * P], ACT.Identity,
                                     scale=scale1[:, k, 1:2], bias=mod_t[:, 0, k, 1:2])
            ins.then_inc(S["h_last"], 1)
            act.wait_ge(S["h_last"], 1)
            for n, t in enumerate((2, 0, 1)):
                if n:
                    act.wait_ge(S["h_made"], n)
                act.activation(h_hi[:, :, t * P:(t + 1) * P], h_t[:, :, t * P:(t + 1) * P], ACT.Copy).then_inc(S["h_high"], 1)
            act.wait_ge(S["rpb_loaded"], 7 * 16)
            act.dma_start(rpb_dram.rearrange("r (w c) -> r w c", c=P),
                          rpb_pad[:, :].unsqueeze(1).to_broadcast([7 * H, GW, P])).then_inc(S["rpb_stored"], 16)
            act.dma_start(ck_raw[:, :], cache_k[0, 0].rearrange("s h d -> s (h d)")).then_inc(S["cache_loaded"], 16)
            act.dma_start(cv_sb[:, :], cache_v[0, 0].rearrange("s h d -> s (h d)")).then_inc(S["cache_loaded"], 16)
            act.wait_ge(S["blocks_zero"], 1)
            for d in range(2):
                for kind, w in enumerate((rg_wa, rg_wx)):
                    for par in range(2):
                        rows = slice(DH * par, DH * par + DH)
                        act.dma_start(block_w[rows, d, kind, :, DH * par:DH * par + DH],
                                      w[0, d].rearrange("(t a) d e -> a d t e", a=2)[par]).then_inc(S["block_loaded"], 16)
            act.dma_start(router_b[:, :], b_router[0:1, :].to_broadcast([P, NE])).then_inc(S["late_loaded"], 16)
            act.wait_ge(S["soft_in"], 1)
            act.activation(abs_lam[:, :], abs_lam[:, :], ACT.Exp, scale=-1.0).then_inc(S["soft_exp"], 1)
            act.wait_ge(S["soft_exp"], 1)
            act.wait_ge(S["consts"], 3)
            act.activation(softplus[:, :], abs_lam[:, :], ACT.Ln, bias=one[:, 0:1]).then_inc(S["soft_ln"], 1)
            act.wait_ge(S["rpb_stored"], 16)
            act.wait_ge(S["xt1"], 6)
            for r in range(2):
                src = bass.AP(rpb_dram.tensor, (1 - r) * H * GW * P + P // 2 - 1, [[P - 1, GW], [GW * P, 6 * H], [1, GW]])
                act.dma_start(bias_sb[GW * r:GW * r + GW, :, :, :].rearrange("p s h c -> p (s h) c"), src).then_inc(S["bias_loaded"], 16)

            def evacuate(n):
                act.wait_ge(S["w_mm"], n + 1)
                src = bank[2 + n % 2]
                if n < 4:
                    ins = act.activation(q_t[:, n, :], src[:, 0:NTOK], ACT.Copy, scale=DH ** -0.5)
                elif n < 8:
                    ins = act.activation(k_t[:, n - 4, :], src[:, 0:NTOK], ACT.Copy)
                elif n < 14:
                    half, t = divmod(n - 8, 3)
                    ins = act.activation(v_sb[:, t, CH * half:CH * half + CH], src[:, 0:CH], ACT.Copy)
                elif n < 18:
                    if n == 14:
                        act.wait_ge(S["pads_zero"], 3)
                    act.activation(xr_pad[:, n - 14, 2:2 + NCTX], src[:, 0:NCTX], ACT.Copy)
                    ins = act.activation(xr_pad[:, n - 14, LAT0 + 2:LAT0 + 2 + NLAT], src[:, NCTX:NTOK], ACT.Copy)
                elif n < 22:
                    ins = act.activation(yg[:, n - 18, :], src[:, 0:NTOK], ACT.Copy)
                elif n < 30:
                    ins = act.activation(ga[:, n - 22, :], src[:, 0:NTOK], ACT.Tanh, scale=0.5)
                else:
                    ins = act.activation(gb[:, n - 30, :], src[:, 0:NTOK], ACT.Tanh, scale=0.5)
                ins.then_inc(S["w_evac"], 1)

            for n in range(8):
                evacuate(n)
                if n % 2:
                    split_high(act, 10 + n // 2)
            act.wait_ge(S["ckt_mm"], 1)
            act.activation(ck_t[:, :, :].rearrange("p m s -> p (m s)"), bank[4][:, :], ACT.Copy).then_inc(S["ckt_evac"], 1)
            for n in range(8, 14):
                evacuate(n)
                if n in (10, 13):
                    split_high(act, 14 + (n == 13))
            act.wait_ge(S["kn_mm"], 1)
            act.activation(k_new[:, :], bank[6][:, :], ACT.Copy).then_inc(S["kn_evac"], 1)
            act.wait_ge(S["kn_evac"], 1)
            act.wait_ge(S["w_evac"], 14)
            act.dma_start(new_k[0, 0].rearrange("s h d -> s (h d)"), k_new[:, :]).then_inc(S["kv_stored"], 16)
            act.dma_start(new_v[0, 0].rearrange("s h d -> s (h d)"), v_sb[:, 0, :]).then_inc(S["kv_stored"], 16)
            for s in range(NSTEP + 2):
                if s < NSTEP:
                    h, t = unit(s)
                    act.wait_ge(S["max_ready"], s + 1)
                    if s >= 2:
                        act.wait_ge(S["pt_mm"], s - 1)
                    if t == 0:
                        ins = act.activation(e_sb[:, s % 2, 0:NCTX], bank[s % 2][:, 0:NCTX], ACT.Exp,
                                             bias=neg_max[:, s % 2:s % 2 + 1], accum_out=row_sum[:, s % 2:s % 2 + 1])
                    else:
                        ins = act.activation(e_sb[:, s % 2, :], s_sb[:, s % 2, :], ACT.Exp,
                                             bias=neg_max[:, s % 2:s % 2 + 1], accum_out=row_sum[:, s % 2:s % 2 + 1])
                    ins.then_inc(S["exp_done"], 1)
                    evacuate(14 + s)
                if s >= 2:
                    h, t = unit(s - 2)
                    rows = half_rows(h)
                    act.wait_ge(S["o_mm"], s - 1)
                    act.activation(oa_t[rows, h // 2, t * P:(t + 1) * P], bank[6 + s % 2][rows, 0:P],
                                   ACT.Copy).then_inc(S["o_evac"], 1)
                if s < 20 and s % 2:
                    split_high(act, 16 + s // 2)
            act.wait_ge(S["kv_stored"], 32)
            act.wait_ge(S["decay_ready"], 1)
            n = 0
            for kind, dst in enumerate((gate_r, gate_i)):
                for d in range(2):
                    for t in range(CT):
                        act.wait_ge(S["gates_mm"], n + 1)
                        j = kind * 8 + d * CT + t
                        act.activation(dst[:, d, t, :], bank[n % 4][:, 0:RC], ACT.Tanh, scale=0.5,
                                       bias=half_b[:, j:j + 1]).then_inc(S["gates_tanh"], 1)
                        n += 1
            act.wait_ge(S["o_evac"], NSTEP)
            act.activation(oa_hi[:, :, :], oa_t[:, :, :], ACT.Copy).then_inc(S["oa_high"], 1)
            act.wait_ge(S["gates_tanh"], 16)
            for d in range(2):
                for t in range(CT):
                    j = d * CT + t
                    act.activation(gate_e[:, d, t, :], gate_r[:, d, t, :], ACT.Exp, scale=decay2[:, j:j + 1],
                                   bias=decay2[:, j:j + 1]).then_inc(S["e2_done"], 1)
            act.wait_ge(S["e2_done"], 8)
            for d in range(2):
                for t in range(CT):
                    j = d * CT + t
                    act.activation(gate_r[:, d, t, :], gate_r[:, d, t, :], ACT.Exp, scale=decay[:, j:j + 1],
                                   bias=decay[:, j:j + 1]).then_inc(S["a_done"], 1)
            act.wait_ge(S["e2_capped"], 1)
            act.activation(gate_e[:, :, :, :], gate_e[:, :, :, :], ACT.Sqrt, scale=-0.25,
                           bias=quarter[:, 0:1]).then_inc(S["root_done"], 1)
            act.activation(yg[:, :, :], yg[:, :, :], ACT.Gelu_apprx_tanh).then_inc(S["gelu_done"], 1)

            def spread_copy(i, dst, scale):
                for n in range(4):
                    at_n = n + (4 if i == 5 else 0)
                    act.wait_ge(S["bc_mm"], at_n + 1)
                    act.activation(dst[:, n // 2, 512 * (n % 2):512 * (n % 2) + 512], bank[4 + n % 2][:, :],
                                   ACT.Copy, scale=scale).then_inc(S["bc_evac"], 1)

            spread_copy(2, gate_mix, 0.5)
            mod_copy(3)
            mod_copy(4)
            split_high(act, number[("pa", 0)])
            split_high(act, number[("pb", 0)])
            spread_copy(5, gate_ffn, 1.0)
            act.wait_ge(S["ob_ready"], 1)
            act.activation(ob_hi[:, :, :], ob_t[:, :, :], ACT.Copy).then_inc(S["ob_high"], 1)
            split_high(act, number[("pa", 1)])
            for m in range(KD):
                if m == 4:
                    split_high(act, number[("pb", 1)])
                    split_high(act, number[("out", 0)])
                act.wait_ge(S["merge_done"], m + 1)
                act.activation(merged_hi[:, m, :], merged[:, m, :], ACT.Copy).then_inc(S["merged_high"], 1)
            split_high(act, number[("out", 1)])
            act.wait_ge(S["hl_mm"], 1)
            act.activation(h_last_rows[:, :], bank[6][0:8, 0:P], ACT.Copy).then_inc(S["hl_copied"], 1)
            act.wait_ge(S["hl_copied"], 1)
            act.dma_start(new_hf[0].rearrange("a (t p) -> (a t) p", p=P), h_last_rows[0:4, :]).then_inc(S["hl_stored"], 16)
            act.dma_start(new_hb[0].rearrange("a (t p) -> (a t) p", p=P), h_last_rows[4:8, :]).then_inc(S["hl_stored"], 16)
            act.wait_ge(S["merge_done"], KD)
            act.wait_ge(S["m_spread"], 6)
            act.dma_start(final_g_sb[:, :], final_g.rearrange("(a n) -> a n", a=1).to_broadcast([P, D])).then_inc(S["late_loaded"], 16)
            act.dma_start(w_router_sb[:, :, :], w_router[0].rearrange("(p k) n -> p k n", k=KD)).then_inc(S["router_loaded"], 16)
            for n in range(number[("out", 2)], number[("out", 3)] + 1):
                split_high(act, n)
            squares(1, xhat2, S["sumsq2"])
            for n in range(number[("sgu", 0)], number[("sgu", 1)] + 1):
                split_high(act, n)
            for t in range(TT):
                act.wait_ge(S["h2_ready"], 2 * t + 2)
                if t == 0:
                    act.wait_ge(S["merged_ready"], KD)
                    act.wait_ge(S["out_mm"], 12)
                act.activation(h2_hi[:, :, t * P:(t + 1) * P], h2_t[:, :, t * P:(t + 1) * P], ACT.Copy).then_inc(S["h2_high"], 1)
            act.wait_ge(S["router_mm"], 1)
            act.activation(score[:, :, :].rearrange("p t e -> p (t e)"), bank[0][:, 0:TT * NE],
                           ACT.Sigmoid).then_inc(S["score_done"], 1)
            for t in range(TT):
                for half in range(2):
                    n = 2 * t + half
                    act.wait_ge(S["h2r_mm"], n + 1)
                    act.activation(h2_row[:, t, 512 * half:512 * half + 512], bank[6 + n % 2][:, :],
                                   ACT.Copy).then_inc(S["h2r_evac"], 1)
                act.wait_ge(S["h2r_evac"], 2 * t + 2)
                act.dma_start(h2_dram[t * P:(t + 1) * P, :], h2_row[:, t, :]).then_inc(S["h2_stored"], 16)
            for m in range(2):
                act.wait_ge(S["sh_mm"], m + 1)
                act.activation(hs_g[:, m, :], bank[2 + m][:, 0:NTOK], ACT.Silu).then_inc(S["sh_silu"], 1)
            split_high(act, number[("sd", 0)])
            act.wait_ge(S["sh_act"], 2)
            act.activation(hs_hi[:, :, :], hs_t[:, :, :], ACT.Copy).then_inc(S["hs_high"], 1)
            act.wait_ge(S["kv_stored"], 32)
            for n in range(6):
                act.wait_ge(S["shd_mm"], n + 1)
                act.activation(shared_sb[:, n // 2, 512 * (n % 2):512 * (n % 2) + 512], bank[2 * (n % 2)][:, :],
                               ACT.Copy).then_inc(S["shd_evac"], 1)
            act.wait_ge(S["passes_ready"], 1)
            passes = act.value_load(more_i[0:1, 0:1], min_val=0, max_val=MAXPASS - 1) + 1
            act.wait_ge(S["h2_stored"], 16 * TT)

            def hi(i, u, j, first):
                if first:
                    act.wait_ge(raw_ready[u % RAW][j], (16 if j == 2 else 32) * (u // RAW + 1))
                    if u:
                        act.wait_ge(chunk_used[j], u)
                else:
                    act.wait_ge(raw_ready[u % RAW][j], (i - u % RAW) * ((16 if j == 2 else 32) // RAW) + (16 if j == 2 else 32))
                    act.wait_ge(chunk_used[j], i)
                act.activation(w_hi[j][:, :], raw[u % RAW][j][:, :], ACT.Copy).then_inc(hi_ready[j], 1)

            def x_high(i):
                act.wait_ge(S["xgt_mm"], i + 1)
                for half in range(2):
                    act.activation(x_hi[:, half * 512:half * 512 + 512], bank[half][:, :], ACT.Copy).then_inc(S["x_hi_ready"], 1)

            def rows_out(i, u, first):
                act.wait_ge(chunk_used[2], i + 1)
                act.wait_ge(S["idx_ready"], i + 1)
                if not (first and u == 0):
                    act.wait_ge(S["added"], 16 * (i - 1) + 16 * TT)
                for half in range(2):
                    ins = act.activation(y_sb[u % 2][:, half * 512:half * 512 + 512], bank[5 + half][:, :], ACT.Copy,
                                         scale=slot_gate[:, u:u + 1])
                ins.then_inc(S["y_ready"], 1)

            def block_turn(b, first):
                for u in range(UN):
                    i = u if first else b * UN + u
                    head = first and u == 0
                    if not head:
                        hi(i - 1, (u - 1) % UN, 2, first and u > 0)
                    hi(i + 1, u + 1, 0, first)
                    act.wait_ge(chunk_used[1], i + 1)
                    act.activation(silu_sb[:, :], bank[2 + u % 2][:, 0:FE], ACT.Silu).then_inc(S["silu_done"], 1)
                    x_high(i + 1)
                    hi(i + 1, u + 1, 1, first)
                    if not head:
                        rows_out(i - 1, (u - 1) % UN, first)
                    act.wait_ge(S["at_mm"], i + 1)
                    act.activation(a_hi[:, :], bank[4][:, 0:FE], ACT.Copy).then_inc(S["a_hi_ready"], 1)

            hi(0, 0, 0, True)
            hi(0, 0, 1, True)
            x_high(0)
            block_turn(0, True)
            with act.Fori(1, passes * (NE // UN)) as b:
                block_turn(b, False)
            hi(passes * NE - 1, UN - 1, 2, False)
            rows_out(passes * NE - 1, UN - 1, False)
            for t in range(TT):
                act.wait_ge(S["x2_ready"], t + 1)
                act.activation(squared[t][:, :], x_sb[:, t, :], ACT.Square,
                               accum_out=sumsq[:, 2, t:t + 1]).then_inc(S["sumsq3"], 1)
            act.wait_ge(S["hl_stored"], 32)

        @block.tensor
        def _(pe):
            def arrived(kind, i):
                n = number[(kind, i)]
                pe.wait_ge(S["chunk_ready"], split_no[n] + 1)
                return chunk_hi[split_no[n] % HIGHS], chunk_lo[n % SLOTS]

            def three_products(out, left, right, start, stop):
                pe.matmul(out, left[1], right[0], start=start, stop=False)
                pe.matmul(out, left[0], right[1], start=False, stop=False)
                return pe.matmul(out, left[0], right[0], start=False, stop=stop)

            pe.wait_ge(S["ident_made"], 1)
            for t in range(TT):
                pe.wait_ge(S["xhat1"], t + 1)
                for half in range(2):
                    for j in range(4):
                        k = 4 * half + j
                        mm = pe.transpose(bank[2 * t + half][:, j * P:(j + 1) * P], xhat[:, t, k:D:KD], ident[:, :])
                    mm.then_inc(S["xt1"], 1)

            def modulation(i):
                for c in range(4 * i, 4 * i + 4):
                    n = number[("ada", c)]
                    w = chunk_raw[n % SLOTS]
                    pe.wait_ge(chunk_loaded[n % SLOTS], arrival[n])
                    if c == 0:
                        pe.wait_ge(S["cond_silu"], 1)
                    if c >= 2:
                        pe.wait_ge(S["ada_row"], c - 1)
                    if c % 2 and c in (5, 13, 17, 21):
                        pe.wait_ge(S["mod_copied"], {5: 1, 13: 2, 17: 3, 21: 4}[c])
                    if c == 9:
                        pe.wait_ge(S["vec_copied"], 1)
                    for k in range(KD):
                        mm = pe.matmul(bank[6 + c % 2][0:2, 0:CH], cond_t[:, k, :], w[:, k * CH:(k + 1) * CH],
                                       start=(k == 0), stop=(k == KD - 1))
                    mm.then_inc(S["ada_mm"], 1)
                pe.wait_ge(S["ada_row"], 4 * i + 4)
                if i in (2, 5):
                    for n in range(4):
                        at_n = n + (4 if i == 5 else 0)
                        if at_n >= 2:
                            pe.wait_ge(S["bc_evac"], at_n - 1)
                        if n == 0:
                            pe.wait_ge(S["pick_made"], 1)
                        mm = pe.matmul(bank[4 + n % 2][:, :], pick[:, n // 2, :], m_row[:, 512 * (n % 2):512 * (n % 2) + 512],
                                       start=True, stop=True)
                        mm.then_inc(S["bc_mm"], 1)
                    pe.wait_ge(S["bc_mm"], at_n + 1)
                    pe.sem_inc(S["m_spread"], 1)
                else:
                    if i == 3:
                        pe.wait_ge(S["vec_copied"], 1)
                    if i:
                        pe.wait_ge(S["mod_copied"], {1: 1, 3: 2, 4: 3}[i])
                    for k in range(KD):
                        mm = pe.transpose(bank[7][:, 2 * k:2 * k + 2], m_row[:, k:D:KD], ident[0:2, 0:2])
                    mm.then_inc(S["m_spread"], 1)

            modulation(0)
            modulation(1)
            pe.wait_ge(S["mod_copied"], 2)
            pe.wait_ge(S["vec_loaded"], 7 * 16)
            pe.transpose(bank[7][:, 0:NVEC], vec_rows[:, :], ident[0:NVEC, 0:NVEC]).then_inc(S["vec_mm"], 1)
            pe.wait_ge(S["h_ready"], 3)

            def project(n):
                if n >= 2:
                    pe.wait_ge(S["w_evac"], n - 1)
                out = bank[2 + n % 2]
                if 8 <= n < 14:
                    half, t = divmod(n - 8, 3)
                    w = arrived("in", 4 + half)
                    for k in range(KD):
                        mm = three_products(out[:, 0:CH], [a[:, k, t * P:(t + 1) * P] for a in (h_hi, h_lo)],
                                            [a[:, k * CH:(k + 1) * CH] for a in w], k == 0, k == KD - 1)
                else:
                    c, m = divmod(n if n < 8 else n - 2, 2)
                    w = arrived("in", c)
                    for k in range(KD):
                        mm = three_products(out[:, 0:NTOK], [a[:, k * CH + m * P:k * CH + (m + 1) * P] for a in w],
                                            [a[:, k, :] for a in (h_hi, h_lo)], k == 0, k == KD - 1)
                mm.then_inc(S["w_mm"], 1)

            for n in range(8):
                project(n)
            pe.wait_ge(S["cache_loaded"], 32)
            for m in range(4):
                mm = pe.transpose(bank[4][:, m * P:(m + 1) * P], ck_raw[:, m * P:(m + 1) * P], ident[:, :])
            mm.then_inc(S["ckt_mm"], 1)
            for n in range(8, 14):
                project(n)
            for m in range(4):
                mm = pe.transpose(bank[6][:, m * P:(m + 1) * P], k_t[:, m, 0:NCTX], ident[:, :])
            mm.then_inc(S["kn_mm"], 1)

            def scores(s):
                h, t = unit(s)
                rows = half_rows(h)
                if s >= 2:
                    pe.wait_ge(S["exp_done"], s - 1)
                q = q_t[rows, h // 2, t * P:(t + 1) * P]
                if t == 0:
                    mm = pe.matmul(bank[s % 2][:, 0:NCTX], q, k_t[rows, h // 2, 0:NCTX], start=True, stop=True)
                else:
                    pe.matmul(bank[s % 2][:, 0:NLAT], q, k_t[rows, h // 2, NCTX:NTOK], start=True, stop=True)
                    mm = pe.matmul(bank[s % 2][:, NLAT:384], q, ck_t[rows, h // 2, :], start=True, stop=True)
                mm.then_inc(S["s_mm"], 1)

            def turn(s):
                pe.wait_ge(S["p_ready"], s + 1)
                if s >= 2:
                    pe.wait_ge(S["pt_evac"], s - 1)
                for j in range(1 if s < H else 3):
                    mm = pe.transpose(bank[4 + s % 2][:, j * P:(j + 1) * P], e_sb[:, s % 2, j * P:(j + 1) * P], ident[:, :])
                mm.then_inc(S["pt_mm"], 1)

            def values(s):
                h, t = unit(s)
                rows = half_rows(h)
                pe.wait_ge(S["pt_evac"], s + 1)
                if s >= 2:
                    pe.wait_ge(S["o_evac"], s - 1)
                heads = slice(h * DH, (h + 1) * DH)
                vs = [v_sb[:, 0, heads]] if t == 0 else [v_sb[:, 1, heads], v_sb[:, 2, heads], cv_sb[:, heads]]
                for j, v in enumerate(vs):
                    mm = pe.matmul(bank[6 + s % 2][rows, 0:P], v, pt_sb[:, s % 2, j * P:(j + 1) * P],
                                   start=(j == 0), stop=(j == len(vs) - 1))
                mm.then_inc(S["o_mm"], 1)

            pe.wait_ge(S["ckt_evac"], 1)
            pe.wait_ge(S["kn_evac"], 1)
            for s in range(NSTEP + 2):
                if s < NSTEP:
                    scores(s)
                    project(14 + s)
                if 1 <= s <= NSTEP:
                    turn(s - 1)
                if s >= 2:
                    values(s - 2)
            pe.wait_ge(S["block_loaded"], 8 * 16)
            pe.wait_ge(S["conv_done"], 1)
            pe.wait_ge(S["w_evac"], 38)
            n = 0
            for kind in range(2):
                for d in range(2):
                    for t in range(CT):
                        if n >= 4:
                            pe.wait_ge(S["gates_tanh"], n - 3)
                        pe.matmul(bank[n % 4][:, 0:RC], block_w[:, d, kind, t, :], xc[:, t, :],
                                  start=True, stop=True).then_inc(S["gates_mm"], 1)
                        n += 1
            pe.wait_ge(S["o_evac"], NSTEP)
            for i in range(2, 6):
                modulation(i)
            pe.wait_ge(S["gates_tanh"], 16)
            pe.wait_ge(S["oa_ready"], 1)
            for i in range(2):
                for b, (kind, o) in enumerate((("pa", (oa_hi, oa_lo)), ("pb", (ob_hi, ob_lo)))):
                    w = arrived(kind, i)
                    if i == 0 and b == 1:
                        pe.wait_ge(S["ob_split"], 1)
                        pe.wait_ge(S["bc_evac"], 8)
                        pe.wait_ge(S["mod_copied"], 4)
                    for m in range(4):
                        if i:
                            pe.wait_ge(S["merge_gated"], 4 * b + m + 1)
                        for k in range(4):
                            at_m = k * 512 + m * P
                            mm = three_products(bank[4 * b + m][:, 0:NTOK], [a[:, at_m:at_m + P] for a in w],
                                                [a[:, k, :] for a in o], k == 0, k == 3)
                        mm.then_inc(S["merge_mm"], 1)
            pe.wait_ge(S["hl_ready"], 1)
            pe.wait_ge(S["merge_gated"], 2 * KD)
            pe.transpose(bank[6][0:8, 0:P], h_last[:, :], ident[:, :]).then_inc(S["hl_mm"], 1)
            pe.wait_ge(S["merged_ready"], KD)
            for c in range(4):
                w = arrived("out", c)
                for t in range(TT):
                    n = 3 * c + t
                    if n >= 4:
                        pe.wait_ge(S["out_done"], n - 3)
                    for k in range(KD):
                        mm = three_products(bank[n % 4][:, 0:CH], [a[:, k, t * P:(t + 1) * P] for a in (merged_hi, merged_lo)],
                                            [a[:, k * CH:(k + 1) * CH] for a in w], k == 0, k == KD - 1)
                    mm.then_inc(S["out_mm"], 1)
            for t in range(TT):
                pe.wait_ge(S["xhat2"], t + 1)
                for half in range(2):
                    n = 2 * t + half
                    if n >= 4:
                        pe.wait_ge(S["h2_ready"], n - 3)
                    if n == 2:
                        pe.wait_ge(S["hl_copied"], 1)
                    for j in range(4):
                        k = 4 * half + j
                        mm = pe.transpose(bank[4 + n % 4][:, j * P:(j + 1) * P], xhat2[:, t, k:D:KD], ident[:, :])
                    mm.then_inc(S["xt2"], 1)
            pe.wait_ge(S["router_loaded"], 16)
            for t in range(TT):
                pe.wait_ge(S["h2_ready"], 2 * t + 2)
                for k in range(KD):
                    mm = pe.matmul(bank[0][:, t * NE:(t + 1) * NE], h2_t[:, k, t * P:(t + 1) * P], w_router_sb[:, k, :],
                                   start=(k == 0), stop=(k == KD - 1))
            mm.then_inc(S["router_mm"], 1)
            pe.wait_ge(S["hl_copied"], 1)
            for n in range(6):
                t, half = divmod(n, 2)
                if n >= 2:
                    pe.wait_ge(S["h2r_evac"], n - 1)
                for j in range(4):
                    mm = pe.transpose(bank[6 + n % 2][:, j * P:(j + 1) * P], h2_t[:, 4 * half + j, t * P:(t + 1) * P], ident[:, :])
                mm.then_inc(S["h2r_mm"], 1)
            pe.wait_ge(S["h2_split"], TT)
            for m in range(4):
                kind, half = divmod(m, 2)
                w = arrived("sgu", kind)
                for k in range(KD):
                    at_m = k * FE + half * P
                    mm = three_products(bank[2 + m][:, 0:NTOK], [a[:, at_m:at_m + P] for a in w],
                                        [a[:, k, :] for a in (h2_hi, h2_lo)], k == 0, k == KD - 1)
                mm.then_inc(S["sh_mm"], 1)
                if m == 1:
                    pe.wait_ge(S["chosen_ready"], 1)
                    pe.wait_ge(S["tables_made"], 6)
                    for t in range(TT + 1):
                        lhs = [ones_b] * min(t, TT) + [before] * (t < TT)
                        for j, table in enumerate(lhs):
                            mm = pe.matmul(bank[1][:, t * NE:(t + 1) * NE], table[:, :], chosen_b[:, j, :],
                                           start=(j == 0), stop=(j == len(lhs) - 1))
                    mm.then_inc(S["rank_mm"], 1)
            def block_rows(i, u):
                pe.wait_ge(S["onehot_ready"], i + 1)
                for t in range(TT):
                    mm = pe.matmul(bank[7][:, 0:5], onehot[u % 2][:, t, :], row_tab[:, bass.ds(i, 1), t, :]
                                   .rearrange("p a c -> p (a c)"), start=(t == 0), stop=(t == TT - 1))
                mm.then_inc(S["idx_mm"], 1)

            pe.wait_ge(S["tables_ready"], 1)
            pe.wait_ge(S["h2r_evac"], 6)
            block_rows(0, 0)
            pe.wait_ge(S["idx_ready"], 1)
            block_rows(1, 1)
            w = arrived("sd", 0)
            pe.wait_ge(S["hs_ready"], 1)
            for n in range(6):
                t, half = divmod(n, 2)
                if n == 0:
                    pe.wait_ge(S["score_done"], 1)
                    pe.wait_ge(S["sh_silu"], 1)
                if n >= 2:
                    pe.wait_ge(S["shd_evac"], n - 1)
                for k in range(2):
                    at_k = k * D + 512 * half
                    mm = three_products(bank[2 * (n % 2)][:, :], [a[:, k, t * P:(t + 1) * P] for a in (hs_hi, hs_lo)],
                                        [a[:, at_k:at_k + 512] for a in w], k == 0, k == 1)
                mm.then_inc(S["shd_mm"], 1)
            pe.wait_ge(S["passes_ready"], 1)
            passes = pe.value_load(more_i[0:1, 0:1], min_val=0, max_val=MAXPASS - 1) + 1
            pe.wait_ge(S["shd_evac"], 6)
            pe.wait_ge(S["h2r_evac"], 6)
            def turn_tokens(i, u, first):
                pe.wait_ge(gathered[u % 2], 16 * (u // 2 + 1) if first else (i - u % 2) * 8 + 16)
                for k in range(KD):
                    mm = pe.transpose(bank[k // 4][:, (k % 4) * P:(k % 4 + 1) * P], xg[u % 2][:, k * P:(k + 1) * P], ident[:, :])
                mm.then_inc(S["xgt_mm"], 1)

            def gate_up(i, u, j):
                pe.wait_ge(lo_ready[j], i + 1)
                if j == 0:
                    pe.wait_ge(S["x_hi_ready"], 2 * i + 2)
                    pe.wait_ge(S["x_lo_ready"], 2 * i + 2)
                wide = [w[j][:, :].rearrange("p (g k n) -> p g k n", g=2, n=FE) for w in (w_hi, w_lo)]
                for k in range(KD // 2):
                    cols = slice((4 * j + k) * CAP, (4 * j + k + 1) * CAP)
                    mm = three_products(bank[2 + u % 2][:, :].rearrange("p (g n) -> p g n", g=2), (x_hi[:, cols], x_lo[:, cols]),
                                        [a[:, :, k, :] for a in wide], j == 0 and k == 0, j == 1 and k == 3)
                mm.then_inc(chunk_used[j], 1)

            def down(i, first):
                pe.wait_ge(lo_ready[2], i + 1)
                pe.wait_ge(S["a_lo_ready"], i + 1)
                if not first:
                    pe.wait_ge(S["y_ready"], i)
                for half in range(2):
                    for k in range(2):
                        cols, wc = slice(k * CAP, (k + 1) * CAP), slice(k * D + 512 * half, k * D + 512 * half + 512)
                        mm = three_products(bank[5 + half][:, :], (a_hi[:, cols], a_lo[:, cols]),
                                            (w_hi[2][:, wc], w_lo[2][:, wc]), k == 0, k == 1)
                mm.then_inc(chunk_used[2], 1)

            def block_turn(b, first):
                for u in range(UN):
                    i = u if first else b * UN + u
                    gate_up(i, u, 0)
                    gate_up(i, u, 1)
                    turn_tokens(i + 1, u + 1, first)
                    if not (first and u == 0):
                        down(i - 1, first and u == 1)
                    pe.wait_ge(S["act_ready"], i + 1)
                    for k in range(2):
                        mm = pe.transpose(bank[4][:, k * P:(k + 1) * P], act_sb[:, k * P:(k + 1) * P], ident[:, :])
                    mm.then_inc(S["at_mm"], 1)
                    pe.wait_ge(S["idx_ready"], i + 3)
                    block_rows(i + 3, u + 3)

            pe.wait_ge(S["idx_ready"], 2)
            block_rows(2, 2)
            turn_tokens(0, 0, True)
            block_turn(0, True)
            with pe.Fori(1, passes * (NE // UN)) as b:
                block_turn(b, False)
            down(passes * NE - 1, False)

        @block.vector
        def _(dve):
            go = link(dve, S["dve_step"])
            CW, CB, BA, BX, LAM, H0 = 0, 16, 20, 28, 36, 44
            def normalise(n, t, dst, signal):
                dve.tensor_scalar(dst[:, t, :], x_sb[:, t, :], rstd[:, n, t:t + 1], None, ALU.mult).then_inc(signal, 1)

            for t in range(TT):
                dve.wait_ge(S["rstd1"], t + 1)
                normalise(0, t, xhat, S["xhat1"])

            def row(c):
                dve.wait_ge(S["ada_mm"], c + 1)
                if c % 4 == 0 and c:
                    dve.wait_ge(S["m_spread"], c // 4)
                at_c = CH * (c % 4)
                dve.tensor_tensor(m_row[:, at_c:at_c + CH], bank[6 + c % 2][0:2, 0:CH],
                                  b_row[:, c % BROWS, :], ALU.add).then_inc(S["ada_row"], 1)

            for c in range(8):
                if c >= 6:
                    split_low(dve, c + 2)
                row(c)

            def scales(dst, i, g):
                dve.wait_ge(S["cond_loaded"], 64)
                go(dve.scalar_tensor_tensor(dst[:, :, :], mod_t[:, i, :, :], 1.0,
                                            g[:, :].unsqueeze(2).to_broadcast([P, KD, 2]), ALU.add, ALU.mult))

            dve.wait_ge(S["mod_copied"], 2)
            scales(scale1, 1, g1_sb)
            dve.engine_nop().then_inc(S["scale1_ready"], 1)
            for t in range(TT - 1):
                cond = int(t > 0)
                for k in range(KD):
                    dve.wait_ge(S["xt1"], 2 * t + k // 4 + 1)
                    ins = dve.tensor_scalar(h_t[:, k, t * P:(t + 1) * P], bank[2 * t + k // 4][:, (k % 4) * P:(k % 4 + 1) * P],
                                            scale1[:, k, cond:cond + 1], mod_t[:, 0, k, cond:cond + 1], ALU.mult, ALU.add)
                ins.then_inc(S["h_made"], 1)
            for n, t in enumerate((2, 0, 1)):
                cols = slice(t * P, (t + 1) * P)
                dve.wait_ge(S["h_high"], n + 1)
                dve.tensor_tensor(h_lo[:, :, cols], h_t[:, :, cols], h_hi[:, :, cols].bitcast(F32), ALU.subtract).then_inc(S["h_ready"], 1)
            dve.wait_ge(S["vec_mm"], 1)
            dve.tensor_copy(vec_t[:, :], bank[7][:, 0:NVEC]).then_inc(S["vec_copied"], 1)
            dve.wait_ge(S["vec_copied"], 1)
            go(dve.tensor_scalar(neg_lam[:, :], vec_t[:, LAM:LAM + 8], -1.0, None, ALU.mult))
            dve.tensor_tensor(abs_lam[:, :], vec_t[:, LAM:LAM + 8], neg_lam[:, :], ALU.max).then_inc(S["soft_in"], 1)
            go(dve.tensor_scalar(half_b[:, :], vec_t[:, BA:BA + 16], 0.5, None, ALU.mult))
            for n in range(10, 14):
                split_low(dve, n)
            for n in range(14, 16):
                split_low(dve, n)
            for s in range(NSTEP + 1):
                if s < NSTEP:
                    h, t = unit(s)
                    b = s % 2
                    if s == H:
                        dve.wait_ge(S["bias_loaded"], 32)
                        dve.wait_ge(S["mask_made"], 2)
                        go(dve.tensor_tensor(bias_sb[:, :, :, :].rearrange("p s h c -> p (s h) c"),
                                             bias_sb[:, :, :, :].rearrange("p s h c -> p (s h) c"),
                                             col_mask[:, :].unsqueeze(1).to_broadcast([P, 6 * H, GW]), ALU.add))
                    dve.wait_ge(S["s_mm"], s + 1)
                    if t == 0:
                        dve.tensor_reduce(neg_max[:, b:b + 1], bank[b][:, 0:NCTX], AX, ALU.max, negate=True).then_inc(S["max_ready"], 1)
                    else:
                        first = 2 if t == 1 else 0
                        dve.tensor_tensor(s_sb[:, b, 0:NLAT].rearrange("p (j c) -> p j c", c=GW),
                                          bank[b][:, 0:NLAT].rearrange("p (j c) -> p j c", c=GW),
                                          bias_sb[:, first:first + 4, h, :], ALU.add)
                        go(dve.tensor_copy(s_sb[:, b, NLAT:384], bank[b][:, NLAT:384]))
                        dve.tensor_reduce(neg_max[:, b:b + 1], s_sb[:, b, :], AX, ALU.max, negate=True).then_inc(S["max_ready"], 1)
                    n = NCTX if t == 0 else 384
                    dve.wait_ge(S["exp_done"], s + 1)
                    go(dve.reciprocal(row_inv[:, b:b + 1], row_sum[:, b:b + 1]))
                    dve.tensor_scalar(e_sb[:, b, 0:n], e_sb[:, b, 0:n], row_inv[:, b:b + 1], None, ALU.mult).then_inc(S["p_ready"], 1)
                if s >= 1:
                    n = NCTX if s - 1 < H else 384
                    dve.wait_ge(S["pt_mm"], s)
                    if s >= 3:
                        dve.wait_ge(S["o_mm"], s - 2)
                    dve.tensor_copy(pt_sb[:, (s - 1) % 2, 0:n], bank[4 + (s - 1) % 2][:, 0:n]).then_inc(S["pt_evac"], 1)
                if 2 <= s <= 20 and s % 2 == 0:
                    split_low(dve, 16 + (s - 1) // 2)
                if 9 <= s < 9 + CT:
                    t = s - 9
                    dve.wait_ge(S["w_evac"], 18)
                    go(dve.tensor_scalar(xc[:, t, :], xr_pad[:, t, 0:RC], vec_t[:, CW + t:CW + t + 1],
                                         vec_t[:, CB + t:CB + t + 1], ALU.mult, ALU.add))
                    for tap in range(1, 4):
                        j = CW + tap * CT + t
                        go(dve.scalar_tensor_tensor(xc[:, t, :], xr_pad[:, t, tap:tap + RC], vec_t[:, j:j + 1],
                                                    xc[:, t, :], ALU.mult, ALU.add))
            dve.engine_nop().then_inc(S["conv_done"], 1)
            dve.wait_ge(S["soft_ln"], 1)
            go(dve.scalar_tensor_tensor(softplus[:, :], neg_lam[:, :], 0.0, softplus[:, :], ALU.max, ALU.add))
            go(dve.tensor_scalar(decay2[:, :], softplus[:, :], -RG_C, None, ALU.mult))
            dve.tensor_scalar(decay[:, :], softplus[:, :], -RG_C / 2, None, ALU.mult).then_inc(S["decay_ready"], 1)
            dve.wait_ge(S["oa_high"], 1)
            dve.tensor_tensor(oa_lo[:, :, :], oa_t[:, :, :], oa_hi[:, :, :].bitcast(F32), ALU.subtract).then_inc(S["oa_ready"], 1)
            row(8)
            dve.wait_ge(S["e2_done"], 8)
            dve.tensor_scalar(gate_e[:, :, :, :], gate_e[:, :, :, :], 1.0, None, ALU.min).then_inc(S["e2_capped"], 1)
            row(9)
            dve.wait_ge(S["gates_tanh"], 16)
            for d in range(2):
                go(dve.scalar_tensor_tensor(gate_i[:, d, :, :], gate_i[:, d, :, :], 1.0, xc[:, :, :], ALU.add, ALU.mult))
            row(10)
            row(11)
            dve.wait_ge(S["root_done"], 1)
            for d in range(2):
                go(dve.tensor_tensor(gate_e[:, d, :, :], gate_e[:, d, :, :], gate_i[:, d, :, :], ALU.mult))
            row(12)
            row(13)
            dve.wait_ge(S["a_done"], 8)
            for d in range(2):
                for t in range(CT):
                    for lo, hi, init in ((0, NCTX, 0.0), (LAT0, RC, vec_t[:, H0 + CT * d + t:H0 + CT * d + t + 1])):
                        cut = slice(lo, hi) if d == 0 else slice(hi - 1, lo - 1 if lo else None, -1)
                        ins = dve.tensor_tensor_scan(gate_i[:, d, t, cut], gate_r[:, d, t, cut], gate_e[:, d, t, cut],
                                                     init, ALU.mult, ALU.add)
                        go(ins)
                row(14 + 2 * d)
                row(15 + 2 * d)
            go(dve.tensor_copy(h_last[:, 0:CT], gate_i[:, 0, :, NCTX - 1]))
            dve.tensor_copy(h_last[:, CT:2 * CT], gate_i[:, 1, :, 0]).then_inc(S["hl_ready"], 1)
            dve.wait_ge(S["gelu_done"], 1)
            for lo, hi, at_tok in ((0, NCTX, 0), (LAT0, RC, NCTX)):
                dst = ob_t[:, :, at_tok:at_tok + hi - lo]
                go(dve.tensor_tensor(dst, gate_i[:, 0, :, lo:hi], gate_i[:, 1, :, lo:hi], ALU.add))
                go(dve.tensor_tensor(dst, dst, yg[:, :, at_tok:at_tok + hi - lo], ALU.mult))
            dve.engine_nop().then_inc(S["ob_ready"], 1)
            for c in range(18, NADA):
                row(c)
            split_low(dve, number[("pa", 0)])
            split_low(dve, number[("pb", 0)])
            dve.wait_ge(S["ob_high"], 1)
            dve.tensor_tensor(ob_lo[:, :, :], ob_t[:, :, :], ob_hi[:, :, :].bitcast(F32), ALU.subtract).then_inc(S["ob_split"], 1)
            for i in range(2):
                for m in range(4):
                    dve.wait_ge(S["merge_mm"], 8 * i + m + 1)
                    g = ga[:, 4 * i + m, :]
                    dve.scalar_tensor_tensor(g, g, 1.0, bank[m][:, 0:NTOK], ALU.add, ALU.mult).then_inc(S["merge_gated"], 1)
                split_low(dve, number[("out", 0)] if i else number[("pa", 1)])
                for m in range(4):
                    dve.wait_ge(S["merge_mm"], 8 * i + m + 5)
                    g = gb[:, 4 * i + m, :]
                    dve.scalar_tensor_tensor(g, g, 1.0, bank[4 + m][:, 0:NTOK], ALU.add, ALU.mult).then_inc(S["merge_gated"], 1)
                    dve.wait_ge(S["merge_gated"], 8 * i + m + 5)
                    at_m = 4 * i + m
                    dve.tensor_tensor(merged[:, at_m, :], ga[:, at_m, :], gb[:, at_m, :], ALU.add).then_inc(S["merge_done"], 1)
                    dve.wait_ge(S["merged_high"], at_m + 1)
                    dve.tensor_tensor(merged_lo[:, at_m, :], merged[:, at_m, :], merged_hi[:, at_m, :].bitcast(F32),
                                      ALU.subtract).then_inc(S["merged_ready"], 1)
                split_low(dve, number[("out", 1)] if i else number[("pb", 1)])
            dve.wait_ge(S["bc_evac"], 4)
            for n in range(12):
                c, t = divmod(n, 3)
                cols = slice(CH * c, CH * c + CH)
                dve.wait_ge(S["out_mm"], n + 1)
                go(dve.tensor_tensor(gated[:, n, :], bank[n % 4][:, 0:CH], gate_mix[:, int(t > 0), cols], ALU.mult))
                dve.tensor_tensor(x_sb[:, t, cols], x_sb[:, t, cols], gated[:, n, :], ALU.add).then_inc(S["out_done"], 1)
                if t == 2 and c < 2:
                    split_low(dve, number[("out", 2 + c)])
            dve.wait_ge(S["mod_copied"], 4)
            scales(scale2, 4, g2_sb)
            for t in range(TT):
                dve.wait_ge(S["rstd2"], t + 1)
                normalise(1, t, xhat2, S["xhat2"])
            for t in range(TT):
                cond = int(t > 0)
                for k in range(KD):
                    n = 2 * t + k // 4
                    dve.wait_ge(S["xt2"], n + 1)
                    ins = dve.tensor_scalar(h2_t[:, k, t * P:(t + 1) * P], bank[4 + n % 4][:, (k % 4) * P:(k % 4 + 1) * P],
                                            scale2[:, k, cond:cond + 1], mod_t[:, 3, k, cond:cond + 1], ALU.mult, ALU.add)
                    if k % 4 == 3:
                        ins.then_inc(S["h2_ready"], 1)
            for t in range(TT):
                cols = slice(t * P, (t + 1) * P)
                dve.wait_ge(S["h2_high"], t + 1)
                dve.tensor_tensor(h2_lo[:, :, cols], h2_t[:, :, cols], h2_hi[:, :, cols].bitcast(F32), ALU.subtract).then_inc(S["h2_split"], 1)
            for i in range(2):
                split_low(dve, number[("sgu", i)])
            dve.wait_ge(S["tables_made"], 6)
            dve.wait_ge(S["late_loaded"], 32)
            dve.wait_ge(S["score_done"], 1)
            go(dve.tensor_tensor(biased[:, :, :], score[:, :, :], router_b[:, :].unsqueeze(1).to_broadcast([P, TT, NE]), ALU.add))
            for t in range(TT):
                for g in range(NG):
                    ins = dve.max(group_top[:, t, g, :], biased[:, t, g * GE:(g + 1) * GE])
            go(ins)
            go(dve.tensor_tensor(group_score[:, :, 0:NG], group_top[:, :, :, 0], group_top[:, :, :, 1], ALU.add))
            for t in range(TT):
                ins = dve.max(best_groups[:, t, :], group_score[:, t, 0:8])
            go(ins)
            go(dve.memset(best_groups[:, :, 4:8], LOWEST))
            for t in range(TT):
                ins = dve.match_replace(group_left[:, t, 0:12], best_groups[:, t, :], group_score[:, t, 0:12], BIG)
            go(ins)
            go(dve.tensor_scalar(group_mask[:, :, :], group_left[:, :, 0:NG], BIG, None, ALU.is_equal))
            go(dve.tensor_scalar(group_pen[:, :, :], group_mask[:, :, :], BIG, -BIG, ALU.mult, ALU.add))
            by_group = lambda ap: ap.rearrange("p t (g e) -> p (t g) e", e=GE)
            spread = lambda ap: ap.rearrange("p t g -> p (t g)").unsqueeze(2).to_broadcast([P, TT * NG, GE])
            go(dve.tensor_tensor(by_group(masked[:, :, :]), by_group(biased[:, :, :]), spread(group_mask[:, :, :]), ALU.mult))
            go(dve.tensor_tensor(by_group(masked[:, :, :]), by_group(masked[:, :, :]), spread(group_pen[:, :, :]), ALU.add))
            for t in range(TT):
                ins = dve.max(top8[:, t, :], masked[:, t, :])
            go(ins)
            for t in range(TT):
                ins = dve.match_replace(left[:, t, :], top8[:, t, :], masked[:, t, :], LOWEST)
            go(ins)
            go(dve.tensor_scalar(chosen[:, :, :], left[:, :, :], LOWEST, None, ALU.is_equal))
            dve.tensor_copy(chosen_b[:, :, :], chosen[:, :, :]).then_inc(S["chosen_ready"], 1)
            go(dve.tensor_tensor(gates[:, :, :], score[:, :, :], chosen[:, :, :], ALU.mult))
            go(dve.tensor_reduce(gate_sum[:, :], gates[:, :, :], AX, ALU.add))
            go(dve.reciprocal(gate_sum[:, :], gate_sum[:, :]))
            for t in range(TT):
                ins = dve.tensor_scalar(gates[:, t, :], gates[:, t, :], gate_sum[:, t:t + 1], SCALED, ALU.mult, ALU.mult)
            go(ins)
            go(dve.memset(row_tab[:, NBLK:NTAB, :, :], 0.0))
            for t in range(TT):
                col = lambda j: row_tab[:, 0:NE, t, j]
                go(dve.memset(col(0), float(P * t - 4 * P)))
                go(dve.tensor_scalar(col(1), ones_row[:, :], lane[:, 0:1], None, ALU.mult))
                go(dve.tensor_copy(col(2), gates[:, t, :]))
                go(dve.tensor_tensor(g_rest[:, t, :], gates[:, t, :], col(2), ALU.subtract))
                go(dve.tensor_copy(col(3), g_rest[:, t, :]))
                go(dve.tensor_tensor(g_rest[:, t, :], g_rest[:, t, :], col(3), ALU.subtract))
                go(dve.tensor_copy(col(4), g_rest[:, t, :]))
            for pas in range(1, MAXPASS):
                go(dve.tensor_copy(row_tab[:, pas * NE:(pas + 1) * NE, :, :], row_tab[:, 0:NE, :, :]))
            dve.wait_ge(S["rank_mm"], 1)
            go(dve.scalar_tensor_tensor(rank_f[:, :, :], bank[1][:, 0:TT * NE].rearrange("p (t e) -> p t e", t=TT), 1.0,
                                        chosen[:, :, :], ALU.add, ALU.mult))
            for pas in range(MAXPASS):
                go(dve.tensor_scalar(rank_tab[:, pas * NE:(pas + 1) * NE, :].rearrange("p e t -> p t e"), rank_f[:, :, :],
                                     -1.0 - CAP * pas, None, ALU.add))
            go(dve.memset(rank_tab[:, NBLK:NTAB, :], -1.0))
            go(dve.tensor_reduce(load_f[:, 0:1], bank[1][:, TT * NE:(TT + 1) * NE], AX, ALU.max))
            go(dve.tensor_scalar(load_f[:, 1:2], load_f[:, 0:1], CAP + 0.5, None, ALU.is_gt))
            go(dve.tensor_scalar(load_f[:, 2:3], load_f[:, 0:1], 2 * CAP + 0.5, None, ALU.is_gt))
            go(dve.tensor_tensor(more_i[:, 0:1], load_f[:, 1:2], load_f[:, 2:3], ALU.add))
            dve.engine_nop().then_inc(S["tables_ready"], 1)
            dve.engine_nop().then_inc(S["passes_ready"], 1)
            def select(i, u):
                dve.tensor_tensor(onehot[u % 2][:, :, :], slot_no[:, :, :],
                                  rank_tab[:, bass.ds(i, 1), :].rearrange("p a t -> p (a t)").unsqueeze(2)
                                  .to_broadcast([P, TT, CAP]), ALU.is_equal).then_inc(S["onehot_ready"], 1)

            def numbers(i, u):
                u = u % UN
                dve.wait_ge(S["idx_mm"], i + 1)
                dve.tensor_reduce(slot_val[:, u:u + 1], bank[7][:, 0:2], AX, ALU.add).then_inc(S["num_step"], 1)
                dve.tensor_reduce(slot_gate[:, u:u + 1], bank[7][:, 2:5], AX, ALU.add).then_inc(S["num_step"], 1)
                dve.wait_ge(S["num_step"], 2 * i + 2)
                dve.tensor_scalar(slot_tok[:, u:u + 1], slot_val[:, u:u + 1], float(4 * P), None, ALU.add).then_inc(S["idx_ready"], 1)

            select(0, 0)
            select(1, 1)
            for m in range(2):
                dve.wait_ge(S["sh_silu"], m + 1)
                dve.wait_ge(S["sh_mm"], m + 3)
                dve.tensor_tensor(hs_t[:, m, :], hs_g[:, m, :], bank[4 + m][:, 0:NTOK], ALU.mult).then_inc(S["sh_act"], 1)
            numbers(0, 0)
            select(2, 2)
            split_low(dve, number[("sd", 0)])
            dve.wait_ge(S["hs_high"], 1)
            dve.tensor_tensor(hs_lo[:, :, :], hs_t[:, :, :], hs_hi[:, :, :].bitcast(F32), ALU.subtract).then_inc(S["hs_ready"], 1)
            numbers(1, 1)
            select(3, 3)
            passes = dve.value_load(more_i[0:1, 0:1], min_val=0, max_val=MAXPASS - 1) + 1

            def lo(i, u, j):
                dve.wait_ge(hi_ready[j], i + 1)
                dve.tensor_tensor(w_lo[j][:, :], raw[u % RAW][j][:, :], w_hi[j][:, :].bitcast(F32),
                                  ALU.subtract).then_inc(lo_ready[j], 1)

            def x_low(i):
                for half in range(2):
                    cols = slice(half * 512, half * 512 + 512)
                    dve.wait_ge(S["x_hi_ready"], 2 * i + 1 + half)
                    dve.tensor_tensor(x_lo[:, cols], bank[half][:, :], x_hi[:, cols].bitcast(F32),
                                      ALU.subtract).then_inc(S["x_lo_ready"], 1)

            def block_turn(b, first):
                for u in range(UN):
                    i = u if first else b * UN + u
                    if not (first and u == 0):
                        lo(i - 1, u - 1, 2)
                    lo(i + 1, u + 1, 0)
                    dve.wait_ge(S["silu_done"], i + 1)
                    dve.tensor_tensor(act_sb[:, :], silu_sb[:, :], bank[2 + u % 2][:, FE:2 * FE],
                                      ALU.mult).then_inc(S["act_ready"], 1)
                    x_low(i + 1)
                    lo(i + 1, u + 1, 1)
                    dve.wait_ge(S["a_hi_ready"], i + 1)
                    dve.tensor_tensor(a_lo[:, :], bank[4][:, 0:FE], a_hi[:, :].bitcast(F32), ALU.subtract).then_inc(S["a_lo_ready"], 1)
                    numbers(i + 3, u + 3)
                    select(i + 4, u + 4)

            numbers(2, 2)
            lo(0, 0, 0)
            lo(0, 0, 1)
            x_low(0)
            block_turn(0, True)
            with dve.Fori(1, passes * (NE // UN)) as b:
                block_turn(b, False)
            lo(passes * NE - 1, UN - 1, 2)
            dve.wait_ge(S["bc_evac"], 8)
            for t in range(TT):
                dve.wait_ge(ffn_loaded[t], 16)
                go(dve.tensor_tensor(ffn[t][:, :], ffn[t][:, :], gate_ffn[:, int(t > 0), :], ALU.mult))
                dve.tensor_tensor(x_sb[:, t, :], x_sb[:, t, :], ffn[t][:, :], ALU.add).then_inc(S["x2_ready"], 1)
            for t in range(TT):
                dve.wait_ge(S["rstd3"], t + 1)
                dve.scalar_tensor_tensor(x_sb[:, t, :], x_sb[:, t, :], rstd[:, 2, t:t + 1], final_g_sb[:, :],
                                         ALU.mult, ALU.mult).then_inc(S["y_done"], 1)


_INS = ['x_prompt', 'x_sample', 'cache_k', 'cache_v', 'state_h_fwd', 'state_h_bwd', 'c', 'c_ctx', 'norm1_g', 'norm2_g',
        'final_g', 'w_ada', 'b_ada', 'w_in', 'rpb', 'conv_w', 'conv_b', 'rg_wa', 'rg_ba', 'rg_wx', 'rg_bx', 'rg_lam',
        'w_pa', 'w_pb', 'w_out', 'w_router', 'b_router', 'w_gate_e', 'w_up_e', 'w_down_e', 'w_gate_s', 'w_up_s', 'w_down_s']
_OUTS = [(1, 128, 1024), (1, 256, 1024), (1, 1, 128, 8, 64), (1, 1, 128, 8, 64), (1, 1, 512), (1, 1, 512)]


def kernel(**inputs):
    import numpy as _np
    import concourse.bacc as _bacc
    from concourse import mybir as _mybir
    from concourse.bass_utils import run_bass_kernel_spmd as _run

    nc = _bacc.Bacc("TRN2", target_bir_lowering=False, num_devices=1)
    arrays, args = {}, []
    for name in _INS:
        a = _np.ascontiguousarray(inputs[name])
        arrays[f"in_{name}_dram"] = a
        args.append(nc.dram_tensor(f"in_{name}_dram", a.shape, _mybir.dt.from_np(a.dtype), kind="ExternalInput").ap())
    for i, shape in enumerate(_OUTS):
        args.append(nc.dram_tensor(f"out_{i}_dram", shape, _mybir.dt.float32, kind="ExternalOutput").ap())
    hybrid_step(nc, *args)
    r = _run(nc, [arrays], core_ids=[0])
    return tuple(r.results[0][f"out_{i}_dram"] for i in range(len(_OUTS)))
```
